# Optimizing a Trainium2 kernel written in Bass

```python
import math
import jax
import jax.numpy as jnp
from jax import lax
import numpy as np
import jax, jax.numpy as jnp

D_MODEL = 1024
BATCH = 1
SEQ = 256
DEPTH = 2

HEAD_DIM = 64
CONV_CH = 512
CONV_K = 3
FOX_HEADS = 8
FOX_WIDTH = FOX_HEADS * HEAD_DIM
EVEN_IN = 3 * CONV_CH + 3 * FOX_WIDTH + FOX_HEADS
Q_BLOCK = 128
NSA_GROUPS = 4
NSA_HPG = 4
NSA_HEADS = NSA_GROUPS * NSA_HPG
NSA_WIDTH = NSA_HEADS * HEAD_DIM
NSA_KV = NSA_GROUPS * HEAD_DIM
CMP_LEN = 32
CMP_STRIDE = 16
SLC_LEN = 64
SLC_TOPN = 16
WINDOW = 512
SLC_QCHUNK = 16
ODD_IN = NSA_WIDTH + 6 * NSA_KV + 3 * NSA_HEADS
REL_BUCKETS = 32
REL_MAX_DIST = 128
PEER_HEADS = 8
PEER_NKEYS = 128
PEER_EXPERTS = PEER_NKEYS * PEER_NKEYS
PEER_QDIM = 128
PEER_TOPK = 16
PEER_CHUNK = 128
N_EVEN = (DEPTH + 1) // 2
N_ODD = DEPTH // 2
EPS = 1e-6
NEG_INF = -1e30
FORCE_SCORE = 1e6


def rms_norm(x, g):
    xf = x.astype(jnp.float32)
    y = xf * lax.rsqrt(jnp.mean(xf * xf, axis=-1, keepdims=True) + EPS)
    return (y * g.astype(jnp.float32)).astype(x.dtype)

def modulate(h, shift, scale):
    return h * (1 + scale[:, None, :]) + shift[:, None, :]

def masked_softmax(s, mask):
    s = jnp.where(mask, s.astype(jnp.float32), NEG_INF)
    return jax.nn.softmax(s, axis=-1) * mask

def rel_bucket(dist):
    n = jnp.maximum(dist, 0)
    max_exact = REL_BUCKETS // 2
    nf = jnp.maximum(n, 1).astype(jnp.float32)
    large = max_exact + (jnp.log(nf / max_exact) / math.log(REL_MAX_DIST / max_exact)
                         * (REL_BUCKETS - max_exact)).astype(jnp.int32)
    large = jnp.minimum(large, REL_BUCKETS - 1)
    return jnp.where(n < max_exact, n, large)

def short_conv(u, w):
    return lax.conv_general_dilated(
        u, w.astype(u.dtype)[:, None, :], window_strides=(1,), padding=((CONV_K - 1, 0),),
        dimension_numbers=('NWC', 'WIO', 'NWC'), feature_group_count=u.shape[-1])

def fox_attention(q, k, v, logf):
    B, S, H, Dh = q.shape
    nb = S // Q_BLOCK
    cum_t = jnp.cumsum(logf, axis=1).transpose(0, 2, 1)
    kpos = jnp.arange(S)
    scale = Dh ** -0.5
    qb = q.reshape(B, nb, Q_BLOCK, H, Dh).swapaxes(0, 1)
    cb = cum_t.reshape(B, H, nb, Q_BLOCK).transpose(2, 0, 1, 3)
    tb = kpos.reshape(nb, Q_BLOCK)

    def block(args):
        qi, ci, ti = args
        s = jnp.einsum('bqhd,bkhd->bhqk', qi, k).astype(jnp.float32) * scale
        s = s + (ci[..., None] - cum_t[:, :, None, :])
        p = masked_softmax(s, ti[:, None] >= kpos[None, :])
        return jnp.einsum('bhqk,bkhd->bqhd', p.astype(v.dtype), v)

    out = lax.map(block, (qb, cb, tb))
    return out.swapaxes(0, 1).reshape(B, S, H, Dh)

def conv_fox_mixer(h, w_in, b_f, conv_w, q_g, k_g, w_out):
    B, S, _ = h.shape
    splits = list(np.cumsum([CONV_CH] * 3 + [FOX_WIDTH] * 3))
    cb, cc, ch, q, k, v, f = jnp.split(h @ w_in, splits, axis=-1)
    conv_out = cb * short_conv(cc * ch, conv_w)
    q = rms_norm(q.reshape(B, S, FOX_HEADS, HEAD_DIM), q_g)
    k = rms_norm(k.reshape(B, S, FOX_HEADS, HEAD_DIM), k_g)
    v = v.reshape(B, S, FOX_HEADS, HEAD_DIM)
    logf = jax.nn.log_sigmoid((f + b_f).astype(jnp.float32))
    attn = fox_attention(q, k, v, logf).reshape(B, S, FOX_WIDTH)
    return jnp.concatenate([conv_out, attn], axis=-1) @ w_out

def nsa_mixer(h, w_in, b_gate, q_g, k_g, cmp_pos, cmp_w1, cmp_w2, rel_table, w_out):
    B, S, _ = h.shape
    G, J, Dh = NSA_GROUPS, NSA_HPG, HEAD_DIM
    f32 = jnp.float32
    splits = list(np.cumsum([NSA_WIDTH] + [NSA_KV] * 6))
    q, kc, vc, ks, vs, kw, vw, gl = jnp.split(h @ w_in, splits, axis=-1)
    q = rms_norm(q.reshape(B, S, G, J, Dh), q_g)
    kc, vc, ks, vs, kw, vw = [a.reshape(B, S, G, Dh) for a in (kc, vc, ks, vs, kw, vw)]
    ks = rms_norm(ks, k_g[1])
    kw = rms_norm(kw, k_g[2])
    gates = jax.nn.sigmoid((gl + b_gate).astype(f32)).reshape(B, S, G, J, 3).astype(h.dtype)
    tpos = jnp.arange(S)
    table = rel_table.reshape(REL_BUCKETS, G, J)
    scale = Dh ** -0.5

    n_cmp = (S - CMP_LEN) // CMP_STRIDE + 1
    starts = jnp.arange(n_cmp) * CMP_STRIDE
    ends = starts + CMP_LEN - 1
    tok = starts[:, None] + jnp.arange(CMP_LEN)[None, :]

    def compress(a, pos, w1, w2):
        blk = a[:, tok] + pos[:, None, :]
        blk = blk.transpose(0, 1, 3, 2, 4).reshape(B, n_cmp, G, CMP_LEN * Dh)
        return jax.nn.gelu(blk @ w1) @ w2

    Kc = rms_norm(compress(kc, cmp_pos[0], cmp_w1[0], cmp_w2[0]), k_g[0])
    Vc = compress(vc, cmp_pos[1], cmp_w1[1], cmp_w2[1])
    s_c = jnp.einsum('bsgjd,bngd->bgjsn', q, Kc).astype(f32) * scale
    s_c = s_c + table[rel_bucket(tpos[:, None] - ends[None, :])].transpose(2, 3, 0, 1)
    p_c = masked_softmax(s_c, ends[None, :] <= tpos[:, None])
    o_c = jnp.einsum('bgjsn,bngd->bsgjd', p_c.astype(Vc.dtype), Vc)

    n_slc = S // SLC_LEN
    top_n = min(SLC_TOPN, n_slc)
    blk_ids = jnp.arange(n_slc)
    bstart = blk_ids * SLC_LEN
    overlap = ((starts[:, None] < bstart[None, :] + SLC_LEN)
               & (starts[:, None] + CMP_LEN > bstart[None, :])).astype(f32)
    imp = jnp.einsum('bgjsn,nm->bgsm', p_c, overlap)
    cur = tpos // SLC_LEN
    forced = (blk_ids[None, :] == 0) | (blk_ids[None, :] == cur[:, None]) | (blk_ids[None, :] == cur[:, None] - 1)
    imp = jnp.where(forced, FORCE_SCORE, jnp.where(bstart[None, :] <= tpos[:, None], imp, -1.0))
    sel_score, sel_idx = lax.top_k(imp, top_n)
    sel_valid = sel_score >= 0

    Ks = ks.reshape(B, n_slc, SLC_LEN, G, Dh).transpose(0, 3, 1, 2, 4)
    Vs = vs.reshape(B, n_slc, SLC_LEN, G, Dh).transpose(0, 3, 1, 2, 4)
    nq = S // SLC_QCHUNK
    bi = jnp.arange(B)[:, None, None, None]
    gi = jnp.arange(G)[None, :, None, None]

    def slc_chunk(args):
        qi, idx, val, ti = args
        Kg = Ks[bi, gi, idx]
        Vg = Vs[bi, gi, idx]
        kpos = idx[..., None] * SLC_LEN + jnp.arange(SLC_LEN)
        dist = ti[None, None, :, None, None] - kpos
        mask = val[..., None] & (dist >= 0)
        bias = jnp.moveaxis(table[rel_bucket(dist), gi[..., None]], -1, 2)
        s = jnp.einsum('bqgjd,bgqnld->bgjqnl', qi, Kg).astype(f32) * scale + bias
        sh = s.shape
        m = jnp.broadcast_to(mask[:, :, None], sh).reshape(sh[:4] + (-1,))
        p = masked_softmax(s.reshape(sh[:4] + (-1,)), m).reshape(sh)
        return jnp.einsum('bgjqnl,bgqnld->bqgjd', p.astype(Vg.dtype), Vg)

    qs = q.reshape(B, nq, SLC_QCHUNK, G, J, Dh).swapaxes(0, 1)
    idx_s = sel_idx.reshape(B, G, nq, SLC_QCHUNK, top_n).transpose(2, 0, 1, 3, 4)
    val_s = sel_valid.reshape(B, G, nq, SLC_QCHUNK, top_n).transpose(2, 0, 1, 3, 4)
    t_s = tpos.reshape(nq, SLC_QCHUNK)
    o_s = lax.map(slc_chunk, (qs, idx_s, val_s, t_s)).swapaxes(0, 1).reshape(B, S, G, J, Dh)

    kwp = jnp.pad(kw, ((0, 0), (WINDOW, 0), (0, 0), (0, 0)))
    vwp = jnp.pad(vw, ((0, 0), (WINDOW, 0), (0, 0), (0, 0)))
    nb = S // Q_BLOCK
    span = Q_BLOCK + WINDOW
    koff = jnp.arange(span)
    dist_w = jnp.arange(Q_BLOCK)[:, None] + WINDOW - koff[None, :]
    band = (dist_w >= 0) & (dist_w < WINDOW)
    bias_w = table[rel_bucket(dist_w)].transpose(2, 3, 0, 1)

    def win_block(args):
        qi, i = args
        start = i * Q_BLOCK
        kb = lax.dynamic_slice_in_dim(kwp, start, span, axis=1)
        vb = lax.dynamic_slice_in_dim(vwp, start, span, axis=1)
        s = jnp.einsum('bqgjd,bkgd->bgjqk', qi, kb).astype(f32) * scale + bias_w
        mask = band & ((start - WINDOW + koff) >= 0)[None, :]
        p = masked_softmax(s, mask)
        return jnp.einsum('bgjqk,bkgd->bqgjd', p.astype(vb.dtype), vb)

    qw = q.reshape(B, nb, Q_BLOCK, G, J, Dh).swapaxes(0, 1)
    o_w = lax.map(win_block, (qw, jnp.arange(nb))).swapaxes(0, 1).reshape(B, S, G, J, Dh)

    o = gates[..., 0:1] * o_c + gates[..., 1:2] * o_s + gates[..., 2:3] * o_w
    return o.reshape(B, S, NSA_WIDTH) @ w_out

def peer_ffn(h, w_q, sub_keys, u, v):
    B, S, D = h.shape
    T = B * S
    half = PEER_QDIM // 2
    hc = h.reshape(T // PEER_CHUNK, PEER_CHUNK, D)

    def chunk(xc):
        q = (xc @ w_q).reshape(-1, PEER_HEADS, 2, half)
        s = jnp.einsum('thpd,pkd->thpk', q, sub_keys).astype(jnp.float32)
        sv, si = lax.top_k(s, PEER_TOPK)
        cand = (sv[:, :, 0, :, None] + sv[:, :, 1, None, :]).reshape(-1, PEER_HEADS, PEER_TOPK * PEER_TOPK)
        cand_id = (si[:, :, 0, :, None] * PEER_NKEYS + si[:, :, 1, None, :]).reshape(-1, PEER_HEADS, PEER_TOPK * PEER_TOPK)
        cv, ci = lax.top_k(cand, PEER_TOPK)
        eid = jnp.take_along_axis(cand_id, ci, axis=-1)
        g = jax.nn.softmax(cv, axis=-1)
        ue = u[eid]
        ve = v[eid]
        a = jax.nn.gelu(jnp.einsum('td,thkd->thk', xc, ue)).astype(jnp.float32)
        return jnp.einsum('thk,thkd->td', (g * a).astype(ve.dtype), ve)

    return lax.map(chunk, hc).reshape(B, S, D)

def first_inputs(seed: int = 0) -> dict:
    key = jax.random.key(seed)
    ks = jax.random.split(key, 24)
    D = D_MODEL

    def nrm(k, shape, s):
        return jax.random.normal(k, shape, jnp.float32) * s

    return {
        'x': nrm(ks[0], (BATCH, SEQ, D), 1.0),
        'c': nrm(ks[1], (BATCH, D), 1.0),
        'ada_w': nrm(ks[2], (DEPTH, D, 6 * D), 0.5 * D ** -0.5),
        'ada_b': nrm(ks[3], (DEPTH, 6 * D), 0.01),
        'norm_g': 1.0 + nrm(ks[4], (DEPTH, 2, D), 0.05),
        'even_w_in': nrm(ks[5], (N_EVEN, D, EVEN_IN), D ** -0.5),
        'even_b_f': jax.random.uniform(ks[6], (N_EVEN, FOX_HEADS), jnp.float32, 1.0, 6.0),
        'even_conv_w': nrm(ks[7], (N_EVEN, CONV_K, CONV_CH), CONV_K ** -0.5),
        'even_q_g': 1.0 + nrm(ks[8], (N_EVEN, HEAD_DIM), 0.05),
        'even_k_g': 1.0 + nrm(ks[9], (N_EVEN, HEAD_DIM), 0.05),
        'even_w_out': nrm(ks[10], (N_EVEN, CONV_CH + FOX_WIDTH, D), (CONV_CH + FOX_WIDTH) ** -0.5),
        'odd_w_in': nrm(ks[11], (N_ODD, D, ODD_IN), D ** -0.5),
        'odd_b_gate': nrm(ks[12], (N_ODD, 3 * NSA_HEADS), 0.01),
        'odd_q_g': 1.0 + nrm(ks[13], (N_ODD, HEAD_DIM), 0.05),
        'odd_k_g': 1.0 + nrm(ks[14], (N_ODD, 3, HEAD_DIM), 0.05),
        'odd_cmp_pos': nrm(ks[15], (N_ODD, 2, CMP_LEN, HEAD_DIM), 0.1),
        'odd_cmp_w1': nrm(ks[16], (N_ODD, 2, CMP_LEN * HEAD_DIM, HEAD_DIM), (CMP_LEN * HEAD_DIM) ** -0.5),
        'odd_cmp_w2': nrm(ks[17], (N_ODD, 2, HEAD_DIM, HEAD_DIM), HEAD_DIM ** -0.5),
        'odd_w_out': nrm(ks[18], (N_ODD, NSA_WIDTH, D), NSA_WIDTH ** -0.5),
        'rel_table': nrm(ks[19], (REL_BUCKETS, NSA_HEADS), 0.5),
        'peer_w_q': nrm(ks[20], (DEPTH, D, PEER_HEADS * PEER_QDIM), D ** -0.5),
        'peer_keys': nrm(ks[21], (DEPTH, 2, PEER_NKEYS, PEER_QDIM // 2), (PEER_QDIM // 2) ** -0.5),
        'peer_u': nrm(ks[22], (DEPTH, PEER_EXPERTS, D), D ** -0.5),
        'peer_v': nrm(ks[23], (DEPTH, PEER_EXPERTS, D), PEER_HEADS ** -0.5),
    }

def first_block(x, c, ada_w, ada_b, norm_g, even_w_in, even_b_f, even_conv_w, even_q_g, even_k_g,
              even_w_out, odd_w_in, odd_b_gate, odd_q_g, odd_k_g, odd_cmp_pos, odd_cmp_w1, odd_cmp_w2,
              odd_w_out, rel_table, peer_w_q, peer_keys, peer_u, peer_v):
    mods = jnp.einsum('bd,lde->lbe', jax.nn.silu(c), ada_w) + ada_b[:, None, :]
    for layer in range(DEPTH):
        sh1, sc1, g1, sh2, sc2, g2 = jnp.split(mods[layer], 6, axis=-1)
        h = modulate(rms_norm(x, norm_g[layer, 0]), sh1, sc1)
        i = layer // 2
        if layer % 2 == 0:
            y = conv_fox_mixer(h, even_w_in[i], even_b_f[i], even_conv_w[i], even_q_g[i], even_k_g[i],
                               even_w_out[i])
        else:
            y = nsa_mixer(h, odd_w_in[i], odd_b_gate[i], odd_q_g[i], odd_k_g[i], odd_cmp_pos[i],
                          odd_cmp_w1[i], odd_cmp_w2[i], rel_table, odd_w_out[i])
        x = x + g1[:, None, :] * y
        h = modulate(rms_norm(x, norm_g[layer, 1]), sh2, sc2)
        x = x + g2[:, None, :] * peer_ffn(h, peer_w_q[layer], peer_keys[layer], peer_u[layer], peer_v[layer])
    return x


N_HEADS = D_MODEL // HEAD_DIM
SWA_Q_HEADS = N_HEADS // 2
SWA_KV_HEADS = max(1, SWA_Q_HEADS // 4)
MOBA_HEADS = N_HEADS - SWA_Q_HEADS
SWA_WIDTH = SWA_Q_HEADS * HEAD_DIM
SWA_KV_WIDTH = SWA_KV_HEADS * HEAD_DIM
MOBA_WIDTH = MOBA_HEADS * HEAD_DIM
MIX_WIDTH = SWA_WIDTH + MOBA_WIDTH
IN_COLS = SWA_WIDTH + 2 * SWA_KV_WIDTH + 3 * MOBA_WIDTH
IN_SPLITS = (SWA_WIDTH,
             SWA_WIDTH + SWA_KV_WIDTH,
             SWA_WIDTH + 2 * SWA_KV_WIDTH,
             SWA_WIDTH + 2 * SWA_KV_WIDTH + MOBA_WIDTH,
             SWA_WIDTH + 2 * SWA_KV_WIDTH + 2 * MOBA_WIDTH)
SWA_WINDOW = 128
SWA_BLOCK = 128
MOBA_BLOCK = 256
MOBA_TOPK = 3
MOBA_Q_CHUNK = 128
T5_BUCKETS = 32
T5_MAX_DIST = 128
D_FF = ((8 * D_MODEL // 3 + 255) // 256) * 256
N_MOD = 9
NEG = -1e30


def rmsnorm(x, g):
    xf = x.astype(jnp.float32)
    y = xf * lax.rsqrt(jnp.mean(xf * xf, axis=-1, keepdims=True) + EPS)
    return (y * g.astype(jnp.float32)).astype(x.dtype)

def t5_bucket(dist):
    n = jnp.maximum(dist, 0)
    max_exact = T5_BUCKETS // 2
    nf = jnp.maximum(n, 1).astype(jnp.float32)
    large = max_exact + (jnp.log(nf / max_exact) / math.log(T5_MAX_DIST / max_exact)
                         * (T5_BUCKETS - max_exact)).astype(jnp.int32)
    large = jnp.minimum(large, T5_BUCKETS - 1)
    return jnp.where(n < max_exact, n, large)

def swiglu(h, w_gate, w_up, w_down):
    return (jax.nn.silu(h @ w_gate) * (h @ w_up)) @ w_down

def swa_attention(q, k, v, sinks, table):
    B_, S, Hq, dh = q.shape
    Hkv = k.shape[2]
    G = Hq // Hkv
    L = SWA_BLOCK
    nblk = S // L
    qb = q.reshape(B_, nblk, L, Hkv, G, dh)
    kb = k.reshape(B_, nblk, L, Hkv, dh)
    vb = v.reshape(B_, nblk, L, Hkv, dh)
    pad = ((0, 0), (1, 0), (0, 0), (0, 0), (0, 0))
    kw = jnp.concatenate([jnp.pad(kb, pad)[:, :-1], kb], axis=2)
    vw = jnp.concatenate([jnp.pad(vb, pad)[:, :-1], vb], axis=2)
    s = jnp.einsum('bnqhgd,bnkhd->bnhgqk', qb, kw).astype(jnp.float32) * (dh ** -0.5)
    qi = jnp.arange(L)[:, None]
    kj = jnp.arange(2 * L)[None, :]
    dist = qi + L - kj
    bias = table.T[:, t5_bucket(dist)].astype(jnp.float32).reshape(Hkv, G, L, 2 * L)
    kpos = jnp.arange(nblk)[:, None, None] * L - L + kj[None]
    valid = (dist >= 0)[None] & (dist < SWA_WINDOW)[None] & (kpos >= 0)
    s = jnp.where(valid[None, :, None, None], s + bias, NEG)
    sink = jnp.broadcast_to(sinks.astype(jnp.float32).reshape(1, 1, Hkv, G, 1, 1),
                            s.shape[:-1] + (1,))
    p = jax.nn.softmax(jnp.concatenate([s, sink], axis=-1), axis=-1)[..., :-1]
    o = jnp.einsum('bnhgqk,bnkhd->bnqhgd', p.astype(v.dtype), vw)
    return o.reshape(B_, S, Hq, dh)

def moba_attention(q, k, v, table):
    B_, S, H, dh = q.shape
    L = MOBA_BLOCK
    C = MOBA_Q_CHUNK
    nb = -(-S // L)
    Sp = nb * L
    padw = ((0, 0), (0, Sp - S), (0, 0), (0, 0))
    q, k, v = jnp.pad(q, padw), jnp.pad(k, padw), jnp.pad(v, padw)
    kb = k.reshape(B_, nb, L, H, dh).transpose(0, 3, 1, 2, 4)
    vb = v.reshape(B_, nb, L, H, dh).transpose(0, 3, 1, 2, 4)
    kmean = jnp.mean(kb, axis=3)
    topk = min(MOBA_TOPK, nb)
    nchunk = Sp // C
    qc = q.reshape(B_, nchunk, C, H, dh).transpose(1, 0, 3, 2, 4)
    scale = dh ** -0.5
    tableT = table.T.astype(jnp.float32)
    bi = jnp.arange(B_)[:, None, None, None]
    hi = jnp.arange(H)[None, :, None, None]
    hi5 = jnp.arange(H)[None, :, None, None, None]

    def chunk_fn(args):
        qblk, ci = args
        q_pos = ci * C + jnp.arange(C)
        cur = (ci * C) // L
        gate = jnp.einsum('bhcd,bhnd->bhcn', qblk, kmean)
        gate = jnp.where(jnp.arange(nb) < cur, gate, NEG)
        _, sel = lax.top_k(gate, topk)
        sel_ok = jnp.arange(topk) < cur
        k_sel = kb[bi, hi, sel]
        v_sel = vb[bi, hi, sel].reshape(B_, H, C, topk * L, dh)
        s_sel = jnp.einsum('bhcd,bhctld->bhctl', qblk, k_sel).astype(jnp.float32) * scale
        k_pos_sel = sel[..., None] * L + jnp.arange(L)
        dist_sel = q_pos[None, None, :, None, None] - k_pos_sel
        s_sel = s_sel + tableT[hi5, t5_bucket(dist_sel)]
        s_sel = jnp.where(sel_ok[None, None, None, :, None], s_sel, NEG)
        s_sel = s_sel.reshape(B_, H, C, topk * L)
        k_own = lax.dynamic_index_in_dim(kb, cur, axis=2, keepdims=False)
        v_own = lax.dynamic_index_in_dim(vb, cur, axis=2, keepdims=False)
        dist_own = q_pos[:, None] - (cur * L + jnp.arange(L))[None, :]
        s_own = jnp.einsum('bhcd,bhld->bhcl', qblk, k_own).astype(jnp.float32) * scale
        s_own = jnp.where(dist_own >= 0, s_own + tableT[:, t5_bucket(dist_own)], NEG)
        p = jax.nn.softmax(jnp.concatenate([s_sel, s_own], axis=-1), axis=-1).astype(v.dtype)
        o = (jnp.einsum('bhck,bhckd->bhcd', p[..., :topk * L], v_sel)
             + jnp.einsum('bhcl,bhld->bhcd', p[..., topk * L:], v_own))
        return o

    out = lax.map(chunk_fn, (qc, jnp.arange(nchunk)))
    out = out.transpose(1, 0, 3, 2, 4).reshape(B_, Sp, H, dh)
    return out[:, :S]

def hybrid_mixer(h, w_in, b_in, w_out, sinks, group_gain, rel_bias):
    B_, S, _ = h.shape
    proj = h @ w_in + b_in
    qa, ka, va, qb, kb, vb = jnp.split(proj, IN_SPLITS, axis=-1)
    qa = qa.reshape(B_, S, SWA_Q_HEADS, HEAD_DIM)
    ka = ka.reshape(B_, S, SWA_KV_HEADS, HEAD_DIM)
    va = va.reshape(B_, S, SWA_KV_HEADS, HEAD_DIM)
    qb = qb.reshape(B_, S, MOBA_HEADS, HEAD_DIM)
    kb = kb.reshape(B_, S, MOBA_HEADS, HEAD_DIM)
    vb = vb.reshape(B_, S, MOBA_HEADS, HEAD_DIM)
    ya = swa_attention(qa, ka, va, sinks, rel_bias[:, :SWA_Q_HEADS]).reshape(B_, S, SWA_WIDTH)
    yb = moba_attention(qb, kb, vb, rel_bias[:, SWA_Q_HEADS:]).reshape(B_, S, MOBA_WIDTH)
    y = jnp.concatenate([rmsnorm(ya, group_gain[:SWA_WIDTH]),
                         rmsnorm(yb, group_gain[SWA_WIDTH:])], axis=-1)
    return y @ w_out

def second_inputs(seed: int = 0) -> dict:
    key = jax.random.key(seed)
    ks = jax.random.split(key, 16)
    f = jnp.float32

    def w(k, shape, fan_in, gain=1.0):
        return jax.random.normal(k, shape, f) * (gain * fan_in ** -0.5)

    return {
        'x': jax.random.normal(ks[0], (BATCH, SEQ, D_MODEL), f),
        'c': jax.random.normal(ks[1], (BATCH, D_MODEL), f),
        'rel_bias': 0.5 * jax.random.normal(ks[2], (T5_BUCKETS, N_HEADS), f),
        'ada_w': w(ks[3], (DEPTH, D_MODEL, N_MOD * D_MODEL), D_MODEL, 0.5),
        'ada_b': 0.01 * jax.random.normal(ks[4], (DEPTH, N_MOD * D_MODEL), f),
        'norm_pre': 1.0 + 0.05 * jax.random.normal(ks[5], (DEPTH, 3, D_MODEL), f),
        'norm_post': 1.0 + 0.05 * jax.random.normal(ks[6], (DEPTH, 3, D_MODEL), f),
        'ffn_w_gate': w(ks[7], (DEPTH, 2, D_MODEL, D_FF), D_MODEL),
        'ffn_w_up': w(ks[8], (DEPTH, 2, D_MODEL, D_FF), D_MODEL),
        'ffn_w_down': w(ks[9], (DEPTH, 2, D_FF, D_MODEL), D_FF),
        'mix_w_in': w(ks[10], (DEPTH, D_MODEL, IN_COLS), D_MODEL),
        'mix_b_in': 0.01 * jax.random.normal(ks[11], (DEPTH, IN_COLS), f),
        'mix_w_out': w(ks[12], (DEPTH, MIX_WIDTH, D_MODEL), MIX_WIDTH),
        'attn_sinks': jax.random.normal(ks[13], (DEPTH, SWA_Q_HEADS), f),
        'group_gain': 1.0 + 0.05 * jax.random.normal(ks[14], (DEPTH, MIX_WIDTH), f),
    }

def second_block(x, c, rel_bias, ada_w, ada_b, norm_pre, norm_post, ffn_w_gate, ffn_w_up,
              ffn_w_down, mix_w_in, mix_b_in, mix_w_out, attn_sinks, group_gain):
    c_act = jax.nn.silu(c)
    for l in range(DEPTH):
        mod = (c_act @ ada_w[l] + ada_b[l])[:, None, :]
        sh1, sc1, g1, sh2, sc2, g2, sh3, sc3, g3 = jnp.split(mod, N_MOD, axis=-1)
        h = rmsnorm(x, norm_pre[l, 0]) * (1.0 + sc1) + sh1
        y = swiglu(h, ffn_w_gate[l, 0], ffn_w_up[l, 0], ffn_w_down[l, 0])
        x = x + 0.5 * g1 * rmsnorm(y, norm_post[l, 0])
        h = rmsnorm(x, norm_pre[l, 1]) * (1.0 + sc2) + sh2
        y = hybrid_mixer(h, mix_w_in[l], mix_b_in[l], mix_w_out[l], attn_sinks[l],
                         group_gain[l], rel_bias)
        x = x + g2 * rmsnorm(y, norm_post[l, 1])
        h = rmsnorm(x, norm_pre[l, 2]) * (1.0 + sc3) + sh3
        y = swiglu(h, ffn_w_gate[l, 1], ffn_w_up[l, 1], ffn_w_down[l, 1])
        x = x + 0.5 * g3 * rmsnorm(y, norm_post[l, 2])
    return x


def setup_inputs(seed=0):
    out = dict(first_inputs(seed))
    for name, value in second_inputs(seed + 1).items():
        if name != "x":
            out[name + "_2"] = value
    return out


def reference(
    x, c, ada_w, ada_b, norm_g, even_w_in, even_b_f, even_conv_w, even_q_g, even_k_g,
    even_w_out, odd_w_in, odd_b_gate, odd_q_g, odd_k_g, odd_cmp_pos, odd_cmp_w1, odd_cmp_w2,
    odd_w_out, rel_table, peer_w_q, peer_keys, peer_u, peer_v, c_2, rel_bias_2, ada_w_2,
    ada_b_2, norm_pre_2, norm_post_2, ffn_w_gate_2, ffn_w_up_2, ffn_w_down_2, mix_w_in_2,
    mix_b_in_2, mix_w_out_2, attn_sinks_2, group_gain_2,
):
    x = first_block(
        x, c, ada_w, ada_b, norm_g, even_w_in, even_b_f, even_conv_w, even_q_g, even_k_g,
        even_w_out, odd_w_in, odd_b_gate, odd_q_g, odd_k_g, odd_cmp_pos, odd_cmp_w1, odd_cmp_w2,
        odd_w_out, rel_table, peer_w_q, peer_keys, peer_u, peer_v,
    )
    return second_block(
        x, c_2, rel_bias_2, ada_w_2, ada_b_2, norm_pre_2, norm_post_2, ffn_w_gate_2, ffn_w_up_2,
        ffn_w_down_2, mix_w_in_2, mix_b_in_2, mix_w_out_2, attn_sinks_2, group_gain_2,
    )


_drawn_inputs = setup_inputs


def setup_inputs(seed=0):
    import zlib

    import numpy as np

    out = dict(_drawn_inputs(seed))
    spreads = {}
    factors = {'ada_b': 3.166,
     'even_q_g': 8.0,
     'even_k_g': 8.0,
     'odd_b_gate': 48.79,
     'odd_q_g': 8.0,
     'odd_k_g': 8.0,
     'odd_cmp_pos': 4.393,
     'ada_b_2': 2.764,
     'mix_b_in_2': 5.7,
     'attn_sinks_2': 4.736,
     'group_gain_2': 8.207,
     'rel_table': 4.234}
    for name, (base, spread) in spreads.items():
        noise = np.random.default_rng([zlib.crc32(name.encode()), seed]).standard_normal(out[name].shape)
        drawn = base * np.exp(spread * noise) if base else spread * noise
        out[name] = jnp.asarray(drawn.astype(out[name].dtype))
    for name, factor in factors.items():
        out[name] = (out[name] * factor).astype(out[name].dtype)
    return out
```

```python
import math
from contextlib import ExitStack

import numpy as np

import concourse.bass as bass
from concourse import mybir

F32 = mybir.dt.float32
U32 = mybir.dt.uint32
ALU = mybir.AluOpType
ACT = mybir.ActivationFunctionType
AX = mybir.AxisListType

P = 128
S = 256
TT = S // P
D = 1024
KD = D // P
HD = 64
SCALE = HD ** -0.5
EPS = 1e-6
BIG = 1e30
FMAX = 3.0e38
UNIT = 1024
SLOTS = 4
FF = 2816
NF = FF // P
NE = 128
PH = 8
TOPK = 16
NCMP = 15
CMP_LEN = 32
NVEC = 30
TW = 384

_COLS = [("ident", P), ("ones", P), ("bd", P), ("iota", P), ("cmask", TW), ("rowmask", 1),
         ("adab", NVEC * KD), ("c", 2 * KD), ("norm", 4 * KD), ("pre", 6 * KD), ("post", 6 * KD),
         ("convw", 12), ("bf", 1), ("fqg", 1), ("fkg", 1), ("nqg", 1), ("nkg", 3),
         ("pos", 2 * CMP_LEN), ("w2", 2 * P), ("keys", 2 * NE), ("bgate", 48),
         ("mixb", 2 * 13), ("gain", 2 * KD), ("sinks", 2 * 8)]
COL = {}
_at = 0
for _n, _w in _COLS:
    COL[_n] = (_at, _w)
    _at += _w
NPAR = _at
TAB = {"rel": (0, 16), "rel2": (16, 16), "hot": (32, 512), "mask": (544, 512), "mask2": (1056, 512)}
NTAB = 1568

MIX0_UNITS = 1 + 24 + 8
MIX1_UNITS = 12 + 8 + 1 + 8 + 8
PEER_UNITS = 8 + 2 * NE
FFN_UNITS = 3 * NF
HYB_UNITS = 2 + 16 + 8
PHASES = ["mix0", "peer0", "mix1", "peer1", "ffn0", "hyb0", "ffn1", "ffn2", "hyb1", "ffn3"]
_SIZE = {"mix0": MIX0_UNITS, "mix1": MIX1_UNITS, "peer": PEER_UNITS, "ffn": FFN_UNITS, "hyb": HYB_UNITS}


def phase_units(name):
    return _SIZE[name] if name in _SIZE else _SIZE[name[:-1]]


def program(nc, xT, par, tab, vrow, ada, stream, outT, upto=None):
    phases = PHASES[:upto]
    start = {}
    units = 0
    for ph in phases:
        start[ph] = units
        units += phase_units(ph)
    att0 = {"mix0": 0, "mix1": 8, "hyb0": 8 + 48, "hyb1": 8 + 48 + 16}
    pair0 = {"mix0": 0, "mix1": 4, "hyb0": 12, "hyb1": 20}
    bias0 = {"mix1": 0, "hyb0": 8, "hyb1": 16}
    hn0 = {"mix0": 0, "mix1": 8}
    norm_no = {"mix0": 0, "peer0": 1, "mix1": 2, "peer1": 3}
    k = 4
    for ph in PHASES[4:]:
        norm_no[ph] = k
        k += 2

    with ExitStack() as ctx:
        def sb(name, shape, dt=F32):
            return ctx.enter_context(nc.sbuf_tensor(name, shape, dt))

        def sem(name):
            return ctx.enter_context(nc.semaphore(name))

        bias_rows = nc.dram_tensor("bias_rows", (32, P * 512), F32).ap()

        ps = [ctx.enter_context(nc.psum_tensor(f"ps{i}", [P, 512], F32)) for i in range(8)]
        x = sb("x", [P, KD, S])
        hT = sb("hT", [P, KD, S])
        ring = sb("ring", [P, SLOTS, UNIT])
        mods = sb("mods", [P, NVEC, KD])
        prm = sb("prm", [P, NPAR])
        stat = sb("stat", [P, 2, S])
        acol = sb("acol", [P, KD])
        small = sb("small", [P, 64])
        arena = sb("arena", [P, NE, S])
        score = sb("score", [P, TT, 16, NE])
        eq = sb("eq", [P, NE, TOPK])
        pick = sb("pick", [P, 7, NE])

        flat = arena[:].rearrange("p a b -> p (a b)")
        used = [0]

        def cut(n, shape=None):
            a = used[0]
            used[0] += n
            assert used[0] <= NE * S
            return flat[:, a:a + n]

        def pc(name, i=0, n=None):
            a, w = COL[name]
            return prm[:, a + i:a + i + (w - i if n is None else n)]

        ident, ones, bd, iota = pc("ident"), pc("ones"), pc("bd"), pc("iota")
        eps = small[:, 0:1]

        sq = cut(KD * S).rearrange("p (a b) -> p a b", a=KD)
        oT = cut(KD * S).rearrange("p (a b) -> p a b", a=KD)
        qs = cut(S)
        ks = cut(6 * S).rearrange("p (a b) -> p a b", b=S)
        v_sb = cut(4 * TT * 2 * P).rearrange("p (a b) -> p a b", b=P)
        neg = cut(2 * TW).rearrange("p (a b) -> p a b", a=2)
        prob = cut(2 * TW).rearrange("p (a b) -> p a b", a=2)
        pt = cut(2 * TW).rearrange("p (a b) -> p a b", a=2)
        nb = cut(2 * TW).rearrange("p (a b) -> p a b", a=2)
        hsq = cut(S)
        hstd = cut(2 * S).rearrange("p (a b) -> p a b", a=2)
        hrec = cut(S)
        ccs = cut(S)
        u_pad = cut(S + 2)
        conv_t = cut(2 * S).rearrange("p (a b) -> p a b", a=2)
        cum = cut(S)
        ftmp = cut(4 * S).rearrange("p (a b) -> p a b", a=4)
        cumrow = cut(8 * S).rearrange("p (a b) -> p a b", a=8)
        gates = cut(TT * 48).rearrange("p (a b) -> p a b", a=TT)
        gsum = cut(TT * 48).rearrange("p (a b) -> p a b", a=TT)
        blk = cut(2 * CMP_LEN * 2 * NCMP).rearrange("p (a l c n) -> p a l c n", a=2, l=CMP_LEN, c=2)
        kcv = cut(4 * S).rearrange("p (a b) -> p a b", a=4)
        chid = cut(2 * 32).rearrange("p (a b) -> p a b", a=2)
        kc_sb = cut(32)
        vc_sb = cut(2 * P).rearrange("p (a b) -> p a b", a=2)
        negm = cut(4).rearrange("p (a b) -> p a b", a=2)
        rows = cut(4).rearrange("p (a b) -> p a b", a=2)
        sink_e = cut(4).rearrange("p (a b) -> p a b", a=2)
        rinv = cut(4).rearrange("p (a b) -> p a b", a=2)
        coef = cut(4).rearrange("p (a b) -> p a b", a=2)
        nsk = cut(2)
        vr = cut(1280).rearrange("p (l a b) -> p l a b", l=2, a=5)
        hid = cut(NF * S).rearrange("p (a b) -> p a b", a=NF)
        sl = cut(2 * S).rearrange("p (a b) -> p a b", a=2)
        gtmp = cut(2 * S).rearrange("p (a b) -> p a b", a=2)
        used[0] = 0
        adaw = cut(2 * 8 * UNIT).rearrange("p (a k n) -> p a k n", a=2, k=8)
        acc = cut(2 * UNIT).rearrange("p (a n) -> p a n", a=2)
        tabs = cut(NTAB)
        erow = cut(2 * 512).rearrange("p (a n) -> p a n", a=2)
        mraw = cut(NVEC * KD).rearrange("p (a b) -> p a b", a=NVEC)
        cact = cut(2 * KD)
        r_sv = pick[:, 0:2, :].rearrange("p a b -> p (a b)").rearrange("p (g k) -> p g k", g=16)
        r_si = sb("r_si", [P, 16, TOPK], U32)
        r_sif = pick[:, 2:4, :].rearrange("p a b -> p (a b)").rearrange("p (g k) -> p g k", g=16)
        r_cv = pick[:, 4, :].rearrange("p (g k) -> p g k", g=PH)
        r_ci = sb("r_ci", [P, PH, TOPK], U32)
        r_ab = sb("r_ab", [P, 2, NE], U32)
        r_abf = pick[:, 5:7, :]
        r_out = sb("r_out", [P, TT, 3, NE])
        r_outT = sb("r_outT", [P, 3, S])
        r_sum = small[:, 8:16]
        r_rec = small[:, 16:24]
        hot = score[:].rearrange("p a g n -> p (a g n)")[:, 0:2 * 2 * 4 * NE].rearrange(
            "p (b w t n) -> p b w t n", b=2, w=2, t=4)
        pq = eq[:].rearrange("p a b -> p (a b)")[:, 0:2 * S].rearrange("p (a b) -> p a b", a=2)

        away = eq[:].rearrange("p a b -> p (a b)")[:, 0:2 * 4 * NE].rearrange("p (b t n) -> p b t n", b=2, t=4)

        passed = sem("passed")
        params_in = sem("params_in")
        loaded = [sem(f"unit_loaded{s}") for s in range(SLOTS)]
        unit_done = sem("unit_done")
        setup_done = sem("setup_done")
        c_ready = sem("c_ready")
        tab_ready = sem("tab_ready")
        tab_read = sem("tab_read")
        bias_written = sem("bias_written")
        ada_loaded = [sem(f"ada_loaded{s}") for s in range(2)]
        ada_acc = sem("ada_acc")
        ada_sum = sem("ada_sum")
        ada_out = sem("ada_out")
        x_ready = sem("x_ready")
        sq_ready = sem("sq_ready")
        ss_ready = sem("ss_ready")
        std_ready = sem("std_ready")
        mid_ready = sem("mid_ready")
        h_ready = sem("h_ready")
        y_ready = sem("y_ready")
        silu_ready = sem("silu_ready")
        ffn_h = sem("ffn_h")
        hn_sq = sem("hn_sq")
        hn_ss = sem("hn_ss")
        hn_std = sem("hn_std")
        hn_out = sem("hn_out")
        logf_ready = sem("logf_ready")
        logf_act = sem("logf_act")
        cum_ready = sem("cum_ready")
        cum_row = sem("cum_row")
        conv_c = sem("conv_c")
        conv_u = sem("conv_u")
        conv_out = sem("conv_out")
        v_ready = sem("v_ready")
        q_ready = sem("q_ready")
        s_ready = sem("s_ready")
        neg_ready = sem("neg_ready")
        exp_ready = sem("exp_ready")
        coef_ready = sem("coef_ready")
        pn_ready = sem("pn_ready")
        t_ready = sem("t_ready")
        pt_ready = sem("pt_ready")
        o_done = sem("o_done")
        o_read = sem("o_read")
        bias_in = sem("bias_in")
        kv_out = sem("kv_out")
        kv_raw = sem("kv_raw")
        blk_ready = sem("blk_ready")
        cmp_h = sem("cmp_h")
        cmp_mm = sem("cmp_mm")
        cmp_vc = sem("cmp_vc")
        gate_z = sem("gate_z")
        gate_s = sem("gate_s")
        gate_ready = sem("gate_ready")
        on_ready = sem("on_ready")
        pq_ready = sem("pq_ready")
        ps_ready = sem("ps_ready")
        ps_read = sem("ps_read")
        gelu_ready = sem("gelu_ready")
        rexp_in = sem("rexp_in")
        rexp_out = sem("rexp_out")
        route_ready = sem("route_ready")
        routeT_ready = sem("routeT_ready")
        routeT_read = sem("routeT_read")
        hotA_ready = sem("hotA_ready")
        hotB_ready = sem("hotB_ready")
        g_ready = sem("g_ready")
        g_read = sem("g_read")
        out_done = sem("out_done")

        def slot_of(unit):
            return ring[:, unit % SLOTS, :].rearrange("p (k n) -> p k n", k=KD)

        def wait_unit(pe, unit, it=0, per=0):
            pe.wait_ge(loaded[unit % SLOTS], it * (per // SLOTS * 16) + 16 * (unit // SLOTS + 1))

        def wait_used(eng, unit, it=0, per=0):
            eng.wait_ge(unit_done, it * per + unit + 1)

        def wait_alone(eng, semaphore, value):
            eng.wait_ge(semaphore, value)
            eng.sem_inc(passed, 1)

        block = ctx.enter_context(nc.Block())

        @block.sync
        def _(sp):
            sp.dma_start(prm[:], par).then_inc(params_in, 16)
            sp.dma_start(tabs[0:32, :], tab).then_inc(params_in, 16)
            sp.dma_start(x[:], xT).then_inc(params_in, 16)
            for par_ in range(2):
                sp.dma_start(adaw[:, par_], ada[par_].rearrange("k p n -> p k n")).then_inc(ada_loaded[par_], 16)
            with sp.Fori(1, NVEC // 2) as i:
                for par_ in range(2):
                    sp.wait_ge(ada_acc, i * 2 + (par_ - 1))
                    sp.dma_start(adaw[:, par_], ada[i * 2 + par_].rearrange("k p n -> p k n")).then_inc(
                        ada_loaded[par_], 16)
            for u in range(SLOTS):
                sp.dma_start(ring[:, u], stream[u]).then_inc(loaded[u], 16)
            rounds = units // SLOTS
            with sp.Fori(1, rounds) as i:
                for s in range(SLOTS):
                    sp.wait_ge(unit_done, i * SLOTS + (s - SLOTS + 1))
                    sp.dma_start(ring[:, s], stream[i * SLOTS + s]).then_inc(loaded[s], 16)
            for u in range(rounds * SLOTS, units):
                sp.wait_ge(unit_done, u - SLOTS + 1)
                sp.dma_start(ring[:, u % SLOTS], stream[u]).then_inc(loaded[u % SLOTS], 16)
            sp.wait_ge(x_ready, KD * len(phases))
            sp.dma_start(outT, x[:]).then_inc(out_done, 16)
            sp.wait_ge(out_done, 16)

        @block.tensor
        def _(pe):
            def products(out, unit, rhs, it=0, per=0, m=P, inc=True):
                w = slot_of(unit)
                wait_unit(pe, unit, it, per)
                for kt in range(KD):
                    mm = pe.matmul(out, w[:, kt, 0:m], rhs(kt), start=(kt == 0), stop=(kt == KD - 1))
                mm.then_inc(unit_done, 1)

            def products_t(bank, unit, n=P, it=0, per=0, brow=None):
                w = slot_of(unit)
                wait_unit(pe, unit, it, per)
                for tt in range(TT):
                    out = bank[:, tt * n:(tt + 1) * n]
                    for kt in range(KD):
                        mm = pe.matmul(out, hT[:, kt, tt * P:(tt + 1) * P], w[:, kt, 0:n],
                                       start=(kt == 0), stop=(kt == KD - 1 and brow is None))
                    if brow is not None:
                        mm = pe.matmul(out, ones[0:1, :], brow, start=False, stop=True)
                mm.then_inc(unit_done, 1)

            def sum_squares(no):
                for kt in range(KD):
                    pe.wait_ge(sq_ready, 4 * no + kt // 2 + 1)
                    mm = pe.matmul(ps[0][:, 0:S], ones, sq[:, kt, :], start=(kt == 0), stop=(kt == KD - 1))
                mm.then_inc(ss_ready, 1)

            def head_norm(c, bank=ps[3]):
                pe.wait_ge(hn_sq, c + 1)
                pe.wait_ge(hn_std, c)
                pe.matmul(bank[:, 0:S], bd, hsq, start=True, stop=True).then_inc(hn_ss, 1)

            def scores(g, k, inst):
                pe.wait_ge(neg_ready, g + k + 1)
                h = slice(inst["half"] * HD, inst["half"] * HD + HD)
                bank = ps[4 + k % 2]
                if inst["kind"] == "cmp":
                    for tt in range(TT):
                        mm = pe.matmul(bank[:, tt * NCMP:(tt + 1) * NCMP], inst["q"][h, tt * P:(tt + 1) * P],
                                       inst["k"][h, :], start=True, stop=True)
                else:
                    row = inst.get("row")
                    for tt in range(TT):
                        out = bank[:, 0:P] if tt == 0 else bank[:, P:TW]
                        n = P * (tt + 1)
                        mm = pe.matmul(out, inst["q"][h, tt * P:(tt + 1) * P], inst["k"][h, 0:n],
                                       start=True, stop=row is None)
                        if row is not None:
                            mm = pe.matmul(out, ones[0:1, :], row(n), start=False, stop=True)
                mm.then_inc(s_ready, 1)

            def attention(g, pairs, insts):
                scores(g, 0, insts[0])
                scores(g, 1, insts[1])
                first = True
                for k, inst in enumerate(insts):
                    bank = ps[6 + k % 2]
                    pr, pT = prob[:, k % 2], pt[:, k % 2]
                    pe.wait_ge(pn_ready, g + k + 1)
                    if inst["kind"] == "cmp":
                        for tt in range(TT):
                            mm = pe.transpose(bank[0:NCMP, tt * P:(tt + 1) * P],
                                              pr[:, tt * NCMP:(tt + 1) * NCMP], ident)
                    else:
                        for b in range(3):
                            mm = pe.transpose(bank[:, b * P:(b + 1) * P], pr[:, b * P:(b + 1) * P], ident)
                    mm.then_inc(t_ready, 1)
                    if k + 2 < len(insts):
                        scores(g, k + 2, insts[k + 2])
                    pe.wait_ge(pt_ready, g + k + 1)
                    if first:
                        pe.wait_ge(o_read, pairs)
                        first = False
                    half = inst["half"]
                    out = ps[2 + half][half * HD:half * HD + HD, 0:S]
                    begins, ends = inst["begins"], inst["ends"]
                    if inst["kind"] == "cmp":
                        mm = pe.matmul(out, inst["v"], pT[0:NCMP, 0:S], start=begins, stop=ends)
                    else:
                        pe.matmul(out, inst["v"][0], pT[:, 0:S], start=begins, stop=False)
                        mm = pe.matmul(out[:, P:S], inst["v"][1], pT[:, S:TW], start=False, stop=ends)
                mm.then_inc(o_done, 1)

            def output(ph, unit, no_done):
                for n in range(KD):
                    products(ps[4 + n // 2][:, (n % 2) * S:(n % 2 + 1) * S], unit + n, lambda kt: oT[:, kt, :])
                mm = None

            def spread(unit, it, per, rhs, first, last):
                w = slot_of(unit)
                wait_unit(pe, unit, it, per)
                for n in range(KD):
                    mm = pe.matmul(ps[4 + n // 2][:, (n % 2) * S:(n % 2 + 1) * S], w[:, n, :], rhs,
                                   start=first and n % 2 == 0, stop=last, skip_group_check=True)
                mm.then_inc(unit_done, 1)

            def mix0(u):
                pe.wait_ge(h_ready, KD * (norm_no_h["mix0"] + 1))
                products(ps[0][0:8, 0:S], u, lambda kt: hT[:, kt, :], m=8)
                u += 1
                pe.wait_ge(logf_ready, 1)
                with pe.Fori(0, 2) as i:
                    for e in range(2):
                        v = u + 6 * e
                        r = i * 2 + e
                        h = lambda kt: hT[:, kt, :]
                        products(ps[0][:, 0:S], v, h, i, 12)
                        products(ps[1][:, 0:S], v + 1, h, i, 12)
                        pe.wait_ge(o_read, r)
                        products(ps[2][:, 0:S], v + 2, h, i, 12)
                        pe.wait_ge(conv_c, r + 1)
                        products(ps[0][:, 0:S], v + 3, h, i, 12)
                        head_norm(r * 2)
                        pe.wait_ge(conv_u, r + 1)
                        products(ps[1][:, 0:S], v + 4, h, i, 12)
                        head_norm(r * 2 + 1)
                        pe.wait_ge(conv_out, r + 1)
                        products_t(ps[2], v + 5, P, i, 12)
                        pe.wait_ge(hn_out, r * 2 + 2)
                        pe.wait_ge(v_ready, r + 1)
                        if e == 0:
                            pe.wait_ge(cum_row, 16)
                        attention(r * 2, r, [
                            dict(half=f, kind="full", q=qs, k=ks[:, 0], begins=True, ends=True,
                                 v=[v_sb[:, b, f * HD:f * HD + HD] for b in range(2)],
                                 row=lambda n, hd=r * 2 + f: cumrow[0:1, hd, 0:n]) for f in range(2)])
                u += 24
                pe.wait_ge(o_read, 4)
                output("mix0", u, 0)

            def mix1(u):
                pe.wait_ge(h_ready, KD * (norm_no_h["mix1"] + 1))
                h = lambda kt: hT[:, kt, :]
                hn = hn0["mix1"]
                for n in range(4):
                    if n >= 2:
                        pe.wait_ge(kv_raw, n - 1)
                    products(ps[n % 2][:, 0:S], u + n, h)
                pe.wait_ge(kv_raw, 4)
                for n in range(4):
                    if n >= 2:
                        pe.wait_ge(hn_out, hn + n - 1)
                    products(ps[n % 2][:, 0:S], u + 4 + n, h)
                    head_norm(hn + n)
                for n in range(4):
                    if n < 2:
                        pe.wait_ge(hn_out, hn + 3 + n)
                    else:
                        pe.wait_ge(kv_out, n - 1)
                    products_t(ps[n % 2], u + 8 + n)
                pe.wait_ge(kv_out, 4)
                u += 12
                for a in range(2):
                    pe.wait_ge(blk_ready, 2 * (a + 1))
                    for q in range(4):
                        w = slot_of(u + 4 * a + q)
                        wait_unit(pe, u + 4 * a + q)
                        for l in range(8):
                            mm = pe.matmul(ps[a][:, 0:2 * NCMP], w[:, l, :], blk[:, a, q * 8 + l, :, :],
                                           start=(q == 0 and l == 0), stop=(q == 3 and l == 7))
                        mm.then_inc(unit_done, 1)
                u += 8
                pe.wait_ge(cmp_h, 1)
                pe.matmul(ps[0][:, 0:2 * NCMP], pc("w2", 0, P), chid[:, 0, 0:2 * NCMP],
                          start=True, stop=True).then_inc(cmp_mm, 1)
                pe.wait_ge(hn_sq, hn + 5)
                pe.matmul(ps[3][:, 0:2 * NCMP], bd, hsq[:, 0:2 * NCMP], start=True, stop=True).then_inc(hn_ss, 1)
                pe.wait_ge(cmp_h, 2)
                for c in range(2):
                    mm = pe.matmul(ps[1][0:NCMP, c * P:(c + 1) * P], chid[:, 1, c * NCMP:(c + 1) * NCMP],
                                   pc("w2", P, P), start=True, stop=True)
                mm.then_inc(cmp_mm, 1)
                pe.wait_ge(hn_out, hn + 5)
                products_t(ps[0], u, 48)
                u += 1
                pe.wait_ge(gate_ready, 1)
                pe.wait_ge(cmp_vc, 1)
                with pe.Fori(0, 2) as i:
                    for e in range(4):
                        r = i * 4 + e
                        half = e % 2
                        products(ps[0][:, 0:S], u + e, h, i, 4)
                        head_norm(r + (hn + 5), ps[1])
                        pe.wait_ge(hn_out, r + (hn + 6))
                        attention(r * 6 + att0["mix1"], r + pair0["mix1"], [
                            dict(half=f, kind="cmp" if kind == 0 else "full", q=qs,
                                 k=kc_sb[:, half * NCMP:(half + 1) * NCMP] if kind == 0 else ks[:, 1 + 2 * (kind - 1) + half],
                                 v=(vc_sb[0:NCMP, half, f * HD:f * HD + HD] if kind == 0 else
                                    [v_sb[:, (4 * (kind - 1)) + 2 * half + b, f * HD:f * HD + HD] for b in range(2)]),
                                 begins=kind == 0, ends=kind == 2)
                            for kind in range(3) for f in range(2)])
                u += 8
                pe.wait_ge(o_read, pair0["mix1"] + 8)
                output("mix1", u, 0)

            def hyb(ph, l, u):
                pe.wait_ge(h_ready, KD * (norm_no_h[ph] + 1))
                h = lambda kt: hT[:, kt, :]
                products(ps[0][:, 0:S], u, h)
                pe.wait_ge(cum_row, 32)
                products_t(ps[1], u + 1, brow=vr[0:1, l, 0, :])
                u += 2
                pe.wait_ge(q_ready, 13 * l + 1)
                pe.wait_ge(v_ready, 4 + 5 * l + 1)
                with pe.Fori(0, 4) as i:
                    products(ps[0][:, 0:S], u, h, i, 4)
                    pe.wait_ge(q_ready, i * 3 + (13 * l + 2))
                    attention(i * 4 + att0[ph], i * 2 + pair0[ph], [
                        dict(half=f, kind="full", q=qs, k=ks[:, 1], begins=True, ends=True,
                             v=[v_sb[:, 2 + b, f * HD:f * HD + HD] for b in range(2)]) for f in range(2)])
                    products(ps[0][:, 0:S], u + 1, h, i, 4)
                    products(ps[1][:, 0:S], u + 2, h, i, 4)
                    pe.wait_ge(o_read, i * 2 + (pair0[ph] + 1))
                    products_t(ps[2], u + 3, P, i, 4, brow=vr[0:1, l, i + 1, :])
                    pe.wait_ge(q_ready, i * 3 + (13 * l + 4))
                    pe.wait_ge(v_ready, i + (4 + 5 * l + 2))
                    attention(i * 4 + (att0[ph] + 2), i * 2 + (pair0[ph] + 1), [
                        dict(half=f, kind="full", q=qs, k=ks[:, 0], begins=True, ends=True,
                             v=[v_sb[:, b, f * HD:f * HD + HD] for b in range(2)]) for f in range(2)])
                u += 16
                pe.wait_ge(o_read, pair0[ph] + 8)
                for grp in range(2):
                    for kt in range(4):
                        pe.wait_ge(on_ready, 6 * l + 2)
                        mm = pe.matmul(ps[grp][:, 0:S], ones, sq[:, 4 * grp + kt, :], start=(kt == 0), stop=(kt == 3))
                mm.then_inc(on_ready, 1)
                pe.wait_ge(on_ready, 6 * l + 6)
                output(ph, u, 0)

            def ffn(ph, no, u):
                pe.wait_ge(h_ready, KD * (norm_no_h[ph] + 1))
                h = lambda kt: hT[:, kt, :]
                with pe.Fori(0, NF // 2) as i:
                    for e in range(2):
                        pe.wait_ge(ffn_h, i * 2 + (NF * no + e + 1))
                        products(ps[2 * e][:, 0:S], u + 2 * e, h, i, 4)
                        products(ps[2 * e + 1][:, 0:S], u + 2 * e + 1, h, i, 4)
                u += 2 * NF
                pe.wait_ge(ffn_h, NF * (no + 1) + 2)
                for f in range(2):
                    spread(u + f, 0, 0, hid[:, f, :], f == 0, False)
                with pe.Fori(0, 4) as i:
                    for e in range(4):
                        spread(u + 2 + e, i, 4, hid[:, i * 4 + (2 + e), :], False, False)
                for f in range(18, NF):
                    spread(u + f, 0, 0, hid[:, f, :], False, f == NF - 1)

            def peer(ph, l, u):
                pe.wait_ge(h_ready, KD * (norm_no_h[ph] + 1))
                h = lambda kt: hT[:, kt, :]
                keys = pc("keys", l * NE, NE)
                for hd in range(PH):
                    if hd >= 2:
                        pe.wait_ge(pq_ready, PH * l + hd - 1)
                    products(ps[hd % 2][:, 0:S], u + hd, h)
                    pe.wait_ge(pq_ready, PH * l + hd + 1)
                    if hd >= 2:
                        pe.wait_ge(ps_read, PH * l + hd - 1)
                    for tt in range(TT):
                        for half in range(2):
                            rows_ = slice(half * HD, half * HD + HD)
                            mm = pe.matmul(ps[2 + 2 * (hd % 2) + half][:, tt * P:(tt + 1) * P],
                                           pq[rows_, hd % 2, tt * P:(tt + 1) * P], keys[rows_, :],
                                           start=True, stop=True)
                    mm.then_inc(ps_ready, 1)
                u += PH
                pe.wait_ge(ps_read, PH * (l + 1))
                with pe.Fori(0, NE // 4) as i:
                    for e in range(4):
                        pe.wait_ge(gelu_ready, i * 4 + (NE * l + e + 1))
                        products(ps[e % 2][:, 0:S], u + e, h, i, 4)
                u += NE
                for tt in range(TT):
                    pe.wait_ge(route_ready, TT * l + tt + 1)
                    for w in range(3):
                        mm = pe.transpose(ps[2][:, w * P:(w + 1) * P] if tt == 0 else ps[3][:, w * P:(w + 1) * P],
                                          r_out[:, tt, w, :], ident)
                    mm.then_inc(routeT_ready, 1)
                pe.wait_ge(routeT_read, TT * (l + 1))
                with pe.Fori(0, S // 8) as i:
                    for e in range(2):
                        pe.wait_ge(hotA_ready, i * 2 + (S // 4 * l + e + 1))
                        pe.wait_ge(hotB_ready, i * 2 + (S // 4 * l + e + 1))
                        pe.wait_ge(g_read, i * 2 + (S // 4 * l + e + 1))
                        for t in range(4):
                            mm = pe.matmul(ps[2 + e][:, t * NE:(t + 1) * NE], hot[:, e, 0, t, :], hot[:, e, 1, t, :],
                                           start=True, stop=True)
                        mm.then_inc(g_ready, 1)
                pe.wait_ge(g_read, S // 4 * (l + 1) + 2)
                for j in range(4):
                    spread(u + j, 0, 0, arena[:, j, :], j == 0, False)
                with pe.Fori(0, NE // 4 - 2) as i:
                    for e in range(4):
                        spread(u + 4 + e, i, 4, arena[:, i * 4 + (4 + e), :], False, False)
                for j in range(NE - 4, NE):
                    spread(u + j, 0, 0, arena[:, j, :], False, j == NE - 1)

            pe.wait_ge(params_in, 48)
            pe.wait_ge(tab_ready, 1)
            for a, name in enumerate(("rel", "rel2")):
                c0, w = TAB[name]
                h0 = TAB["hot"][0]
                mm = pe.matmul(ps[2 + a][0:16, :], tabs[0:32, c0:c0 + w], tabs[0:32, h0:h0 + 512], start=True, stop=True)
            mm.then_inc(tab_read, 1)
            with pe.Fori(0, NVEC // 2) as i:
                for e in range(2):
                    pe.wait_ge(ada_acc, i * 2 + (e + 1))
                    pe.wait_ge(ada_out, i * 2 + (e + 1))
                    for n in range(KD):
                        mm = pe.matmul(ps[e][:, n:n + 1], acc[:, e, n * P:(n + 1) * P], ones[:, 0:1],
                                       start=True, stop=True)
                    mm.then_inc(ada_sum, 1)
            for ph in phases:
                sum_squares(norm_no[ph])
                u = start[ph]
                if ph == "mix0":
                    mix0(u)
                elif ph == "mix1":
                    mix1(u)
                elif ph.startswith("peer"):
                    peer(ph, int(ph[-1]), u)
                elif ph.startswith("ffn"):
                    ffn(ph, int(ph[-1]), u)
                else:
                    hyb(ph, int(ph[-1]), u)
                if norm_no[ph] >= 4:
                    sum_squares(norm_no[ph] + 1)

        @block.scalar
        def _(act):
            def norm_in(no, ph):
                i = phases.index(ph)
                for q in range(4):
                    if i:
                        act.wait_ge(x_ready, KD * i)
                    nc.scalar.activation(sq[:, 2 * q:2 * q + 2, :], x[:, 2 * q:2 * q + 2, :], ACT.Square).then_inc(sq_ready, 1)
                act.wait_ge(ss_ready, no + 1)
                nc.scalar.activation(stat[:, 0], ps[0][:, 0:S], ACT.Sqrt, bias=eps, scale=1.0 / D).then_inc(std_ready, 1)

            def shift(ph, vec):
                n = norm_no_h[ph]
                for kt in range(KD):
                    act.wait_ge(mid_ready, KD * n + kt + 1)
                    nc.scalar.activation(hT[:, kt, :], hT[:, kt, :], ACT.Identity,
                                         bias=mods[:, vec, kt:kt + 1]).then_inc(h_ready, 1)

            def norm_out(no, unit_last):
                wait_used(act, unit_last)
                for q in range(4):
                    nc.scalar.activation(sq[:, 2 * q:2 * q + 2, :], ps[4 + q][:].rearrange("p (a b) -> p a b", a=2),
                                         ACT.Square).then_inc(sq_ready, 1)
                act.wait_ge(ss_ready, no + 1)
                nc.scalar.activation(stat[:, 0], ps[0][:, 0:S], ACT.Sqrt, bias=eps, scale=1.0 / D).then_inc(std_ready, 1)

            def head_norm(c, bank, n=S, b=0, sums=ps[3]):
                nc.scalar.activation(hsq[:, 0:n], bank[:, 0:n], ACT.Square).then_inc(hn_sq, 1)
                act.wait_ge(hn_ss, c + 1)
                nc.scalar.activation(hstd[:, b, 0:n], sums[:, 0:n], ACT.Sqrt, bias=eps, scale=1.0 / HD).then_inc(hn_std, 1)

            def exps(g, k, inst):
                act.wait_ge(neg_ready, g + k + 3)
                b = k % 2
                n = NCMP if inst["kind"] == "cmp" else None
                for tt in range(TT):
                    cols = slice(tt * NCMP, (tt + 1) * NCMP) if n else (slice(0, P) if tt == 0 else slice(P, TW))
                    a = nc.scalar.activation(prob[:, b, cols], neg[:, b, cols], ACT.Exp, bias=negm[:, b, tt:tt + 1],
                                             scale=-1.0, accum_out=rows[:, b, tt:tt + 1])
                    if inst.get("sink"):
                        a = nc.scalar.activation(sink_e[:, b, tt:tt + 1], nsk[:, inst["half"]:inst["half"] + 1],
                                                 ACT.Exp, bias=negm[:, b, tt:tt + 1], scale=-1.0)
                a.then_inc(exp_ready, 1)

            def attention(g, insts):
                exps(g, 0, insts[0])
                exps(g, 1, insts[1])
                for k, inst in enumerate(insts):
                    act.wait_ge(t_ready, g + k + 1)
                    if inst["kind"] == "cmp":
                        c = nc.scalar.copy(pt[0:NCMP, k % 2, 0:S], ps[6 + k % 2][0:NCMP, 0:S])
                    else:
                        c = nc.scalar.copy(pt[:, k % 2, :], ps[6 + k % 2][:, 0:TW])
                    c.then_inc(pt_ready, 1)
                    if k + 2 < len(insts):
                        exps(g, k + 2, insts[k + 2])

            full = [dict(half=f, kind="full") for f in range(2)]

            def mix0(u):
                act.wait_ge(logf_ready, 1)
                nc.scalar.activation(ftmp[0:8, 2, :], ftmp[0:8, 1, :], ACT.Exp)
                act.drain()
                nc.scalar.activation(ftmp[0:8, 3, :], ftmp[0:8, 2, :], ACT.Ln, bias=1.0).then_inc(logf_act, 1)
                u += 1
                with act.Fori(0, 2) as i:
                    for e in range(2):
                        r = i * 2 + e
                        wait_used(act, u + 6 * e, i, 12)
                        nc.scalar.copy(ccs, ps[0][:, 0:S]).then_inc(conv_c, 1)
                        wait_used(act, u + 6 * e + 3, i, 12)
                        head_norm(r * 2, ps[0])
                        wait_used(act, u + 6 * e + 4, i, 12)
                        head_norm(r * 2 + 1, ps[1], b=1)
                        wait_used(act, u + 6 * e + 5, i, 12)
                        nc.scalar.copy(v_sb[:, 0:2, :], ps[2][:, 0:S].rearrange("p (a b) -> p a b", a=2)).then_inc(v_ready, 1)
                        attention(r * 2, full)

            def mix1(u):
                hn = hn0["mix1"]
                for n in range(4):
                    wait_used(act, u + n)
                    nc.scalar.copy(kcv[:, n, :], ps[n % 2][:, 0:S]).then_inc(kv_raw, 1)
                for n in range(4):
                    wait_used(act, u + 4 + n)
                    head_norm(hn + n, ps[n % 2], b=n % 2)
                for n in range(4):
                    wait_used(act, u + 8 + n)
                    nc.scalar.copy(v_sb[:, 2 * n:2 * n + 2, :],
                                   ps[n % 2][:, 0:S].rearrange("p (a b) -> p a b", a=2)).then_inc(kv_out, 1)
                u += 12
                for a in range(2):
                    wait_used(act, u + 4 * a + 3)
                    nc.scalar.activation(chid[:, a, 0:2 * NCMP], ps[a][:, 0:2 * NCMP], ACT.Gelu_apprx_tanh).then_inc(cmp_h, 1)
                u += 8
                act.wait_ge(cmp_mm, 1)
                head_norm(hn + 4, ps[0], 2 * NCMP)
                act.wait_ge(cmp_mm, 2)
                nc.scalar.copy(vc_sb[0:NCMP, :, :], ps[1][0:NCMP, 0:2 * P].rearrange("p (a b) -> p a b", a=2)).then_inc(cmp_vc, 1)
                act.wait_ge(gate_z, 1)
                nc.scalar.activation(gates, gsum, ACT.Sigmoid).then_inc(gate_s, 1)
                u += 1
                insts = [dict(half=f, kind="cmp" if kind == 0 else "full") for kind in range(3) for f in range(2)]
                with act.Fori(0, 2) as i:
                    for e in range(4):
                        r = i * 4 + e
                        wait_used(act, u + e, i, 4)
                        head_norm(r + (hn + 5), ps[0], sums=ps[1])
                        attention(r * 6 + att0["mix1"], insts)

            def hyb(ph, l, u):
                wait_used(act, u + 1)
                nc.scalar.copy(v_sb[:, 2:4, :], ps[1][:, 0:S].rearrange("p (a b) -> p a b", a=2)).then_inc(v_ready, 1)
                u += 2
                with act.Fori(0, 4) as i:
                    attention(i * 4 + att0[ph], [dict(half=f, kind="full", sink=True) for f in range(2)])
                    wait_used(act, u + 3, i, 4)
                    nc.scalar.copy(v_sb[:, 0:2, :], ps[2][:, 0:S].rearrange("p (a b) -> p a b", a=2)).then_inc(v_ready, 1)
                    attention(i * 4 + (att0[ph] + 2), full)
                act.wait_ge(o_read, pair0[ph] + 8)
                for grp in range(2):
                    nc.scalar.activation(sq[:, 4 * grp:4 * grp + 4, :], oT[:, 4 * grp:4 * grp + 4, :], ACT.Square).then_inc(on_ready, 1)
                act.wait_ge(on_ready, 6 * l + 3)
                for grp in range(2):
                    a = nc.scalar.activation(conv_t[:, grp, :], ps[grp][:, 0:S], ACT.Sqrt, bias=eps, scale=1.0 / 512)
                a.then_inc(on_ready, 1)

            def ffn(no, u):
                with act.Fori(0, NF // 2) as i:
                    for e in range(2):
                        wait_used(act, u + 2 * e, i, 4)
                        nc.scalar.activation(sl[:, e, :], ps[2 * e][:, 0:S], ACT.Silu).then_inc(silu_ready, 1)

            def peer(l, u):
                for hd in range(PH):
                    wait_used(act, u + hd)
                    nc.scalar.copy(pq[:, hd % 2, :], ps[hd % 2][:, 0:S]).then_inc(pq_ready, 1)
                    act.wait_ge(ps_ready, PH * l + hd + 1)
                    for half in range(2):
                        c = nc.scalar.copy(score[:, :, 2 * hd + half, :],
                                           ps[2 + 2 * (hd % 2) + half][:, 0:S].rearrange("p (t n) -> p t n", t=TT))
                    c.then_inc(ps_read, 1)
                u += PH
                with act.Fori(0, NE // 4) as i:
                    for e in range(4):
                        wait_used(act, u + e, i, 4)
                        nc.scalar.activation(arena[:, i * 4 + e, :], ps[e % 2][:, 0:S], ACT.Gelu_apprx_tanh).then_inc(gelu_ready, 1)
                for tt in range(TT):
                    act.wait_ge(rexp_in, TT * l + tt + 1)
                    nc.scalar.activation(r_out[:, tt, 2, :], r_cv[:].rearrange("p g k -> p (g k)"), ACT.Exp).then_inc(rexp_out, 1)

            act.wait_ge(params_in, 48)
            act.wait_ge(setup_done, 1)
            nc.scalar.activation(cact, pc("c"), ACT.Silu).then_inc(c_ready, 1)
            with act.Fori(0, NVEC // 2) as i:
                for e in range(2):
                    act.wait_ge(ada_sum, i * 2 + (e + 1))
                    nc.scalar.copy(mraw[:, i * 2 + e, :], ps[e][:, 0:KD]).then_inc(ada_out, 1)
            for ph in phases:
                norm_in(norm_no[ph], ph)
                shift(ph, vec_of(ph))
                u = start[ph]
                if ph == "mix0":
                    mix0(u)
                elif ph == "mix1":
                    mix1(u)
                elif ph.startswith("peer"):
                    peer(int(ph[-1]), u)
                elif ph.startswith("ffn"):
                    ffn(int(ph[-1]), u)
                else:
                    hyb(ph, int(ph[-1]), u)
                if norm_no[ph] >= 4:
                    norm_out(norm_no[ph] + 1, u + phase_units(ph) - 1)

        @block.vector
        def _(dve):
            V = nc.vector

            def norm_in(ph, vec, gain):
                V.scalar_tensor_tensor(out=acol[:], in0=mods[:, vec + 1, :], scalar=1.0, in1=gain, op0=ALU.add, op1=ALU.mult)
                dve.wait_ge(std_ready, norm_no[ph] + 1)
                V.reciprocal(stat[:, 1], stat[:, 0])
                dve.drain()
                for kt in range(KD):
                    V.scalar_tensor_tensor(out=hT[:, kt, :], in0=x[:, kt, :], scalar=acol[:, kt:kt + 1], in1=stat[:, 1],
                                           op0=ALU.mult, op1=ALU.mult).then_inc(mid_ready, 1)

            def y_of(n):
                return ps[4 + n // 2][:, (n % 2) * S:(n % 2 + 1) * S]

            def add_plain(ph, vec):
                wait_used(dve, start[ph] + phase_units(ph) - 1)
                for n in range(KD):
                    V.scalar_tensor_tensor(out=x[:, n, :], in0=y_of(n), scalar=mods[:, vec + 2, n:n + 1], in1=x[:, n, :],
                                           op0=ALU.mult, op1=ALU.add).then_inc(x_ready, 1)
                dve.drain()

            def add_normed(ph, vec, post, factor):
                V.scalar_tensor_tensor(out=acol[:], in0=mods[:, vec + 2, :], scalar=factor, in1=post, op0=ALU.mult, op1=ALU.mult)
                dve.wait_ge(std_ready, norm_no[ph] + 2)
                V.reciprocal(stat[:, 1], stat[:, 0])
                dve.drain()
                for n in range(KD):
                    V.scalar_tensor_tensor(out=gtmp[:, n % 2, :], in0=y_of(n), scalar=acol[:, n:n + 1], in1=stat[:, 1],
                                           op0=ALU.mult, op1=ALU.mult)
                    dve.drain()
                    V.tensor_tensor(out=x[:, n, :], in0=x[:, n, :], in1=gtmp[:, n % 2, :], op=ALU.add).then_inc(x_ready, 1)
                dve.drain()

            def head_norm(c, out, bank, gcol, n=S, b=0):
                dve.drain()
                dve.wait_ge(hn_std, c + 1)
                V.reciprocal(hrec[:, 0:n], hstd[:, b, 0:n])
                dve.drain()
                V.scalar_tensor_tensor(out=out, in0=bank[:, 0:n], scalar=gcol, in1=hrec[:, 0:n],
                                       op0=ALU.mult, op1=ALU.mult).then_inc(hn_out, 1)

            def lowest(g, k, inst):
                wait_alone(dve, s_ready, g + k + 1)
                b = k % 2
                bank = ps[4 + b]
                first = inst.get("sink", FMAX)
                for tt in range(TT):
                    if inst["kind"] == "cmp":
                        cols = slice(tt * NCMP, (tt + 1) * NCMP)
                        o = (1 - tt) * P + CMP_LEN - 1
                        bias = nb[:, inst["half"], o:o + 16 * (NCMP - 1) + 1:16]
                    else:
                        cols = slice(0, P) if tt == 0 else slice(P, TW)
                        if inst.get("row"):
                            bias = pc("cmask")[:, cols]
                        else:
                            bias = nb[:, inst["half"], P:2 * P] if tt == 0 else nb[:, inst["half"], 0:S]
                    m = V.tensor_tensor_reduce(out=neg[:, b, cols], in0=bank[:, cols], in1=bias, scale=1.0, scalar=first,
                                               op0=ALU.add, op1=ALU.min, accum_out=negm[:, b, tt:tt + 1])
                m.then_inc(neg_ready, 1)

            def attention(g, pairs, insts, chunk):
                lowest(g, 0, insts[0])
                lowest(g, 1, insts[1])
                for k, inst in enumerate(insts):
                    b = k % 2
                    dve.wait_ge(exp_ready, g + k + 1)
                    if "sink" in inst:
                        V.tensor_tensor(out=rows[:, b, :], in0=rows[:, b, :], in1=sink_e[:, b, :], op=ALU.add)
                        dve.drain()
                    if "gate" in inst:
                        V.reciprocal(rinv[:, b, :], rows[:, b, :])
                        dve.drain()
                        V.tensor_tensor(out=coef[:, b, :], in0=rinv[:, b, :], in1=inst["gate"], op=ALU.mult).then_inc(coef_ready, 1)
                    else:
                        V.reciprocal(coef[:, b, :], rows[:, b, :]).then_inc(coef_ready, 1)
                    if k + 2 < len(insts):
                        lowest(g, k + 2, insts[k + 2])
                dve.wait_ge(o_done, pairs + 1)
                V.tensor_copy(oT[0:HD, chunk, :], ps[2][0:HD, 0:S])
                V.tensor_copy(oT[HD:P, chunk, :], ps[3][HD:P, 0:S]).then_inc(o_read, 1)

            def mix0(u):
                V.memset(u_pad[:, 0:2], 0.0)
                wait_used(dve, u)
                V.tensor_scalar(ftmp[0:8, 0, :], ps[0][0:8, 0:S], pc("bf")[0:8, :], None, ALU.add)
                dve.drain()
                V.scalar_tensor_tensor(out=ftmp[0:8, 1, :], in0=ftmp[0:8, 0, :], scalar=-1.0, in1=ftmp[0:8, 0, :],
                                       op0=ALU.mult, op1=ALU.min).then_inc(logf_ready, 1)
                dve.wait_ge(logf_act, 1)
                V.scalar_tensor_tensor(out=ftmp[0:8, 1, :], in0=ftmp[0:8, 0, :], scalar=0.0, in1=ftmp[0:8, 3, :],
                                       op0=ALU.min, op1=ALU.subtract)
                V.memset(ftmp[0:8, 2, :], 1.0)
                dve.drain()
                V.tensor_tensor_scan(cum[0:8, :], ftmp[0:8, 2, :], ftmp[0:8, 1, :], 0.0, ALU.mult, ALU.add).then_inc(cum_ready, 1)
                gq = small[:, 1:2]
                V.tensor_scalar(gq, pc("fqg"), -SCALE, None, ALU.mult)
                dve.drain()
                u += 1
                w0 = COL["convw"][0]
                with dve.Fori(0, 2) as i:
                    for e in range(2):
                        r = i * 2 + e
                        dve.wait_ge(conv_c, r + 1)
                        wait_used(dve, u + 6 * e + 1, i, 12)
                        V.tensor_tensor(out=u_pad[:, 2:S + 2], in0=ps[1][:, 0:S], in1=ccs, op=ALU.mult).then_inc(conv_u, 1)
                        dve.drain()
                        wc = [prm[:, w0:w0 + 12].rearrange("p (c k) -> p c k", k=3)[:, r, q:q + 1] for q in range(3)]
                        V.tensor_scalar(conv_t[:, 0, :], u_pad[:, 0:S], wc[0], None, ALU.mult)
                        dve.drain()
                        V.scalar_tensor_tensor(out=conv_t[:, 1, :], in0=u_pad[:, 1:S + 1], scalar=wc[1], in1=conv_t[:, 0, :],
                                               op0=ALU.mult, op1=ALU.add)
                        dve.drain()
                        V.scalar_tensor_tensor(out=conv_t[:, 0, :], in0=u_pad[:, 2:S + 2], scalar=wc[2], in1=conv_t[:, 1, :],
                                               op0=ALU.mult, op1=ALU.add)
                        dve.drain()
                        wait_used(dve, u + 6 * e + 2, i, 12)
                        V.tensor_tensor(out=oT[:, r, :], in0=ps[2][:, 0:S], in1=conv_t[:, 0, :], op=ALU.mult).then_inc(conv_out, 1)
                        head_norm(r * 2, qs, ps[0], gq)
                        head_norm(r * 2 + 1, ks[:, 0], ps[1], pc("fkg"), b=1)
                        attention(r * 2, r, [dict(half=f, kind="full", row=True) for f in range(2)], r + 4)
                dve.drain()

            def mix1(u):
                hn = hn0["mix1"]
                gq = small[:, 2:3]
                V.tensor_scalar(gq, pc("nqg"), -SCALE, None, ALU.mult)
                dve.drain()
                for n in range(4):
                    head_norm(hn + n, ks[:, 1 + n], ps[n % 2], pc("nkg", 1 + n // 2, 1), b=n % 2)
                head_norm(hn + 4, kc_sb[:, 0:2 * NCMP], ps[0], pc("nkg", 0, 1), 2 * NCMP)
                u += 20
                wait_used(dve, u)
                V.tensor_tensor(out=gsum, in0=ps[0][:, 0:TT * 48].rearrange("p (a b) -> p a b", a=TT),
                                in1=pc("bgate").unsqueeze(1).to_broadcast([P, TT, 48]), op=ALU.add).then_inc(gate_z, 1)
                dve.wait_ge(gate_s, 1)
                g3 = gates[:].rearrange("p t (h y) -> p t h y", y=3)
                V.tensor_scalar(g3[:, 0, :, 0], g3[:, 0, :, 0], pc("rowmask"), None, ALU.mult).then_inc(gate_ready, 1)
                dve.drain()
                g6 = gates[:].rearrange("p t (a f j y) -> p t a f j y", a=2, f=2, j=4)
                u += 1
                with dve.Fori(0, 2) as i:
                    for e in range(4):
                        r = i * 4 + e
                        half = e % 2
                        j = i * 2 + e // 2
                        head_norm(r + (hn + 5), qs, ps[0], gq)
                        dve.wait_ge(bias_in, r * 32 + 32 * (bias0["mix1"] + 1))
                        attention(r * 6 + att0["mix1"], r + pair0["mix1"],
                                  [dict(half=f, kind="cmp" if kind == 0 else "full", gate=g6[:, :, half, f, j, kind])
                                   for kind in range(3) for f in range(2)], r)
                dve.drain()

            def hyb(ph, l, u):
                bcol = prm[:, COL["mixb"][0] + 13 * l:COL["mixb"][0] + 13 * l + 13]

                def project(out, bank, col, scale):
                    V.tensor_scalar(out, bank[:, 0:S], col, scale, ALU.add, ALU.mult).then_inc(q_ready, 1)

                wait_used(dve, u)
                project(ks[:, 1], ps[0], bcol[:, 4:5], 1.0)
                u += 2
                sk = prm[:, COL["sinks"][0] + 8 * l:COL["sinks"][0] + 8 * l + 8].rearrange("p (j f) -> p j f", f=2)
                b3 = bcol[:, 0:4].rearrange("p (a b) -> p a b", b=1)
                b4 = bcol[:, 5:9].rearrange("p (a b) -> p a b", b=1)
                b5 = bcol[:, 9:13].rearrange("p (a b) -> p a b", b=1)
                with dve.Fori(0, 4) as i:
                    V.tensor_scalar(nsk, sk[:, i, :], -1.0, None, ALU.mult)
                    dve.drain()
                    wait_used(dve, u, i, 4)
                    project(qs, ps[0], b3[:, i, :], -SCALE)
                    dve.wait_ge(bias_in, i * 64 + 32 * (bias0[ph] + 1))
                    attention(i * 4 + att0[ph], i * 2 + pair0[ph],
                              [dict(half=f, kind="full", sink=nsk[:, f:f + 1]) for f in range(2)], i)
                    wait_used(dve, u + 1, i, 4)
                    project(qs, ps[0], b4[:, i, :], -SCALE)
                    wait_used(dve, u + 2, i, 4)
                    project(ks[:, 0], ps[1], b5[:, i, :], 1.0)
                    dve.wait_ge(bias_in, i * 64 + 32 * (bias0[ph] + 2))
                    attention(i * 4 + (att0[ph] + 2), i * 2 + (pair0[ph] + 1),
                              [dict(half=f, kind="full") for f in range(2)], i + 4)
                dve.wait_ge(on_ready, 6 * l + 4)
                g0 = COL["gain"][0] + KD * l
                for grp in range(2):
                    V.reciprocal(sq[:, grp, :], conv_t[:, grp, :])
                    dve.drain()
                    for kt in range(4):
                        n = 4 * grp + kt
                        m = V.scalar_tensor_tensor(out=oT[:, n, :], in0=oT[:, n, :], scalar=prm[:, g0 + n:g0 + n + 1],
                                                   in1=sq[:, grp, :], op0=ALU.mult, op1=ALU.mult)
                    m.then_inc(on_ready, 1)
                dve.drain()

            def ffn(no, u):
                with dve.Fori(0, NF // 2) as i:
                    for e in range(2):
                        dve.wait_ge(silu_ready, i * 2 + (NF * no + e + 1))
                        wait_used(dve, u + 2 * e + 1, i, 4)
                        V.tensor_tensor(out=hid[:, i * 2 + e, :], in0=ps[2 * e + 1][:, 0:S], in1=sl[:, e, :],
                                        op=ALU.mult).then_inc(ffn_h, 1)

            def peer(l, u):
                dve.wait_ge(ps_read, PH * (l + 1))
                for tt in range(TT):
                    sc = score[:, tt]
                    for g in range(16):
                        V.max(r_sv[:, g, 0:8], sc[:, g, :])
                    dve.drain()
                    for g in range(16):
                        V.max_index(r_si[:, g, 0:8], r_sv[:, g, 0:8], sc[:, g, :])
                    dve.drain()
                    for g in range(16):
                        V.match_replace(sc[:, g, :], r_sv[:, g, 0:8], sc[:, g, :], -FMAX)
                    dve.drain()
                    for g in range(16):
                        V.max(r_sv[:, g, 8:16], sc[:, g, :])
                    dve.drain()
                    for g in range(16):
                        V.max_index(r_si[:, g, 8:16], r_sv[:, g, 8:16], sc[:, g, :])
                    dve.drain()
                    V.tensor_copy(r_sif, r_si[:])
                    cand = sc.rearrange("p g n -> p (g n)").rearrange("p (h a b) -> p h a b", h=PH, a=TOPK)
                    sv4 = r_sv.rearrange("p (h w) k -> p h w k", w=2)
                    for h in range(PH):
                        V.tensor_tensor(out=cand[:, h], in0=sv4[:, h, 0, :].unsqueeze(2).to_broadcast([P, TOPK, TOPK]),
                                        in1=sv4[:, h, 1, :].unsqueeze(1).to_broadcast([P, TOPK, TOPK]), op=ALU.add)
                    dve.drain()
                    cf = sc.rearrange("p g n -> p (g n)").rearrange("p (h c) -> p h c", h=PH)
                    for h in range(PH):
                        V.max(r_cv[:, h, 0:8], cf[:, h, :])
                    dve.drain()
                    for h in range(PH):
                        V.max_index(r_ci[:, h, 0:8], r_cv[:, h, 0:8], cf[:, h, :])
                    dve.drain()
                    for h in range(PH):
                        V.match_replace(cf[:, h, :], r_cv[:, h, 0:8], cf[:, h, :], -FMAX)
                    dve.drain()
                    for h in range(PH):
                        V.max(r_cv[:, h, 8:16], cf[:, h, :])
                    dve.drain()
                    for h in range(PH):
                        V.max_index(r_ci[:, h, 8:16], r_cv[:, h, 8:16], cf[:, h, :])
                    dve.drain()
                    cif = r_ci[:].rearrange("p h k -> p (h k)")
                    V.tensor_scalar(r_ab[:, 0, :], cif, 4, None, ALU.logical_shift_right)
                    V.tensor_scalar(r_ab[:, 1, :], cif, 15, None, ALU.bitwise_and)
                    V.tensor_copy(r_sum, r_cv[:, :, 0])
                    dve.drain()
                    V.tensor_copy(r_abf, r_ab[:])
                    V.tensor_tensor(out=r_cv, in0=r_cv, in1=r_sum.unsqueeze(2).to_broadcast([P, PH, TOPK]),
                                    op=ALU.subtract).then_inc(rexp_in, 1)
                    dve.drain()
                    si4 = r_sif.rearrange("p (h w) k -> p h w k", w=2)
                    for w in range(2):
                        V.tensor_tensor(out=eq[:], in0=r_abf[:, w, :].unsqueeze(2).to_broadcast([P, NE, TOPK]),
                                        in1=iota[:, 0:TOPK].unsqueeze(1).to_broadcast([P, NE, TOPK]), op=ALU.is_equal)
                        dve.drain()
                        for h in range(PH):
                            V.tensor_tensor(out=eq[:, h * TOPK:(h + 1) * TOPK, :], in0=eq[:, h * TOPK:(h + 1) * TOPK, :],
                                            in1=si4[:, h, w, :].unsqueeze(1).to_broadcast([P, TOPK, TOPK]), op=ALU.mult)
                        dve.drain()
                        V.tensor_reduce(r_out[:, tt, w, :], eq[:], AX.X, ALU.add)
                        dve.drain()
                    dve.wait_ge(rexp_out, TT * l + tt + 1)
                    e3 = r_out[:, tt, 2, :].rearrange("p (h k) -> p h k", h=PH)
                    V.tensor_reduce(r_sum, e3, AX.X, ALU.add)
                    dve.drain()
                    V.reciprocal(r_rec, r_sum)
                    dve.drain()
                    V.tensor_tensor(out=e3, in0=e3, in1=r_rec.unsqueeze(2).to_broadcast([P, PH, TOPK]),
                                    op=ALU.mult).then_inc(route_ready, 1)
                for tt in range(TT):
                    dve.wait_ge(routeT_ready, TT * l + tt + 1)
                    V.tensor_copy(r_outT[:, :, tt * P:(tt + 1) * P],
                                  ps[2 + tt][:, 0:3 * P].rearrange("p (w t) -> p w t", w=3)).then_inc(routeT_read, 1)
                dve.drain()
                dve.wait_ge(gelu_ready, NE * (l + 1) + 2)

                def weigh(i, e):
                    dve.wait_ge(g_ready, i * 2 + (S // 4 * l + e + 1))
                    a = arena[:].rearrange("p j (c b t) -> p j c b t", b=2, t=4)[:, :, i, e, :]
                    V.tensor_tensor(out=a, in0=ps[2 + e][:].rearrange("p (t j) -> p j t", t=4), in1=a,
                                    op=ALU.mult).then_inc(g_read, 1)

                oT4 = r_outT[:].rearrange("p w (c b t) -> p w c b t", b=2, t=4)
                with dve.Fori(0, S // 8) as i:
                    for e in range(2):
                        for t in range(4):
                            m = V.tensor_scalar(hot[:, e, 0, t, :], iota, oT4[:, 0, i, e, t:t + 1], oT4[:, 2, i, e, t:t + 1],
                                                ALU.is_equal, ALU.mult)
                        m.then_inc(hotA_ready, 1)
                    for e in range(2):
                        weigh(i, e)

            V.memset(eps, EPS)
            V.memset(small[:, 4:5], 0.0).then_inc(neg_ready, 2)
            V.memset(small[:, 5:6], 0.0).then_inc(ffn_h, 2)
            V.memset(small[:, 6:7], 0.0).then_inc(gelu_ready, 2)
            V.memset(small[:, 7:8], 0.0).then_inc(g_read, 2)
            V.memset(small[:, 3:4], 0.0).then_inc(ada_out, 2)
            V.memset(small[:, 24:25], 0.0).then_inc(setup_done, 1)
            dve.wait_ge(params_in, 48)
            h0 = TAB["hot"][0]
            V.tensor_scalar(tabs[0:32, h0:h0 + 512], tabs[0:32, h0:h0 + 512], -1.0, None, ALU.mult).then_inc(tab_ready, 1)
            dve.wait_ge(tab_read, 1)
            for a, name in enumerate(("mask", "mask2")):
                m0 = TAB[name][0]
                m = V.tensor_tensor(out=erow[0:16, a, :], in0=ps[2 + a][0:16, :], in1=tabs[0:16, m0:m0 + 512], op=ALU.add)
            m.then_inc(tab_ready, 1)
            dve.wait_ge(c_ready, 1)
            for lo, n, cc in ((0, 12, 0), (12, 18, KD)):
                with dve.Fori(lo // 2, (lo + n) // 2) as i:
                    for e in range(2):
                        dve.wait_ge(ada_loaded[e], i * 16 + 16)
                        dve.wait_ge(ada_out, i * 2 + (e + 1))
                        m = V.tensor_scalar(acc[:, e, :], adaw[:, e, 0, :], cact[:, cc:cc + 1], None, ALU.mult)
                        for k in range(1, KD):
                            dve.drain()
                            m = V.scalar_tensor_tensor(out=acc[:, e, :], in0=adaw[:, e, k, :], scalar=cact[:, cc + k:cc + k + 1],
                                                       in1=acc[:, e, :], op0=ALU.mult, op1=ALU.add)
                        m.then_inc(ada_acc, 1)
            dve.wait_ge(ada_out, NVEC + 2)
            V.tensor_tensor(out=mods[:].rearrange("p a b -> p (a b)"), in0=mraw[:].rearrange("p a b -> p (a b)"),
                            in1=pc("adab"), op=ALU.add)
            dve.drain()
            for ph in phases:
                vec = vec_of(ph)
                if norm_no[ph] < 4:
                    gain = pc("norm", KD * norm_no[ph], KD)
                else:
                    gain = pc("pre", KD * ((norm_no[ph] - 4) // 2), KD)
                norm_in(ph, vec, gain)
                u = start[ph]
                if ph == "mix0":
                    mix0(u)
                elif ph == "mix1":
                    mix1(u)
                elif ph.startswith("peer"):
                    peer(int(ph[-1]), u)
                elif ph.startswith("ffn"):
                    ffn(int(ph[-1]), u)
                else:
                    hyb(ph, int(ph[-1]), u)
                if norm_no[ph] < 4:
                    add_plain(ph, vec)
                else:
                    add_normed(ph, vec, pc("post", KD * ((norm_no[ph] - 4) // 2), KD), 1.0 if ph.startswith("hyb") else 0.5)

        @block.gpsimd
        def _(pool):
            G = nc.gpsimd

            def attention(g, insts):
                for k, inst in enumerate(insts):
                    b = k % 2
                    wait_alone(pool, coef_ready, g + k + 1)
                    for tt in range(TT):
                        if inst == "cmp":
                            cols = slice(tt * NCMP, (tt + 1) * NCMP)
                        else:
                            cols = slice(0, P) if tt == 0 else slice(P, TW)
                        m = G.tensor_scalar(prob[:, b, cols], prob[:, b, cols], coef[:, b, tt:tt + 1], None, ALU.mult)
                    m.then_inc(pn_ready, 1)

            def bias(slot, head):
                src = bias_rows[head, 127:127 + P * 511].rearrange("(p w) -> p w", w=511)[:, 0:TW]
                pool.dma_start(nb[:, slot, :], src).then_inc(bias_in, 16)

            def mix0():
                pool.wait_ge(cum_ready, 1)
                pool.dma_start(cumrow[0:1, :, :], cum[0:8, :]).then_inc(cum_row, 16)
                with pool.Fori(0, 4) as i:
                    attention(i * 2, ["full"] * 2)

            def mix1():
                for a in range(2):
                    pool.wait_ge(kv_raw, 2 * a + 2)
                    for c in range(2):
                        src = kcv[:, 2 * a + c, :]
                        toks = bass.AP(src.tensor, src.offset, [list(src.ap[0]), [1, CMP_LEN], [16, NCMP]])
                        G.tensor_tensor(out=blk[:, a, :, c, :], in0=toks,
                                        in1=pc("pos", a * CMP_LEN, CMP_LEN).unsqueeze(2).to_broadcast([P, CMP_LEN, NCMP]),
                                        op=ALU.add).then_inc(blk_ready, 1)
                with pool.Fori(0, 2) as i:
                    for e in range(4):
                        r = i * 4 + e
                        j = i * 2 + e // 2
                        for f in range(2):
                            bias(f, j + (8 * (e % 2) + 4 * f))
                        attention(r * 6 + att0["mix1"], ["cmp"] * 2 + ["full"] * 4)

            def hyb(ph, l):
                pool.wait_ge(x_ready, KD * phases.index(ph))
                if l == 0:
                    pool.dma_start(vr[0:1, :, :, :], vrow).then_inc(cum_row, 16)
                with pool.Fori(0, 4) as i:
                    for f in range(2):
                        bias(f, i + (16 + 4 * f))
                    attention(i * 4 + att0[ph], ["full"] * 2)
                    for f in range(2):
                        bias(f, i * 2 + (24 + f))
                    attention(i * 4 + (att0[ph] + 2), ["full"] * 2)

            def peer(l):
                pool.wait_ge(routeT_read, TT * (l + 1))
                oT3 = r_outT[:, 1, :].rearrange("p (c b t) -> p c b t", b=2, t=4)
                with pool.Fori(0, S // 8) as i:
                    for e in range(2):
                        pool.wait_ge(g_read, i * 2 + (S // 4 * l + e + 1))
                        G.tensor_tensor(out=away[:, e], in0=iota.unsqueeze(1).to_broadcast([P, 4, NE]),
                                        in1=oT3[:, i, e, :].unsqueeze(2).to_broadcast([P, 4, NE]), op=ALU.subtract)
                        pool.drain()
                        G.tensor_scalar(hot[:, e, 1], away[:, e], 0.0, None, ALU.is_equal).then_inc(hotB_ready, 1)

            pool.wait_ge(tab_ready, 2)
            for a in range(2):
                pool.dma_start(bias_rows[16 * a:16 * a + 16].rearrange("h (p n) -> h p n", p=P),
                               erow[0:16, a, :].unsqueeze(1).to_broadcast([16, P, 512])).then_inc(bias_written, 16)
            pool.wait_ge(bias_written, 32)
            for ph in phases:
                if ph == "mix0":
                    mix0()
                elif ph == "mix1":
                    mix1()
                elif ph.startswith("peer"):
                    peer(int(ph[-1]))
                elif ph.startswith("hyb"):
                    hyb(ph, int(ph[-1]))


def vec_of(ph):
    return 3 * PHASES.index(ph)


norm_no_h = {ph: i for i, ph in enumerate(PHASES)}


def column_units(w):
    n = w.shape[1] // P
    return np.ascontiguousarray(w.reshape(KD, P, n, P).transpose(2, 1, 0, 3)).reshape(n, P, UNIT)


def padded(w):
    out = np.zeros((w.shape[0], P), w.dtype)
    out[:, :w.shape[1]] = w
    return out


def columns(v):
    return np.ascontiguousarray(v.reshape(-1, P).T)


def twice(v):
    return np.concatenate([v, v]).reshape(P, 1)


def block_diagonal(w):
    out = np.zeros(w.shape[:-2] + (P, P), w.dtype)
    out[..., :HD, :HD] = w
    out[..., HD:, HD:] = w
    return out


def head_columns(w, heads):
    return np.concatenate([w[:, h * HD:(h + 1) * HD] for h in heads], axis=1)


def head_rows(w, heads):
    return np.concatenate([w[h * HD:(h + 1) * HD] for h in heads], axis=0)


NSA_ORDER = [(2 * half + f) * 4 + j for j in range(4) for half in range(2) for f in range(2)]
SWA_ORDER = [4 * f + j for j in range(4) for f in range(2)]


def weight_stream(a):
    out = []
    w = a["even_w_in"][0]
    cb, cc, ch, q, k, v, f = (column_units(x) if x.shape[1] > 8 else column_units(padded(x))
                              for x in np.split(w, [512, 1024, 1536, 2048, 2560, 3072], axis=1))
    out += [f, np.stack([cc, ch, cb, q, k, v], axis=1).reshape(24, P, UNIT), column_units(a["even_w_out"][0])]

    def experts(l):
        u = a["peer_u"][l].reshape(NE, NE, KD, P).transpose(1, 3, 2, 0).reshape(NE, P, UNIT)
        v = a["peer_v"][l].reshape(NE, NE, D).transpose(1, 0, 2)
        return [column_units(a["peer_w_q"][l]), u, v]

    out += experts(0)
    q, kc, vc, ks, vs, kw, vw, gl = np.split(a["odd_w_in"][0], [1024 + 256 * i for i in range(7)], axis=1)
    w1 = block_diagonal(a["odd_cmp_w1"][0].reshape(2, CMP_LEN, HD, HD))
    w1 = w1.reshape(2, 4, 8, P, P).transpose(0, 1, 3, 2, 4).reshape(8, P, UNIT)
    out += [column_units(x) for x in (kc, vc, ks, kw, vs, vw)]
    out += [w1, column_units(padded(gl)), column_units(head_columns(q, NSA_ORDER)),
            column_units(head_rows(a["odd_w_out"][0], NSA_ORDER))]
    out += experts(1)

    def ffn(l, n):
        g, u = column_units(a["ffn_w_gate_2"][l, n]), column_units(a["ffn_w_up_2"][l, n])
        return [np.stack([g, u], axis=1).reshape(2 * NF, P, UNIT), a["ffn_w_down_2"][l, n].reshape(NF, P, D)]

    for l in range(2):
        out += ffn(l, 0)
        qa, ka, va, qb, kb, vb = np.split(a["mix_w_in_2"][l], [512, 640, 768, 1280, 1792], axis=1)
        out += [column_units(ka), column_units(va)]
        out += [np.stack([column_units(x) for x in (head_columns(qa, SWA_ORDER), qb, kb, vb)], axis=1).reshape(16, P, UNIT)]
        wo = a["mix_w_out_2"][l]
        out += [column_units(np.concatenate([head_rows(wo[:512], SWA_ORDER), wo[512:]], axis=0))]
        out += ffn(l, 1)
    return np.concatenate(out, axis=0)


def buckets(dist):
    n = np.maximum(dist, 0)
    nf = np.maximum(n, 1).astype(np.float32)
    large = 16 + (np.log(nf / np.float32(16)) / np.float32(math.log(128 / 16)) * np.float32(16)).astype(np.int32)
    return np.where(n < 16, n, np.minimum(large, 31))


def bias_constants():
    dist = 255 - np.arange(512)
    hot = ((buckets(dist)[None] == np.arange(32)[:, None]) & (dist >= 0)[None]).astype(np.float32)
    causal = np.where(dist >= 0, 0.0, BIG).astype(np.float32)
    window = np.where((dist >= 0) & (dist < 128), 0.0, BIG).astype(np.float32)
    mask = np.broadcast_to(causal, (16, 512))
    mask2 = np.concatenate([np.broadcast_to(window, (8, 512)), np.broadcast_to(causal, (8, 512))])
    return hot, mask, mask2


def packed_params(a):
    f = np.float32
    t = np.arange(P)
    cmask = np.concatenate([np.where(t[None] > t[:, None], BIG, 0.0),
                            np.where(np.arange(S)[None] > P + t[:, None], BIG, 0.0)], axis=1).astype(f)
    adab = np.concatenate([columns(a["ada_b"].reshape(-1)), columns(a["ada_b_2"].reshape(-1))], axis=1)
    mixb = []
    gain = []
    for l in range(2):
        b = a["mix_b_in_2"][l]
        mixb += [columns(head_rows(b[:512].reshape(-1, 1), SWA_ORDER).reshape(-1)), columns(b[512:640]),
                 columns(b[768:1280]), columns(b[1280:1792])]
        g = a["group_gain_2"][l]
        gain += [columns(head_rows(g[:512].reshape(-1, 1), SWA_ORDER).reshape(-1)), columns(g[512:])]
    sinks = np.concatenate([a["attn_sinks_2"][l][SWA_ORDER] for l in range(2)])
    bf = np.zeros((P, 1), f)
    bf[:8, 0] = a["even_b_f"][0]
    parts = {
        "ident": np.eye(P, dtype=f), "ones": np.ones((P, P), f), "bd": block_diagonal(np.ones((HD, HD), f)),
        "iota": np.broadcast_to(t.astype(f), (P, P)), "cmask": cmask,
        "rowmask": (t >= CMP_LEN - 1).astype(f).reshape(P, 1), "adab": adab,
        "c": np.concatenate([columns(a["c"][0]), columns(a["c_2"][0])], axis=1),
        "norm": columns(a["norm_g"].reshape(-1)), "pre": columns(a["norm_pre_2"].reshape(-1)),
        "post": columns(a["norm_post_2"].reshape(-1)),
        "convw": a["even_conv_w"][0].reshape(3, 4, P).transpose(2, 1, 0).reshape(P, 12), "bf": bf,
        "fqg": twice(a["even_q_g"][0]), "fkg": twice(a["even_k_g"][0]), "nqg": twice(a["odd_q_g"][0]),
        "nkg": np.concatenate([twice(a["odd_k_g"][0, i]) for i in range(3)], axis=1),
        "pos": np.concatenate([np.concatenate([a["odd_cmp_pos"][0, i].T] * 2) for i in range(2)], axis=1),
        "w2": np.concatenate([block_diagonal(a["odd_cmp_w2"][0, i]) for i in range(2)], axis=1),
        "keys": np.concatenate([a["peer_keys"][l].transpose(0, 2, 1).reshape(P, NE) for l in range(2)], axis=1),
        "bgate": np.broadcast_to(a["odd_b_gate"][0], (P, 48)), "mixb": np.concatenate(mixb, axis=1),
        "gain": np.concatenate(gain, axis=1), "sinks": np.broadcast_to(sinks, (P, 16)),
    }
    return np.ascontiguousarray(np.concatenate([parts[n] for n, _ in _COLS], axis=1))


def packed_tables(a):
    hot, mask, mask2 = bias_constants()
    out = np.zeros((32, NTAB), np.float32)
    for name, v in (("rel", a["rel_table"]), ("rel2", a["rel_bias_2"]), ("hot", hot), ("mask", mask), ("mask2", mask2)):
        c, w = TAB[name]
        out[:v.shape[0], c:c + w] = v
    return out


def packed_ada(a):
    def cut(w):
        l, _, n = w.shape
        return w.reshape(l, KD, P, n // UNIT, UNIT).transpose(0, 3, 1, 2, 4).reshape(-1, KD, P, UNIT)
    return np.concatenate([cut(a["ada_w"]), cut(a["ada_w_2"])], axis=0)


def layout(a):
    b = a["mix_b_in_2"]
    vrow = np.stack([np.concatenate([b[l, 640:768], b[l, 1792:2304]]) for l in range(2)]).reshape(1, 2, 5, P)
    return {
        "xT": np.ascontiguousarray(a["x"][0].T.reshape(KD, P, S).transpose(1, 0, 2)),
        "par": packed_params(a), "tab": packed_tables(a), "vrow": np.ascontiguousarray(vrow),
        "ada": packed_ada(a), "stream": weight_stream(a),
    }


def build(nc, arrays, upto=None):
    args = [nc.dram_tensor(n, v.shape, F32, kind="ExternalInput").ap() for n, v in arrays.items()]
    out = nc.dram_tensor("outT", (P, KD, S), F32, kind="ExternalOutput").ap()
    program(nc, *args, out, upto=upto)


def kernel(**inputs):
    import concourse.bacc as bacc
    from concourse.bass_utils import run_bass_kernel_spmd

    arrays = layout({k: np.asarray(v) for k, v in inputs.items()})
    nc = bacc.Bacc("TRN2", target_bir_lowering=False, num_devices=1)
    build(nc, arrays)
    got = run_bass_kernel_spmd(nc, [arrays], core_ids=[0]).results[0]["outT"]
    return np.ascontiguousarray(got.transpose(1, 0, 2).reshape(D, S).T).reshape(1, S, D)
```

```python
import math
from contextlib import ExitStack

import numpy as np

import concourse.bass as bass
from concourse import mybir

F32 = mybir.dt.float32
U32 = mybir.dt.uint32
ALU = mybir.AluOpType
ACT = mybir.ActivationFunctionType
AX = mybir.AxisListType

P = 128
S = 256
TT = S // P
D = 1024
KD = D // P
HD = 64
SCALE = HD ** -0.5
EPS = 1e-6
BIG = 1e30
FMAX = 3.0e38
UNIT = 1024
SLOTS = 4
FF = 2816
NF = FF // P
NE = 128
PH = 8
TOPK = 16
NCMP = 15
CMP_LEN = 32
GB = 4
NVEC = 30
TW = 384

_COLS = [("ident", P), ("ones", P), ("bd", P), ("iota", P), ("cmask", TW), ("rowmask", 1),
         ("adab", NVEC * KD), ("c", 2 * KD), ("norm", 4 * KD), ("pre", 6 * KD), ("post", 6 * KD),
         ("convw", 12), ("bf", 1), ("fqg", 1), ("fkg", 1), ("nqg", 1), ("nkg", 3),
         ("pos", 2 * CMP_LEN), ("w2", 2 * P), ("keys", 2 * NE), ("bgate", 48),
         ("mixb", 2 * 13), ("gain", 2 * KD), ("sinks", 2 * 8)]
COL = {}
_at = 0
for _n, _w in _COLS:
    COL[_n] = (_at, _w)
    _at += _w
NPAR = _at
TAB = {"rel": (0, 16), "rel2": (16, 16), "hot": (32, 512), "mask": (544, 512), "mask2": (1056, 512)}
NTAB = 1568

MIX0_UNITS = 1 + 24 + 8
MIX1_UNITS = 12 + 8 + 1 + 8 + 8
PEER_UNITS = 8 + 2 * NE
FFN_UNITS = 3 * NF
HYB_UNITS = 2 + 16 + 8
PHASES = ["mix0", "peer0", "mix1", "peer1", "ffn0", "hyb0", "ffn1", "ffn2", "hyb1", "ffn3"]
_SIZE = {"mix0": MIX0_UNITS, "mix1": MIX1_UNITS, "peer": PEER_UNITS, "ffn": FFN_UNITS, "hyb": HYB_UNITS}


def phase_units(name):
    return _SIZE[name] if name in _SIZE else _SIZE[name[:-1]]


def program(nc, xT, par, tab, vrow, ada, stream, outT, upto=None):
    phases = PHASES[:upto]
    start = {}
    units = 0
    for ph in phases:
        start[ph] = units
        units += phase_units(ph)
    att0 = {"mix0": 0, "mix1": 8, "hyb0": 8 + 48, "hyb1": 8 + 48 + 16}
    pair0 = {"mix0": 1, "mix1": 5, "hyb0": 13, "hyb1": 21}
    bias0 = {"mix1": 0, "hyb0": 4, "hyb1": 8}
    hn0 = {"mix0": 0, "mix1": 8}
    norm_no = {"mix0": 0, "peer0": 1, "mix1": 2, "peer1": 3}
    k = 4
    for ph in PHASES[4:]:
        norm_no[ph] = k
        k += 2

    with ExitStack() as ctx:
        def sb(name, shape, dt=F32):
            return ctx.enter_context(nc.sbuf_tensor(name, shape, dt))

        def sem(name):
            return ctx.enter_context(nc.semaphore(name))

        bias_rows = nc.dram_tensor("bias_rows", (32, P * 512), F32).ap()

        ps = [ctx.enter_context(nc.psum_tensor(f"ps{i}", [P, 512], F32)) for i in range(8)]
        x = sb("x", [P, KD, S])
        hT = sb("hT", [P, KD, S])
        ring = sb("ring", [P, SLOTS, UNIT])
        mods = sb("mods", [P, NVEC, KD])
        prm = sb("prm", [P, NPAR])
        stat = sb("stat", [P, 2, S])
        acol = sb("acol", [P, KD])
        small = sb("small", [P, 64])
        arena = sb("arena", [P, NE, S])
        score = sb("score", [P, TT, 16, NE])
        eq = sb("eq", [P, NE, TOPK])
        pick = sb("pick", [P, 7, NE])

        flat = arena[:].rearrange("p a b -> p (a b)")
        used = [0]

        def cut(n, shape=None):
            a = used[0]
            used[0] += n
            assert used[0] <= NE * S
            return flat[:, a:a + n]

        def pc(name, i=0, n=None):
            a, w = COL[name]
            return prm[:, a + i:a + i + (w - i if n is None else n)]

        ident, ones, bd, iota = pc("ident"), pc("ones"), pc("bd"), pc("iota")
        eps = small[:, 0:1]

        sq = cut(KD * S).rearrange("p (a b) -> p a b", a=KD)
        oT = cut(KD * S).rearrange("p (a b) -> p a b", a=KD)
        qs = cut(2 * S).rearrange("p (a b) -> p a b", a=2)
        qs_all = cut(8 * S).rearrange("p (a b) -> p a b", a=8)
        ks = cut(6 * S).rearrange("p (a b) -> p a b", b=S)
        v_sb = cut(4 * TT * 2 * P).rearrange("p (a b) -> p a b", b=P)
        neg = cut(2 * TW).rearrange("p (a b) -> p a b", a=2)
        prob = cut(2 * TW).rearrange("p (a b) -> p a b", a=2)
        pt = cut(2 * TW).rearrange("p (a b) -> p a b", a=2)
        nb = cut(4 * TW).rearrange("p (e a b) -> p e a b", e=2, a=2)
        hsq = cut(S)
        hstd = cut(2 * S).rearrange("p (a b) -> p a b", a=2)
        hrec = cut(S)
        ccs = cut(S)
        u_pad = cut(S + 2)
        conv_t = cut(2 * S).rearrange("p (a b) -> p a b", a=2)
        cum = cut(S)
        ftmp = cut(4 * S).rearrange("p (a b) -> p a b", a=4)
        cumrow = cut(8 * S).rearrange("p (a b) -> p a b", a=8)
        gates = cut(TT * 48).rearrange("p (a b) -> p a b", a=TT)
        gsum = cut(TT * 48).rearrange("p (a b) -> p a b", a=TT)
        blk = cut(2 * CMP_LEN * 2 * NCMP).rearrange("p (a l c n) -> p a l c n", a=2, l=CMP_LEN, c=2)
        kcv = cut(4 * S).rearrange("p (a b) -> p a b", a=4)
        chid = cut(2 * 32).rearrange("p (a b) -> p a b", a=2)
        kc_sb = cut(32)
        vc_sb = cut(2 * P).rearrange("p (a b) -> p a b", a=2)
        negm = cut(4).rearrange("p (a b) -> p a b", a=2)
        rows = cut(4).rearrange("p (a b) -> p a b", a=2)
        sink_e = cut(4).rearrange("p (a b) -> p a b", a=2)
        rinv = cut(4).rearrange("p (a b) -> p a b", a=2)
        coef = cut(4).rearrange("p (a b) -> p a b", a=2)
        nsk = cut(2)
        vr = cut(1280).rearrange("p (l a b) -> p l a b", l=2, a=5)
        ffn_at = used[0]
        hid = cut(NF * S).rearrange("p (a b) -> p a b", a=NF)
        sl = cut(2 * S).rearrange("p (a b) -> p a b", a=2)
        gtmp = cut(KD * S).rearrange("p (a b) -> p a b", a=KD)
        used[0] = ffn_at
        tabs = cut(NTAB)
        erow = cut(2 * 512).rearrange("p (a n) -> p a n", a=2)
        acc4 = cut(4 * UNIT).rearrange("p (a n) -> p a n", a=4)
        adaw = score[:].rearrange("p a g n -> p (a g n)").rearrange("p (a n) -> p a n", a=SLOTS)
        acc = eq[:].rearrange("p a b -> p (a b)").rearrange("p (a n) -> p a n", a=2)
        cact = small[:, 40:56]
        r_sv = pick[:, 0:2, :].rearrange("p a b -> p (a b)").rearrange("p (g k) -> p g k", g=16)
        r_si = sb("r_si", [P, 16, TOPK], U32)
        r_sif = pick[:, 2:4, :].rearrange("p a b -> p (a b)").rearrange("p (g k) -> p g k", g=16)
        r_cv = pick[:, 4, :].rearrange("p (g k) -> p g k", g=PH)
        r_ci = sb("r_ci", [P, PH, TOPK], U32)
        r_ab = sb("r_ab", [P, 2, NE], U32)
        r_abf = pick[:, 5:7, :]
        r_out = sb("r_out", [P, TT, 3, NE])
        r_outT = sb("r_outT", [P, 3, S])
        r_sum = small[:, 8:16]
        r_rec = small[:, 16:24]
        hot = score[:].rearrange("p a g n -> p (a g n)").rearrange(
            "p (b w t n) -> p b w t n", b=GB, w=2, t=4)
        pq = eq[:].rearrange("p a b -> p (a b)")[:, 0:2 * S].rearrange("p (a b) -> p a b", a=2)

        passed = sem("passed")
        params_in = sem("params_in")
        loaded = [sem(f"unit_loaded{s}") for s in range(SLOTS)]
        unit_done = sem("unit_done")
        setup_done = sem("setup_done")
        c_ready = sem("c_ready")
        tab_ready = sem("tab_ready")
        tab_read = sem("tab_read")
        bias_written = sem("bias_written")
        ada_loaded = [sem(f"ada_loaded{s}") for s in range(SLOTS)]
        ada_used = sem("ada_used")
        ada_acc = sem("ada_acc")
        ada_sum = sem("ada_sum")
        ada_read = sem("ada_read")
        x_ready = sem("x_ready")
        sq_ready = sem("sq_ready")
        ss_ready = sem("ss_ready")
        std_ready = sem("std_ready")
        mid_ready = sem("mid_ready")
        h_ready = sem("h_ready")
        y_ready = sem("y_ready")
        silu_ready = sem("silu_ready")
        ffn_h = sem("ffn_h")
        hn_sq = sem("hn_sq")
        hn_ss = sem("hn_ss")
        hn_std = sem("hn_std")
        hn_out = sem("hn_out")
        logf_ready = sem("logf_ready")
        logf_act = sem("logf_act")
        cum_ready = sem("cum_ready")
        cum_row = sem("cum_row")
        conv_c = sem("conv_c")
        conv_u = sem("conv_u")
        conv_out = sem("conv_out")
        v_ready = sem("v_ready")
        q_ready = sem("q_ready")
        s_ready = sem("s_ready")
        neg_ready = sem("neg_ready")
        exp_ready = sem("exp_ready")
        q_staged = sem("q_staged")
        pn_ready = sem("pn_ready")
        t_ready = sem("t_ready")
        pt_ready = sem("pt_ready")
        o_done = sem("o_done")
        o_read = sem("o_read")
        bias_in = [sem(f"bias_in{e}") for e in range(2)]
        kv_out = sem("kv_out")
        kv_raw = sem("kv_raw")
        blk_ready = sem("blk_ready")
        cmp_h = sem("cmp_h")
        cmp_mm = sem("cmp_mm")
        cmp_vc = sem("cmp_vc")
        gate_z = sem("gate_z")
        gate_s = sem("gate_s")
        gate_ready = sem("gate_ready")
        on_ready = sem("on_ready")
        pq_ready = sem("pq_ready")
        ps_ready = sem("ps_ready")
        ps_read = sem("ps_read")
        gelu_ready = sem("gelu_ready")
        rexp_in = sem("rexp_in")
        rexp_out = sem("rexp_out")
        route_ready = sem("route_ready")
        routeT_ready = sem("routeT_ready")
        routeT_read = sem("routeT_read")
        hot_ready = sem("hot_ready")
        hot2_ready = sem("hot2_ready")
        g_ready = sem("g_ready")
        g_read = sem("g_read")
        out_done = sem("out_done")

        def slot_of(unit):
            return ring[:, unit % SLOTS, :].rearrange("p (k n) -> p k n", k=KD)

        def wait_unit(pe, unit, it=0, per=0):
            pe.wait_ge(loaded[unit % SLOTS], it * (per // SLOTS * 16) + 16 * (unit // SLOTS + 1))

        def wait_used(eng, unit, it=0, per=0):
            eng.wait_ge(unit_done, it * per + unit + 1)

        def wait_alone(eng, semaphore, value):
            eng.wait_ge(semaphore, value)
            eng.sem_inc(passed, 1)

        block = ctx.enter_context(nc.Block())

        @block.sync
        def _(sp):
            sp.dma_start(prm[:], par).then_inc(params_in, 16)
            sp.dma_start(tabs[0:32, :], tab).then_inc(params_in, 16)
            sp.dma_start(x[:], xT).then_inc(params_in, 16)
            for u in range(SLOTS):
                sp.dma_start(ring[:, u], stream[u]).then_inc(loaded[u], 16)
            rounds = units // SLOTS
            with sp.Fori(1, rounds) as i:
                for s in range(SLOTS):
                    sp.wait_ge(unit_done, i * SLOTS + (s - SLOTS + 1))
                    sp.dma_start(ring[:, s], stream[i * SLOTS + s]).then_inc(loaded[s], 16)
            for u in range(rounds * SLOTS, units):
                sp.wait_ge(unit_done, u - SLOTS + 1)
                sp.dma_start(ring[:, u % SLOTS], stream[u]).then_inc(loaded[u % SLOTS], 16)
            sp.wait_ge(x_ready, KD * len(phases))
            sp.dma_start(outT, x[:]).then_inc(out_done, 16)
            sp.wait_ge(out_done, 16)

        @block.tensor
        def _(pe):
            def products(out, unit, rhs, it=0, per=0, m=P, h_from=None):
                w = slot_of(unit)
                wait_unit(pe, unit, it, per)
                for kt in range(KD):
                    if h_from is not None:
                        pe.wait_ge(h_ready, h_from + kt + 1)
                    mm = pe.matmul(out, w[:, kt, 0:m], rhs(kt), start=(kt == 0), stop=(kt == KD - 1))
                mm.then_inc(unit_done, 1)

            def products_t(bank, unit, n=P, it=0, per=0, brow=None):
                w = slot_of(unit)
                wait_unit(pe, unit, it, per)
                for tt in range(TT):
                    out = bank[:, tt * n:(tt + 1) * n]
                    for kt in range(KD):
                        mm = pe.matmul(out, hT[:, kt, tt * P:(tt + 1) * P], w[:, kt, 0:n],
                                       start=(kt == 0), stop=(kt == KD - 1 and brow is None))
                    if brow is not None:
                        mm = pe.matmul(out, ones[0:1, :], brow, start=False, stop=True)
                mm.then_inc(unit_done, 1)

            def sum_squares(no):
                for kt in range(KD):
                    pe.wait_ge(sq_ready, 4 * no + kt // 2 + 1)
                    mm = pe.matmul(ps[0][:, 0:S], ones, sq[:, kt, :], start=(kt == 0), stop=(kt == KD - 1))
                mm.then_inc(ss_ready, 1)

            def head_norm(c, bank=ps[3]):
                pe.wait_ge(hn_sq, c + 1)
                pe.wait_ge(hn_std, c + 1)
                pe.matmul(bank[:, 0:S], bd, hsq, start=True, stop=True).then_inc(hn_ss, 1)

            def scores(g, k, inst):
                pe.wait_ge(neg_ready, g + k + 1)
                h = slice(inst["half"] * HD, inst["half"] * HD + HD)
                bank = ps[4 + k % 2]
                if inst["kind"] == "cmp":
                    for tt in range(TT):
                        mm = pe.matmul(bank[:, tt * NCMP:(tt + 1) * NCMP], inst["q"][h, tt * P:(tt + 1) * P],
                                       inst["k"][h, :], start=True, stop=True)
                else:
                    row = inst.get("row")
                    for tt in range(TT):
                        out = bank[:, 0:P] if tt == 0 else bank[:, P:TW]
                        n = P * (tt + 1)
                        mm = pe.matmul(out, inst["q"][h, tt * P:(tt + 1) * P], inst["k"][h, 0:n],
                                       start=True, stop=row is None)
                        if row is not None:
                            mm = pe.matmul(out, ones[0:1, :], row(n), start=False, stop=True)
                mm.then_inc(s_ready, 1)

            def attend(g, k, inst, ahead=None, before=()):
                bank = ps[6 + k % 2]
                pr, pT = prob[:, k % 2], pt[:, k % 2]
                pe.wait_ge(pn_ready, g + k + 1)
                if inst["kind"] == "cmp":
                    for tt in range(TT):
                        mm = pe.transpose(bank[0:NCMP, tt * P:(tt + 1) * P], pr[:, tt * NCMP:(tt + 1) * NCMP], ident)
                else:
                    for b in range(3):
                        mm = pe.transpose(bank[:, b * P:(b + 1) * P], pr[:, b * P:(b + 1) * P], ident)
                mm.then_inc(t_ready, 1)
                if ahead is not None:
                    scores(g, k + 2, ahead)
                pe.wait_ge(pt_ready, g + k + 1)
                for semaphore, value in before:
                    pe.wait_ge(semaphore, value)
                half = inst["half"]
                out = ps[inst.get("bank", 2) + half][half * HD:half * HD + HD, 0:S]
                begins, ends = inst["begins"], inst["ends"]
                if inst["kind"] == "cmp":
                    mm = pe.matmul(out, inst["v"], pT[0:NCMP, 0:S], start=begins, stop=ends)
                else:
                    pe.matmul(out, inst["v"][0], pT[:, 0:S], start=begins, stop=False)
                    mm = pe.matmul(out[:, P:S], inst["v"][1], pT[:, S:TW], start=False, stop=ends)
                if inst["last"]:
                    mm.then_inc(o_done, 1)

            def output(unit):
                for n in range(KD):
                    products(ps[4 + n // 2][:, (n % 2) * S:(n % 2 + 1) * S], unit + n, lambda kt: oT[:, kt, :])

            def column_sums(bank, sums):
                for n in range(KD):
                    mm = pe.matmul(bank[:, n:n + 1], sums[:, n * P:(n + 1) * P], ones[:, 0:1], start=True, stop=True)
                mm.then_inc(ada_sum, 1)

            def spread(unit, it, per, rhs, first, last):
                w = slot_of(unit)
                wait_unit(pe, unit, it, per)
                for n in range(KD):
                    mm = pe.matmul(ps[4 + n // 2][:, (n % 2) * S:(n % 2 + 1) * S], w[:, n, :], rhs,
                                   start=first and n % 2 == 0, stop=last, skip_group_check=True)
                mm.then_inc(unit_done, 1)

            def mix0(u):
                products(ps[0][0:8, 0:S], u, lambda kt: hT[:, kt, :], m=8, h_from=0)
                u += 1
                pe.wait_ge(logf_ready, 1)
                h = lambda kt: hT[:, kt, :]
                with pe.Fori(0, 2) as i:
                    for e in range(2):
                        v = u + 6 * e
                        r = i * 2 + e
                        pe.wait_ge(conv_c, r + 1)
                        products(ps[0][:, 0:S], v, h, i, 12)
                        pe.wait_ge(conv_u, r + 1)
                        products(ps[1][:, 0:S], v + 1, h, i, 12)
                        pe.wait_ge(o_read, r + pair0["mix0"])
                        head_norm(r * 2)
                        products_t(ps[2], v + 2, P, i, 12)
                        head_norm(r * 2 + 1)
                        pe.wait_ge(hn_out, r * 2 + 2)
                        if e == 0:
                            pe.wait_ge(cum_row, 16)
                        insts = [dict(half=f, kind="full", q=qs[:, 0], k=ks[:, 0], begins=True, ends=True, last=f == 1,
                                      v=[v_sb[:, b, f * HD:f * HD + HD] for b in range(2)],
                                      row=lambda n, hd=r * 2 + f: cumrow[0:1, hd, 0:n]) for f in range(2)]
                        scores(r * 2, 0, insts[0])
                        scores(r * 2, 1, insts[1])
                        products(ps[0][:, 0:S], v + 3, h, i, 12)
                        products(ps[1][:, 0:S], v + 4, h, i, 12)
                        pe.wait_ge(v_ready, r + 1)
                        products(ps[2][:, 0:S], v + 5, h, i, 12)
                        attend(r * 2, 0, insts[0], before=((conv_out, r + 1),))
                        attend(r * 2, 1, insts[1])
                u += 24
                pe.wait_ge(o_read, pair0["mix0"] + 4)
                output(u)
                pe.wait_ge(ada_acc, 6)
                for a in range(4):
                    column_sums(ps[a], acc4[:, a])

            def mix1(u):
                h = lambda kt: hT[:, kt, :]
                hn = hn0["mix1"]
                for n in range(4):
                    if n >= 2:
                        pe.wait_ge(kv_raw, n - 1)
                    products(ps[n % 2][:, 0:S], u + n, h, h_from=KD * norm_no_h["mix1"] if n == 0 else None)
                for n in range(4):
                    if n < 2:
                        pe.wait_ge(kv_raw, 3 + n)
                    else:
                        pe.wait_ge(hn_out, hn + n - 1)
                    products(ps[n % 2][:, 0:S], u + 4 + n, h)
                    if n:
                        head_norm(hn + n - 1)
                for n in range(4):
                    if n == 1:
                        head_norm(hn + 3)
                    if n < 2:
                        pe.wait_ge(hn_out, hn + 3 + n)
                    else:
                        pe.wait_ge(kv_out, n - 1)
                    products_t(ps[n % 2], u + 8 + n)
                pe.wait_ge(kv_out, 4)
                u += 12
                for a in range(2):
                    pe.wait_ge(blk_ready, 2 * (a + 1))
                    for q in range(4):
                        w = slot_of(u + 4 * a + q)
                        wait_unit(pe, u + 4 * a + q)
                        for l in range(8):
                            mm = pe.matmul(ps[a][:, 0:2 * NCMP], w[:, l, :], blk[:, a, q * 8 + l, :, :],
                                           start=(q == 0 and l == 0), stop=(q == 3 and l == 7))
                        mm.then_inc(unit_done, 1)
                u += 8
                products_t(ps[2], u, 48)
                u += 1
                pe.wait_ge(cmp_h, 1)
                pe.matmul(ps[0][:, 0:2 * NCMP], pc("w2", 0, P), chid[:, 0, 0:2 * NCMP],
                          start=True, stop=True).then_inc(cmp_mm, 1)
                pe.wait_ge(cmp_h, 2)
                for c in range(2):
                    mm = pe.matmul(ps[1][0:NCMP, c * P:(c + 1) * P], chid[:, 1, c * NCMP:(c + 1) * NCMP],
                                   pc("w2", P, P), start=True, stop=True)
                mm.then_inc(cmp_mm, 1)
                pe.wait_ge(hn_sq, hn + 5)
                pe.matmul(ps[3][:, 0:2 * NCMP], bd, hsq[:, 0:2 * NCMP], start=True, stop=True).then_inc(hn_ss, 1)
                pe.wait_ge(cmp_vc, 1)
                pe.wait_ge(hn_out, hn + 5)
                with pe.Fori(0, 2) as i:
                    for e in range(4):
                        pe.wait_ge(hn_out, i * 4 + (hn + 4 + e))
                        products(ps[e % 2][:, 0:S], u + e, h, i, 4)
                        if e:
                            head_norm(i * 4 + (hn + 4 + e))
                    head_norm(i * 4 + (hn + 8))
                u += 8
                pe.wait_ge(gate_ready, 1)
                with pe.Fori(0, 4) as i:
                    g, r = i * 12 + att0["mix1"], i * 2 + pair0["mix1"]
                    insts = [
                        dict(half=f, kind="cmp" if kind == 0 else "full", q=qs[:, half], bank=2 - 2 * half, pair=half,
                             k=kc_sb[:, half * NCMP:(half + 1) * NCMP] if kind == 0 else ks[:, 1 + 2 * (kind - 1) + half],
                             v=(vc_sb[0:NCMP, half, f * HD:f * HD + HD] if kind == 0 else
                                [v_sb[:, (4 * (kind - 1)) + 2 * half + b, f * HD:f * HD + HD] for b in range(2)]),
                             begins=kind == 0, ends=kind == 2, last=kind == 2 and f == 1)
                        for half in range(2) for kind in range(3) for f in range(2)]
                    pe.wait_ge(q_staged, i * 2 + 1)
                    scores(g, 0, insts[0])
                    scores(g, 1, insts[1])
                    for k, inst in enumerate(insts):
                        if k == 4:
                            pe.wait_ge(q_staged, i * 2 + 2)
                        attend(g, k, inst, insts[k + 2] if k < 10 else None,
                               before=((o_read, r + (inst["pair"] - 1)),) if inst["begins"] else ())
                pe.wait_ge(o_read, pair0["mix1"] + 8)
                output(u)

            def hyb(ph, l, u):
                h = lambda kt: hT[:, kt, :]
                products(ps[1][:, 0:S], u, h, h_from=KD * norm_no_h[ph])
                pe.wait_ge(cum_row, 32)
                products_t(ps[2], u + 1, brow=vr[0:1, l, 0, :])
                products(ps[0][:, 0:S], u + 2, h)
                u += 3
                pe.wait_ge(v_ready, 4 + 5 * l + 1)

                def pairs(i, more):
                    g, r = i * 4 + att0[ph], i * 2 + pair0[ph]
                    pe.wait_ge(q_ready, i * 3 + (13 * l + 2))
                    window = [dict(half=f, kind="full", q=qs[:, 0], k=ks[:, 1], begins=True, ends=True, last=f == 1,
                                   v=[v_sb[:, 2 + b, f * HD:f * HD + HD] for b in range(2)]) for f in range(2)]
                    scores(g, 0, window[0])
                    scores(g, 1, window[1])
                    products(ps[1][:, 0:S], u, h, i, 4)
                    products(ps[0][:, 0:S], u + 1, h, i, 4)
                    pe.wait_ge(q_ready, i * 3 + (13 * l + 3))
                    products_t(ps[1], u + 2, P, i, 4, brow=vr[0:1, l, i + 1, :])
                    attend(g, 0, window[0], before=((o_read, r),))
                    attend(g, 1, window[1])
                    pe.wait_ge(q_ready, i * 3 + (13 * l + 4))
                    pe.wait_ge(v_ready, i + (4 + 5 * l + 2))
                    g = g + 2
                    causal = [dict(half=f, kind="full", q=qs[:, 1], k=ks[:, 0], begins=True, ends=True, last=f == 1,
                                   v=[v_sb[:, b, f * HD:f * HD + HD] for b in range(2)]) for f in range(2)]
                    scores(g, 0, causal[0])
                    scores(g, 1, causal[1])
                    if more:
                        products(ps[0][:, 0:S], u + 3, h, i, 4)
                    attend(g, 0, causal[0], before=((o_read, r + 1),))
                    attend(g, 1, causal[1])

                with pe.Fori(0, 3) as i:
                    pairs(i, True)
                pairs(3, False)
                u += 15
                pe.wait_ge(o_read, pair0[ph] + 8)
                pe.wait_ge(on_ready, 6 * l + 2)
                for grp in range(2):
                    for kt in range(4):
                        mm = pe.matmul(ps[grp][:, 0:S], ones, sq[:, 4 * grp + kt, :], start=(kt == 0), stop=(kt == 3))
                mm.then_inc(on_ready, 1)
                pe.wait_ge(on_ready, 6 * l + 6)
                output(u)

            def ffn(ph, no, u):
                pe.wait_ge(h_ready, KD * norm_no_h[ph] + 1)
                h = lambda kt: hT[:, kt, :]
                with pe.Fori(0, NF // 2) as i:
                    for e in range(2):
                        if e == 0:
                            pe.wait_ge(h_ready, KD * (norm_no_h[ph] + 1))
                        pe.wait_ge(ffn_h, i * 2 + (NF * no + e + 1))
                        products(ps[2 * e][:, 0:S], u + 2 * e, h, i, 4)
                        products(ps[2 * e + 1][:, 0:S], u + 2 * e + 1, h, i, 4)
                u += 2 * NF
                pe.wait_ge(ffn_h, NF * (no + 1) + 2)
                for f in range(2):
                    spread(u + f, 0, 0, hid[:, f, :], f == 0, False)
                with pe.Fori(0, 4) as i:
                    for e in range(4):
                        spread(u + 2 + e, i, 4, hid[:, i * 4 + (2 + e), :], False, False)
                for f in range(18, NF):
                    spread(u + f, 0, 0, hid[:, f, :], False, f == NF - 1)

            def peer(ph, l, u):
                h = lambda kt: hT[:, kt, :]
                keys = pc("keys", l * NE, NE)
                for hd in range(PH):
                    if hd >= 2:
                        pe.wait_ge(pq_ready, PH * l + hd - 1)
                    products(ps[hd % 2][:, 0:S], u + hd, h, h_from=KD * norm_no_h[ph] if hd == 0 else None)
                    pe.wait_ge(pq_ready, PH * l + hd + 1)
                    if hd >= 2:
                        pe.wait_ge(ps_read, PH * l + hd - 1)
                    for tt in range(TT):
                        for half in range(2):
                            rows_ = slice(half * HD, half * HD + HD)
                            mm = pe.matmul(ps[2 + 2 * (hd % 2) + half][:, tt * P:(tt + 1) * P],
                                           pq[rows_, hd % 2, tt * P:(tt + 1) * P], keys[rows_, :],
                                           start=True, stop=True)
                    mm.then_inc(ps_ready, 1)
                u += PH
                pe.wait_ge(ps_read, PH * (l + 1))
                with pe.Fori(0, NE // 4) as i:
                    for e in range(4):
                        pe.wait_ge(gelu_ready, i * 4 + (NE * l + e + 1))
                        products(ps[e % 2][:, 0:S], u + e, h, i, 4)
                u += NE
                for tt in range(TT):
                    pe.wait_ge(route_ready, TT * l + tt + 1)
                    for w in range(3):
                        mm = pe.transpose(ps[2][:, w * P:(w + 1) * P] if tt == 0 else ps[3][:, w * P:(w + 1) * P],
                                          r_out[:, tt, w, :], ident)
                    mm.then_inc(routeT_ready, 1)
                pe.wait_ge(routeT_read, TT * (l + 1))
                pe.wait_ge(gelu_ready, NE * (l + 1) + 2)
                with pe.Fori(0, S // 4 // GB) as i:
                    for e in range(GB):
                        pe.wait_ge(hot_ready, i * GB + (S // 4 * l + e + 1))
                        pe.wait_ge(hot2_ready, i * GB + (S // 4 * l + e + 1))
                        pe.wait_ge(g_read, i * GB + (S // 4 * l + e + 1))
                        for t in range(4):
                            mm = pe.matmul(ps[e][:, t * NE:(t + 1) * NE], hot[:, e, 0, t, :], hot[:, e, 1, t, :],
                                           start=True, stop=True)
                        mm.then_inc(g_ready, 1)
                pe.wait_ge(g_read, S // 4 * (l + 1) + GB)
                for j in range(4):
                    spread(u + j, 0, 0, arena[:, j, :], j == 0, False)
                done = 4
                if l == 0:
                    with pe.Fori(0, 12) as i:
                        for b in range(2):
                            for e in range(4):
                                spread(u + 4 + e, i * 2 + b, 4, arena[:, i * 8 + (4 * b + 4 + e), :], False, False)
                            pe.wait_ge(ada_acc, i * 2 + (6 + b + 1))
                            pe.wait_ge(ada_read, i * 2 + (6 + b - 1))
                            column_sums(ps[b], acc[:, b])
                    done += 96
                with pe.Fori(0, (NE - 4 - done) // 4) as i:
                    for e in range(4):
                        spread(u + done + e, i, 4, arena[:, i * 4 + (done + e), :], False, False)
                for j in range(NE - 4, NE):
                    spread(u + j, 0, 0, arena[:, j, :], False, j == NE - 1)

            pe.wait_ge(params_in, 48)
            pe.wait_ge(tab_ready, 1)
            for a, name in enumerate(("rel", "rel2")):
                c0, w = TAB[name]
                h0 = TAB["hot"][0]
                mm = pe.matmul(ps[2 + a][0:16, :], tabs[0:32, c0:c0 + w], tabs[0:32, h0:h0 + 512], start=True, stop=True)
            mm.then_inc(tab_read, 1)
            for ph in phases:
                sum_squares(norm_no[ph])
                if ph == "mix0":
                    for v in range(2):
                        pe.wait_ge(ada_acc, v + 1)
                        column_sums(ps[4 + v], acc[:, v])
                u = start[ph]
                if ph == "mix0":
                    mix0(u)
                elif ph == "mix1":
                    mix1(u)
                elif ph.startswith("peer"):
                    peer(ph, int(ph[-1]), u)
                elif ph.startswith("ffn"):
                    ffn(ph, int(ph[-1]), u)
                else:
                    hyb(ph, int(ph[-1]), u)
                if norm_no[ph] >= 4:
                    sum_squares(norm_no[ph] + 1)

        @block.scalar
        def _(act):
            def norm_in(no, ph):
                i = phases.index(ph)
                for q in range(4):
                    if i:
                        act.wait_ge(x_ready, KD * (i - 1) + 2 * q + 2)
                    nc.scalar.activation(sq[:, 2 * q:2 * q + 2, :], x[:, 2 * q:2 * q + 2, :], ACT.Square).then_inc(sq_ready, 1)
                act.wait_ge(ss_ready, no + 1)
                nc.scalar.activation(stat[:, 0], ps[0][:, 0:S], ACT.Sqrt, bias=eps, scale=1.0 / D).then_inc(std_ready, 1)

            def shift(ph, vec):
                n = norm_no_h[ph]
                for kt in range(KD):
                    act.wait_ge(mid_ready, KD * n + kt + 1)
                    nc.scalar.activation(hT[:, kt, :], hT[:, kt, :], ACT.Identity,
                                         bias=mods[:, vec, kt:kt + 1]).then_inc(h_ready, 1)

            def norm_out(no, unit_last):
                wait_used(act, unit_last)
                for q in range(4):
                    nc.scalar.activation(sq[:, 2 * q:2 * q + 2, :], ps[4 + q][:].rearrange("p (a b) -> p a b", a=2),
                                         ACT.Square).then_inc(sq_ready, 1)
                act.wait_ge(ss_ready, no + 1)
                nc.scalar.activation(stat[:, 0], ps[0][:, 0:S], ACT.Sqrt, bias=eps, scale=1.0 / D).then_inc(std_ready, 1)

            def head_norm(c, bank, n=S, b=0, sums=ps[3]):
                nc.scalar.activation(hsq[:, 0:n], bank[:, 0:n], ACT.Square).then_inc(hn_sq, 1)
                act.wait_ge(hn_ss, c + 1)
                nc.scalar.activation(hstd[:, b, 0:n], sums[:, 0:n], ACT.Sqrt, bias=eps, scale=1.0 / HD).then_inc(hn_std, 1)

            def exps(g, k, inst):
                act.wait_ge(neg_ready, g + k + 3)
                b = k % 2
                n = NCMP if inst["kind"] == "cmp" else None
                for tt in range(TT):
                    cols = slice(tt * NCMP, (tt + 1) * NCMP) if n else (slice(0, P) if tt == 0 else slice(P, TW))
                    a = nc.scalar.activation(prob[:, b, cols], neg[:, b, cols], ACT.Exp, bias=negm[:, b, tt:tt + 1],
                                             scale=-1.0, accum_out=rows[:, b, tt:tt + 1])
                    if inst.get("sink"):
                        a = nc.scalar.activation(sink_e[:, b, tt:tt + 1], nsk[:, inst["half"]:inst["half"] + 1],
                                                 ACT.Exp, bias=negm[:, b, tt:tt + 1], scale=-1.0)
                a.then_inc(exp_ready, 1)

            def turned(g, k, inst):
                act.wait_ge(t_ready, g + k + 1)
                if inst["kind"] == "cmp":
                    c = nc.scalar.copy(pt[0:NCMP, k % 2, 0:S], ps[6 + k % 2][0:NCMP, 0:S])
                else:
                    c = nc.scalar.copy(pt[:, k % 2, :], ps[6 + k % 2][:, 0:TW])
                c.then_inc(pt_ready, 1)

            def attention(g, insts):
                exps(g, 0, insts[0])
                exps(g, 1, insts[1])
                for k, inst in enumerate(insts):
                    turned(g, k, inst)
                    if k + 2 < len(insts):
                        exps(g, k + 2, insts[k + 2])

            def ada_load(n, it=0, per=0, count=4):
                for q in range(n, n + count):
                    if q >= SLOTS or per:
                        act.wait_ge(ada_used, it * per + (q - SLOTS + 1))
                    act.dma_start(adaw[:, q % SLOTS], ada[it * per + q] if per else ada[q]).then_inc(ada_loaded[q % SLOTS], 16)

            full = [dict(half=f, kind="full") for f in range(2)]

            def mix0(u):
                act.wait_ge(logf_ready, 1)
                nc.scalar.activation(ftmp[0:8, 2, :], ftmp[0:8, 1, :], ACT.Exp)
                act.drain()
                nc.scalar.activation(ftmp[0:8, 3, :], ftmp[0:8, 2, :], ACT.Ln, bias=1.0).then_inc(logf_act, 1)
                u += 1

                def pair(r, more):
                    wait_used(act, u, r, 6)
                    head_norm(r * 2, ps[0])
                    wait_used(act, u + 1, r, 6)
                    head_norm(r * 2 + 1, ps[1], b=1)
                    wait_used(act, u + 2, r, 6)
                    nc.scalar.copy(v_sb[:, 0:2, :], ps[2][:, 0:S].rearrange("p (a b) -> p a b", a=2)).then_inc(v_ready, 1)
                    exps(r * 2, 0, full[0])
                    exps(r * 2, 1, full[1])
                    ada_load(20, r, 8)
                    wait_used(act, u + 3, r, 6)
                    nc.scalar.copy(ccs, ps[0][:, 0:S]).then_inc(conv_c, 1)
                    turned(r * 2, 0, full[0])
                    turned(r * 2, 1, full[1])
                    if more:
                        ada_load(24, r, 8)

                with act.Fori(0, 3) as r:
                    pair(r, True)
                pair(3, False)

            def mix1(u):
                hn = hn0["mix1"]
                for n in range(4):
                    wait_used(act, u + n)
                    nc.scalar.copy(kcv[:, n, :], ps[n % 2][:, 0:S]).then_inc(kv_raw, 1)
                for n in range(4):
                    wait_used(act, u + 4 + n)
                    head_norm(hn + n, ps[n % 2], b=n % 2)
                for n in range(4):
                    wait_used(act, u + 8 + n)
                    nc.scalar.copy(v_sb[:, 2 * n:2 * n + 2, :],
                                   ps[n % 2][:, 0:S].rearrange("p (a b) -> p a b", a=2)).then_inc(kv_out, 1)
                u += 12
                for a in range(2):
                    wait_used(act, u + 4 * a + 3)
                    nc.scalar.activation(chid[:, a, 0:2 * NCMP], ps[a][:, 0:2 * NCMP], ACT.Gelu_apprx_tanh).then_inc(cmp_h, 1)
                u += 8
                act.wait_ge(cmp_mm, 1)
                head_norm(hn + 4, ps[0], 2 * NCMP)
                act.wait_ge(cmp_mm, 2)
                nc.scalar.copy(vc_sb[0:NCMP, :, :], ps[1][0:NCMP, 0:2 * P].rearrange("p (a b) -> p a b", a=2)).then_inc(cmp_vc, 1)
                act.wait_ge(gate_z, 1)
                nc.scalar.activation(gates, gsum, ACT.Sigmoid).then_inc(gate_s, 1)
                u += 1
                with act.Fori(0, 2) as i:
                    for e in range(4):
                        wait_used(act, u + e, i, 4)
                        head_norm(i * 4 + (hn + 5 + e), ps[e % 2], b=e % 2)
                insts = [dict(half=f, kind="cmp" if kind == 0 else "full")
                         for half in range(2) for kind in range(3) for f in range(2)]
                with act.Fori(0, 4) as i:
                    attention(i * 12 + att0["mix1"], insts)

            def hyb(ph, l, u):
                wait_used(act, u + 1)
                nc.scalar.copy(v_sb[:, 2:4, :], ps[2][:, 0:S].rearrange("p (a b) -> p a b", a=2)).then_inc(v_ready, 1)
                u += 3
                window = [dict(half=f, kind="full", sink=True) for f in range(2)]

                def pairs(i):
                    g = i * 4 + att0[ph]
                    exps(g, 0, window[0])
                    exps(g, 1, window[1])
                    wait_used(act, u + 2, i, 4)
                    nc.scalar.copy(v_sb[:, 0:2, :], ps[1][:, 0:S].rearrange("p (a b) -> p a b", a=2)).then_inc(v_ready, 1)
                    turned(g, 0, window[0])
                    turned(g, 1, window[1])
                    attention(g + 2, full)

                with act.Fori(0, 3) as i:
                    pairs(i)
                pairs(3)
                act.wait_ge(o_read, pair0[ph] + 8)
                for grp in range(2):
                    nc.scalar.activation(sq[:, 4 * grp:4 * grp + 4, :], oT[:, 4 * grp:4 * grp + 4, :], ACT.Square).then_inc(on_ready, 1)
                act.wait_ge(on_ready, 6 * l + 3)
                for grp in range(2):
                    a = nc.scalar.activation(conv_t[:, grp, :], ps[grp][:, 0:S], ACT.Sqrt, bias=eps, scale=1.0 / 512)
                a.then_inc(on_ready, 1)

            def ffn(no, u):
                with act.Fori(0, NF // 2) as i:
                    for e in range(2):
                        wait_used(act, u + 2 * e, i, 4)
                        nc.scalar.activation(sl[:, e, :], ps[2 * e][:, 0:S], ACT.Silu).then_inc(silu_ready, 1)

            def peer(l, u):
                for hd in range(PH):
                    wait_used(act, u + hd)
                    nc.scalar.copy(pq[:, hd % 2, :], ps[hd % 2][:, 0:S]).then_inc(pq_ready, 1)
                    act.wait_ge(ps_ready, PH * l + hd + 1)
                    for half in range(2):
                        c = nc.scalar.copy(score[:, :, 2 * hd + half, :],
                                           ps[2 + 2 * (hd % 2) + half][:, 0:S].rearrange("p (t n) -> p t n", t=TT))
                    c.then_inc(ps_read, 1)
                u += PH
                third = NE // 4 // 3
                for tt, (lo, hi) in enumerate(((0, third), (third, 2 * third), (2 * third, NE // 4))):
                    with act.Fori(lo, hi) as i:
                        for e in range(4):
                            wait_used(act, u + e, i, 4)
                            nc.scalar.activation(arena[:, i * 4 + e, :], ps[e % 2][:, 0:S],
                                                 ACT.Gelu_apprx_tanh).then_inc(gelu_ready, 1)
                    if tt < TT:
                        act.wait_ge(rexp_in, TT * l + tt + 1)
                        nc.scalar.activation(r_out[:, tt, 2, :], r_cv[:].rearrange("p g k -> p (g k)"),
                                             ACT.Exp).then_inc(rexp_out, 1)
                act.wait_ge(routeT_read, TT * (l + 1))
                oT4 = r_outT[:].rearrange("p w (c b t) -> p w c b t", b=GB, t=4)
                with act.Fori(0, S // 4 // GB) as i:
                    for c in range(0, GB, 2):
                        for e in range(c, c + 2):
                            act.wait_ge(g_ready, i * GB + (S // 4 * l + e + 1))
                            for t in range(4):
                                nc.scalar.activation(hot[:, e, 1, t, :], iota, ACT.Square, bias=oT4[:, 1, i, e, t:t + 1])
                        act.drain()
                        for e in range(c, c + 2):
                            nc.scalar.activation(hot[:, e, 1, :, :], hot[:, e, 1, :, :], ACT.Relu, bias=1.0,
                                                 scale=-1.0).then_inc(hot2_ready, 1)
                if l == 0:
                    act.wait_ge(g_read, S // 4 + GB)
                    ada_load(48)
                    with act.Fori(0, 24 * KD // SLOTS - 1) as i:
                        ada_load(52, i, SLOTS)

            act.wait_ge(params_in, 48)
            act.wait_ge(setup_done, 1)
            nc.scalar.activation(cact, pc("c"), ACT.Silu).then_inc(c_ready, 1)
            ada_load(0)
            for ph in phases:
                norm_in(norm_no[ph], ph)
                if ph == "mix0":
                    for n in range(4, 20, 4):
                        ada_load(n)
                    act.wait_ge(ada_read, 2)
                shift(ph, vec_of(ph))
                u = start[ph]
                if ph == "mix0":
                    mix0(u)
                elif ph == "mix1":
                    mix1(u)
                elif ph.startswith("peer"):
                    peer(int(ph[-1]), u)
                elif ph.startswith("ffn"):
                    ffn(int(ph[-1]), u)
                else:
                    hyb(ph, int(ph[-1]), u)
                if norm_no[ph] >= 4:
                    norm_out(norm_no[ph] + 1, u + phase_units(ph) - 1)

        @block.vector
        def _(dve):
            V = nc.vector

            def norm_in(ph, vec, gain):
                V.scalar_tensor_tensor(out=acol[:], in0=mods[:, vec + 1, :], scalar=1.0, in1=gain, op0=ALU.add, op1=ALU.mult)
                dve.wait_ge(std_ready, norm_no[ph] + 1)
                V.reciprocal(stat[:, 1], stat[:, 0])
                dve.drain()
                for kt in range(KD):
                    V.scalar_tensor_tensor(out=hT[:, kt, :], in0=x[:, kt, :], scalar=acol[:, kt:kt + 1], in1=stat[:, 1],
                                           op0=ALU.mult, op1=ALU.mult).then_inc(mid_ready, 1)

            def y_of(n):
                return ps[4 + n // 2][:, (n % 2) * S:(n % 2 + 1) * S]

            def add_plain(ph, vec):
                wait_used(dve, start[ph] + phase_units(ph) - 1)
                for n in range(KD):
                    V.scalar_tensor_tensor(out=x[:, n, :], in0=y_of(n), scalar=mods[:, vec + 2, n:n + 1], in1=x[:, n, :],
                                           op0=ALU.mult, op1=ALU.add).then_inc(x_ready, 1)
                dve.drain()

            def add_normed(ph, vec, post, factor):
                V.scalar_tensor_tensor(out=acol[:], in0=mods[:, vec + 2, :], scalar=factor, in1=post, op0=ALU.mult, op1=ALU.mult)
                dve.wait_ge(std_ready, norm_no[ph] + 2)
                V.reciprocal(stat[:, 1], stat[:, 0])
                dve.drain()
                for n in range(KD):
                    V.scalar_tensor_tensor(out=gtmp[:, n, :], in0=y_of(n), scalar=acol[:, n:n + 1], in1=stat[:, 1],
                                           op0=ALU.mult, op1=ALU.mult)
                dve.drain()
                for n in range(KD):
                    V.tensor_tensor(out=x[:, n, :], in0=x[:, n, :], in1=gtmp[:, n, :], op=ALU.add).then_inc(x_ready, 1)
                dve.drain()

            def head_norm(c, out, bank, gcol, n=S, b=0):
                dve.drain()
                dve.wait_ge(hn_std, c + 2)
                V.reciprocal(hrec[:, 0:n], hstd[:, b, 0:n])
                dve.drain()
                V.scalar_tensor_tensor(out=out, in0=bank[:, 0:n], scalar=gcol, in1=hrec[:, 0:n],
                                       op0=ALU.mult, op1=ALU.mult).then_inc(hn_out, 1)

            def lowest(g, k, inst):
                wait_alone(dve, s_ready, g + k + 1)
                b = k % 2
                bank = ps[4 + b]
                first = inst.get("sink", FMAX)
                for tt in range(TT):
                    if inst["kind"] == "cmp":
                        cols = slice(tt * NCMP, (tt + 1) * NCMP)
                        o = (1 - tt) * P + CMP_LEN - 1
                        bias = nb[:, inst["nb"], inst["half"], o:o + 16 * (NCMP - 1) + 1:16]
                    else:
                        cols = slice(0, P) if tt == 0 else slice(P, TW)
                        if inst.get("row"):
                            bias = pc("cmask")[:, cols]
                        else:
                            bias = nb[:, inst["nb"], inst["half"], P:2 * P] if tt == 0 else nb[:, inst["nb"], inst["half"], 0:S]
                    m = V.tensor_tensor_reduce(out=neg[:, b, cols], in0=bank[:, cols], in1=bias, scale=1.0, scalar=first,
                                               op0=ALU.add, op1=ALU.min, accum_out=negm[:, b, tt:tt + 1])
                m.then_inc(neg_ready, 1)

            def normalize(g, k, inst):
                b = k % 2
                dve.wait_ge(exp_ready, g + k + 1)
                if "sink" in inst:
                    V.tensor_tensor(out=rows[:, b, :], in0=rows[:, b, :], in1=sink_e[:, b, :], op=ALU.add)
                    dve.drain()
                V.reciprocal(rinv[:, b, :], rows[:, b, :])
                dve.drain()
                for tt in range(TT):
                    if inst["kind"] == "cmp":
                        cols = slice(tt * NCMP, (tt + 1) * NCMP)
                    else:
                        cols = slice(0, P) if tt == 0 else slice(P, TW)
                    gate = inst["gate"][:, tt:tt + 1] if "gate" in inst else None
                    m = V.tensor_scalar(prob[:, b, cols], prob[:, b, cols], rinv[:, b, tt:tt + 1], gate, ALU.mult,
                                        ALU.bypass if gate is None else ALU.mult)
                m.then_inc(pn_ready, 1)

            def take_outputs(pairs, chunk, bank=2):
                dve.wait_ge(o_done, pairs)
                V.tensor_copy(oT[0:HD, chunk, :], ps[bank][0:HD, 0:S])
                V.tensor_copy(oT[HD:P, chunk, :], ps[bank + 1][HD:P, 0:S]).then_inc(o_read, 1)

            def ada_part(sums, n, cc, first, it=0, per=0):
                for q in range(4):
                    k = (0 if first else 4) + q
                    dve.drain()
                    dve.wait_ge(ada_loaded[q], it * (per // SLOTS * 16) + 16 * (n // SLOTS + 1))
                    col = cact[:, cc + k:cc + k + 1]
                    if k == 0:
                        m = V.tensor_scalar(sums, adaw[:, q], col, None, ALU.mult)
                    else:
                        m = V.scalar_tensor_tensor(out=sums, in0=adaw[:, q], scalar=col, in1=sums, op0=ALU.mult, op1=ALU.add)
                    m.then_inc(ada_used, 1)
                if not first:
                    dve.drain()
                    V.tensor_copy(small[:, 60:61], sums[:, 0:1]).then_inc(ada_acc, 1)

            def ada_take(v, bank):
                V.tensor_tensor(out=mods[:, v, :], in0=bank[:, 0:KD],
                                in1=pc("adab").rearrange("p (v k) -> p v k", v=NVEC)[:, v, :], op=ALU.add).then_inc(ada_read, 1)

            def mix0(u):
                V.memset(u_pad[:, 0:2], 0.0)
                wait_used(dve, u)
                V.tensor_scalar(ftmp[0:8, 0, :], ps[0][0:8, 0:S], pc("bf")[0:8, :], None, ALU.add)
                dve.drain()
                V.scalar_tensor_tensor(out=ftmp[0:8, 1, :], in0=ftmp[0:8, 0, :], scalar=-1.0, in1=ftmp[0:8, 0, :],
                                       op0=ALU.mult, op1=ALU.min).then_inc(logf_ready, 1)
                dve.wait_ge(logf_act, 1)
                V.scalar_tensor_tensor(out=ftmp[0:8, 1, :], in0=ftmp[0:8, 0, :], scalar=0.0, in1=ftmp[0:8, 3, :],
                                       op0=ALU.min, op1=ALU.subtract)
                V.memset(ftmp[0:8, 2, :], 1.0)
                dve.drain()
                V.tensor_tensor_scan(cum[0:8, :], ftmp[0:8, 2, :], ftmp[0:8, 1, :], 0.0, ALU.mult, ALU.add).then_inc(cum_ready, 1)
                gq = small[:, 1:2]
                V.tensor_scalar(gq, pc("fqg"), -SCALE, None, ALU.mult)
                dve.drain()
                u += 1
                w0 = COL["convw"][0]
                with dve.Fori(0, 2) as i:
                    for e in range(2):
                        r = i * 2 + e
                        ada_part(acc4[:, r, :], 16 + 8 * e, 0, True, i, 16)
                        head_norm(r * 2, qs[:, 0], ps[0], gq)
                        head_norm(r * 2 + 1, ks[:, 0], ps[1], pc("fkg"), b=1)
                        insts = [dict(half=f, kind="full", row=True) for f in range(2)]
                        for k in range(2):
                            lowest(r * 2, k, insts[k])
                        for k in range(2):
                            normalize(r * 2, k, insts[k])
                        ada_part(acc4[:, r, :], 20 + 8 * e, 0, False, i, 16)
                        dve.wait_ge(conv_c, r + 2)
                        wait_used(dve, u + 6 * e + 4, i, 12)
                        V.tensor_tensor(out=u_pad[:, 2:S + 2], in0=ps[1][:, 0:S], in1=ccs, op=ALU.mult).then_inc(conv_u, 1)
                        dve.drain()
                        wc = [prm[:, w0:w0 + 12].rearrange("p (c k) -> p c k", k=3)[:, r, q:q + 1] for q in range(3)]
                        V.tensor_scalar(conv_t[:, 0, :], u_pad[:, 0:S], wc[0], None, ALU.mult)
                        dve.drain()
                        V.scalar_tensor_tensor(out=conv_t[:, 1, :], in0=u_pad[:, 1:S + 1], scalar=wc[1], in1=conv_t[:, 0, :],
                                               op0=ALU.mult, op1=ALU.add)
                        dve.drain()
                        V.scalar_tensor_tensor(out=conv_t[:, 0, :], in0=u_pad[:, 2:S + 2], scalar=wc[2], in1=conv_t[:, 1, :],
                                               op0=ALU.mult, op1=ALU.add)
                        dve.drain()
                        wait_used(dve, u + 6 * e + 5, i, 12)
                        V.tensor_tensor(out=oT[:, r, :], in0=ps[2][:, 0:S], in1=conv_t[:, 0, :], op=ALU.mult).then_inc(conv_out, 1)
                        take_outputs(r + pair0["mix0"], r + 4)
                for a in range(4):
                    dve.wait_ge(ada_sum, 3 + a)
                    ada_take(2 + a, ps[a])
                dve.drain()

            def mix1(u):
                hn = hn0["mix1"]
                gq = small[:, 2:3]
                V.tensor_scalar(gq, pc("nqg"), -SCALE, None, ALU.mult)
                dve.drain()
                for n in range(4):
                    head_norm(hn + n, ks[:, 1 + n], ps[n % 2], pc("nkg", 1 + n // 2, 1), b=n % 2)
                head_norm(hn + 4, kc_sb[:, 0:2 * NCMP], ps[0], pc("nkg", 0, 1), 2 * NCMP)
                u += 20
                wait_used(dve, u)
                V.tensor_tensor(out=gsum, in0=ps[2][:, 0:TT * 48].rearrange("p (a b) -> p a b", a=TT),
                                in1=pc("bgate").unsqueeze(1).to_broadcast([P, TT, 48]), op=ALU.add).then_inc(gate_z, 1)
                dve.wait_ge(gate_s, 1)
                g3 = gates[:].rearrange("p t (h y) -> p t h y", y=3)
                V.tensor_scalar(g3[:, 0, :, 0], g3[:, 0, :, 0], pc("rowmask"), None, ALU.mult).then_inc(gate_ready, 1)
                dve.drain()
                g6 = gates[:].rearrange("p t (a f j y) -> p t a f j y", a=2, f=2, j=4)
                u += 1
                with dve.Fori(0, 2) as i:
                    for e in range(4):
                        head_norm(i * 4 + (hn + 5 + e), qs_all[:, i * 4 + e, :], ps[e % 2], gq, b=e % 2)
                with dve.Fori(0, 4) as i:
                    g, r = i * 12 + att0["mix1"], i * 2 + pair0["mix1"]
                    insts = [dict(half=f, kind="cmp" if kind == 0 else "full", nb=half, gate=g6[:, :, half, f, i, kind])
                             for half in range(2) for kind in range(3) for f in range(2)]
                    dve.wait_ge(bias_in[0], i * 32 + 32 * (bias0["mix1"] + 1))
                    lowest(g, 0, insts[0])
                    lowest(g, 1, insts[1])
                    for k, inst in enumerate(insts):
                        normalize(g, k, inst)
                        if k == 4:
                            dve.wait_ge(bias_in[1], i * 32 + 32 * (bias0["mix1"] + 1))
                        if k < 10:
                            lowest(g, k + 2, insts[k + 2])
                        if k == 8:
                            take_outputs(r, i * 2)
                    take_outputs(r + 1, i * 2 + 1, 0)
                dve.drain()

            def hyb(ph, l, u):
                bcol = prm[:, COL["mixb"][0] + 13 * l:COL["mixb"][0] + 13 * l + 13]

                def project(out, bank, col, scale):
                    V.tensor_scalar(out, bank[:, 0:S], col, scale, ALU.add, ALU.mult).then_inc(q_ready, 1)

                sk = prm[:, COL["sinks"][0] + 8 * l:COL["sinks"][0] + 8 * l + 8].rearrange("p (j f) -> p j f", f=2)
                b3 = bcol[:, 0:4].rearrange("p (a b) -> p a b", b=1)
                b4 = bcol[:, 5:9].rearrange("p (a b) -> p a b", b=1)
                b5 = bcol[:, 9:13].rearrange("p (a b) -> p a b", b=1)
                wait_used(dve, u)
                project(ks[:, 1], ps[1], bcol[:, 4:5], 1.0)
                wait_used(dve, u + 2)
                project(qs[:, 0], ps[0], bcol[:, 0:1], -SCALE)
                u += 3
                window = [dict(half=f, kind="full", nb=0, sink=nsk[:, f:f + 1]) for f in range(2)]
                causal = [dict(half=f, kind="full", nb=1) for f in range(2)]

                def pairs(i, more):
                    g, r = i * 4 + att0[ph], i * 2 + pair0[ph]
                    V.tensor_scalar(nsk, sk[:, i, :], -1.0, None, ALU.mult)
                    dve.drain()
                    dve.wait_ge(bias_in[0], i * 32 + 32 * (bias0[ph] + 1))
                    for k in range(2):
                        lowest(g, k, window[k])
                    for k in range(2):
                        normalize(g, k, window[k])
                    wait_used(dve, u, i, 4)
                    project(qs[:, 1], ps[1], b4[:, i, :], -SCALE)
                    wait_used(dve, u + 1, i, 4)
                    project(ks[:, 0], ps[0], b5[:, i, :], 1.0)
                    take_outputs(r, i)
                    dve.wait_ge(bias_in[1], i * 32 + 32 * (bias0[ph] + 1))
                    g = g + 2
                    for k in range(2):
                        lowest(g, k, causal[k])
                    for k in range(2):
                        normalize(g, k, causal[k])
                    if more:
                        wait_used(dve, u + 3, i, 4)
                        project(qs[:, 0], ps[0], b3[:, i + 1, :], -SCALE)
                    take_outputs(r + 1, i + 4)

                with dve.Fori(0, 3) as i:
                    pairs(i, True)
                pairs(3, False)
                dve.wait_ge(on_ready, 6 * l + 4)
                g0 = COL["gain"][0] + KD * l
                for grp in range(2):
                    V.reciprocal(sq[:, grp, :], conv_t[:, grp, :])
                    dve.drain()
                    for kt in range(4):
                        n = 4 * grp + kt
                        m = V.scalar_tensor_tensor(out=oT[:, n, :], in0=oT[:, n, :], scalar=prm[:, g0 + n:g0 + n + 1],
                                                   in1=sq[:, grp, :], op0=ALU.mult, op1=ALU.mult)
                    m.then_inc(on_ready, 1)
                dve.drain()

            def ffn(no, u):
                with dve.Fori(0, NF // 2) as i:
                    for e in range(2):
                        dve.wait_ge(silu_ready, i * 2 + (NF * no + e + 1))
                        wait_used(dve, u + 2 * e + 1, i, 4)
                        V.tensor_tensor(out=hid[:, i * 2 + e, :], in0=ps[2 * e + 1][:, 0:S], in1=sl[:, e, :],
                                        op=ALU.mult).then_inc(ffn_h, 1)

            def peer(l, u):
                dve.wait_ge(ps_read, PH * (l + 1))
                for tt in range(TT):
                    sc = score[:, tt]
                    for g in range(16):
                        V.max(r_sv[:, g, 0:8], sc[:, g, :])
                    dve.drain()
                    for g in range(16):
                        V.max_index(r_si[:, g, 0:8], r_sv[:, g, 0:8], sc[:, g, :])
                    dve.drain()
                    for g in range(16):
                        V.match_replace(sc[:, g, :], r_sv[:, g, 0:8], sc[:, g, :], -FMAX)
                    dve.drain()
                    for g in range(16):
                        V.max(r_sv[:, g, 8:16], sc[:, g, :])
                    dve.drain()
                    for g in range(16):
                        V.max_index(r_si[:, g, 8:16], r_sv[:, g, 8:16], sc[:, g, :])
                    dve.drain()
                    V.tensor_copy(r_sif, r_si[:])
                    cand = sc.rearrange("p g n -> p (g n)").rearrange("p (h a b) -> p h a b", h=PH, a=TOPK)
                    sv4 = r_sv.rearrange("p (h w) k -> p h w k", w=2)
                    for h in range(PH):
                        V.tensor_tensor(out=cand[:, h], in0=sv4[:, h, 0, :].unsqueeze(2).to_broadcast([P, TOPK, TOPK]),
                                        in1=sv4[:, h, 1, :].unsqueeze(1).to_broadcast([P, TOPK, TOPK]), op=ALU.add)
                    dve.drain()
                    cf = sc.rearrange("p g n -> p (g n)").rearrange("p (h c) -> p h c", h=PH)
                    for h in range(PH):
                        V.max(r_cv[:, h, 0:8], cf[:, h, :])
                    dve.drain()
                    for h in range(PH):
                        V.max_index(r_ci[:, h, 0:8], r_cv[:, h, 0:8], cf[:, h, :])
                    dve.drain()
                    for h in range(PH):
                        V.match_replace(cf[:, h, :], r_cv[:, h, 0:8], cf[:, h, :], -FMAX)
                    dve.drain()
                    for h in range(PH):
                        V.max(r_cv[:, h, 8:16], cf[:, h, :])
                    dve.drain()
                    for h in range(PH):
                        V.max_index(r_ci[:, h, 8:16], r_cv[:, h, 8:16], cf[:, h, :])
                    dve.drain()
                    cif = r_ci[:].rearrange("p h k -> p (h k)")
                    V.tensor_scalar(r_ab[:, 0, :], cif, 4, None, ALU.logical_shift_right)
                    V.tensor_scalar(r_ab[:, 1, :], cif, 15, None, ALU.bitwise_and)
                    V.tensor_copy(r_sum, r_cv[:, :, 0])
                    dve.drain()
                    V.tensor_copy(r_abf, r_ab[:])
                    V.tensor_tensor(out=r_cv, in0=r_cv, in1=r_sum.unsqueeze(2).to_broadcast([P, PH, TOPK]),
                                    op=ALU.subtract).then_inc(rexp_in, 1)
                    dve.drain()
                    si4 = r_sif.rearrange("p (h w) k -> p h w k", w=2)
                    for w in range(2):
                        V.tensor_tensor(out=eq[:], in0=r_abf[:, w, :].unsqueeze(2).to_broadcast([P, NE, TOPK]),
                                        in1=iota[:, 0:TOPK].unsqueeze(1).to_broadcast([P, NE, TOPK]), op=ALU.is_equal)
                        dve.drain()
                        for h in range(PH):
                            V.tensor_tensor(out=eq[:, h * TOPK:(h + 1) * TOPK, :], in0=eq[:, h * TOPK:(h + 1) * TOPK, :],
                                            in1=si4[:, h, w, :].unsqueeze(1).to_broadcast([P, TOPK, TOPK]), op=ALU.mult)
                        dve.drain()
                        V.tensor_reduce(r_out[:, tt, w, :], eq[:], AX.X, ALU.add)
                        dve.drain()
                    dve.wait_ge(rexp_out, TT * l + tt + 1)
                    e3 = r_out[:, tt, 2, :].rearrange("p (h k) -> p h k", h=PH)
                    V.tensor_reduce(r_sum, e3, AX.X, ALU.add)
                    dve.drain()
                    V.reciprocal(r_rec, r_sum)
                    dve.drain()
                    V.tensor_tensor(out=e3, in0=e3, in1=r_rec.unsqueeze(2).to_broadcast([P, PH, TOPK]),
                                    op=ALU.mult).then_inc(route_ready, 1)
                for tt in range(TT):
                    dve.wait_ge(routeT_ready, TT * l + tt + 1)
                    toks = slice(tt * P, (tt + 1) * P)
                    V.tensor_copy(r_outT[:, 0:3:2, toks], ps[2 + tt][:, 0:3 * P].rearrange("p (w t) -> p w t", w=3)[:, 0:3:2, :])
                    V.tensor_scalar(r_outT[:, 1, toks], ps[2 + tt][:, P:2 * P], -1.0, None, ALU.mult)
                    dve.drain()
                    V.tensor_copy(small[:, 61:62], r_outT[:, 1, tt * P:tt * P + 1]).then_inc(routeT_read, 1)
                dve.drain()
                dve.wait_ge(gelu_ready, NE * (l + 1) + 2)

                def weigh(i, e):
                    dve.wait_ge(g_ready, i * GB + (S // 4 * l + e + 1 + GB))
                    a = arena[:].rearrange("p j (c b t) -> p j c b t", b=GB, t=4)[:, :, i, e, :]
                    V.tensor_tensor(out=a, in0=ps[e][:].rearrange("p (t j) -> p j t", t=4), in1=a,
                                    op=ALU.mult).then_inc(g_read, 1)

                oT4 = r_outT[:].rearrange("p w (c b t) -> p w c b t", b=GB, t=4)
                def first_rows(i, e):
                    for t in range(4):
                        m = V.tensor_scalar(hot[:, e, 0, t, :], iota, oT4[:, 0, i, e, t:t + 1], oT4[:, 2, i, e, t:t + 1],
                                            ALU.is_equal, ALU.mult)
                    m.then_inc(hot_ready, 1)

                with dve.Fori(0, S // 4 // GB) as i:
                    for e in range(GB):
                        first_rows(i, e)
                        if e >= GB // 2:
                            weigh(i, e - GB // 2)
                    for e in range(GB // 2, GB):
                        weigh(i, e)
                if l == 0:
                    dve.drain()
                    for lo, hi, cc in ((0, 3, 0), (3, 12, KD)):
                        with dve.Fori(lo, hi) as i:
                            for b in range(2):
                                ada_part(acc[:, b], 48 + 8 * b, cc, True, i, 16)
                                ada_part(acc[:, b], 52 + 8 * b, cc, False, i, 16)
                            for b in range(2):
                                dve.wait_ge(ada_sum, i * 2 + (6 + b + 1))
                                ada_take(i * 2 + (6 + b), ps[b])

            V.memset(eps, EPS)
            V.memset(small[:, 4:5], 0.0).then_inc(neg_ready, 2)
            V.memset(small[:, 5:6], 0.0).then_inc(ffn_h, 2)
            V.memset(small[:, 6:7], 0.0).then_inc(gelu_ready, 2)
            V.memset(small[:, 7:8], 0.0).then_inc(g_read, GB)
            for semaphore in (conv_c, conv_u, hn_std, o_read):
                dve.sem_inc(semaphore, 1)
            dve.sem_inc(g_ready, GB)
            V.memset(small[:, 24:25], 0.0).then_inc(setup_done, 1)
            dve.wait_ge(params_in, 48)
            h0 = TAB["hot"][0]
            V.tensor_scalar(tabs[0:32, h0:h0 + 512], tabs[0:32, h0:h0 + 512], -1.0, None, ALU.mult).then_inc(tab_ready, 1)
            dve.wait_ge(tab_read, 1)
            for a, name in enumerate(("mask", "mask2")):
                m0 = TAB[name][0]
                m = V.tensor_tensor(out=erow[0:16, a, :], in0=ps[2 + a][0:16, :], in1=tabs[0:16, m0:m0 + 512], op=ALU.add)
            m.then_inc(tab_ready, 1)
            dve.wait_ge(c_ready, 1)
            for v in range(2):
                ada_part(acc[:, v], 8 * v, 0, True)
                ada_part(acc[:, v], 8 * v + 4, 0, False)
            for v in range(2):
                dve.wait_ge(ada_sum, v + 1)
                ada_take(v, ps[4 + v])
            dve.drain()
            for ph in phases:
                vec = vec_of(ph)
                if norm_no[ph] < 4:
                    gain = pc("norm", KD * norm_no[ph], KD)
                else:
                    gain = pc("pre", KD * ((norm_no[ph] - 4) // 2), KD)
                norm_in(ph, vec, gain)
                u = start[ph]
                if ph == "mix0":
                    mix0(u)
                elif ph == "mix1":
                    mix1(u)
                elif ph.startswith("peer"):
                    peer(int(ph[-1]), u)
                elif ph.startswith("ffn"):
                    ffn(int(ph[-1]), u)
                else:
                    hyb(ph, int(ph[-1]), u)
                if norm_no[ph] < 4:
                    add_plain(ph, vec)
                else:
                    add_normed(ph, vec, pc("post", KD * ((norm_no[ph] - 4) // 2), KD), 1.0 if ph.startswith("hyb") else 0.5)

        @block.gpsimd
        def _(pool):
            G = nc.gpsimd

            def bias(e, f, head):
                src = bias_rows[head, 127:127 + P * 511].rearrange("(p w) -> p w", w=511)[:, 0:TW]
                pool.dma_start(nb[:, e, f, :], src).then_inc(bias_in[e], 16)

            def mix0():
                pool.wait_ge(cum_ready, 1)
                pool.dma_start(cumrow[0:1, :, :], cum[0:8, :]).then_inc(cum_row, 16)

            def mix1():
                for a in range(2):
                    pool.wait_ge(kv_raw, 2 * a + 2)
                    for c in range(2):
                        src = kcv[:, 2 * a + c, :]
                        toks = bass.AP(src.tensor, src.offset, [list(src.ap[0]), [1, CMP_LEN], [16, NCMP]])
                        G.tensor_tensor(out=blk[:, a, :, c, :], in0=toks,
                                        in1=pc("pos", a * CMP_LEN, CMP_LEN).unsqueeze(2).to_broadcast([P, CMP_LEN, NCMP]),
                                        op=ALU.add).then_inc(blk_ready, 1)
                pool.wait_ge(hn_out, hn0["mix1"] + 13)
                with pool.Fori(0, 4) as i:
                    for half in range(2):
                        pool.wait_ge(o_read, i * 2 + (half + pair0["mix1"] - 1))
                        for f in range(2):
                            bias(half, f, i + (8 * half + 4 * f))
                        G.tensor_copy(qs[:, half, :], qs_all[:, i * 2 + half, :]).then_inc(q_staged, 1)

            def hyb(ph, l):
                pool.wait_ge(x_ready, KD * phases.index(ph))
                if l == 0:
                    pool.dma_start(vr[0:1, :, :, :], vrow).then_inc(cum_row, 16)
                with pool.Fori(0, 4) as i:
                    for e in range(2):
                        pool.wait_ge(o_read, i * 2 + (e + pair0[ph] - 1))
                        for f in range(2):
                            bias(e, f, i + (16 + 4 * f) if e == 0 else i * 2 + (24 + f))

            pool.wait_ge(tab_ready, 2)
            pool.wait_ge(h_ready, 1)
            for a in range(2):
                pool.dma_start(bias_rows[16 * a:16 * a + 16].rearrange("h (p n) -> h p n", p=P),
                               erow[0:16, a, :].unsqueeze(1).to_broadcast([16, P, 512])).then_inc(bias_written, 16)
            pool.wait_ge(bias_written, 32)
            for ph in phases:
                if ph == "mix0":
                    mix0()
                elif ph == "mix1":
                    mix1()
                elif ph.startswith("hyb"):
                    hyb(ph, int(ph[-1]))


def vec_of(ph):
    return 3 * PHASES.index(ph)


norm_no_h = {ph: i for i, ph in enumerate(PHASES)}


def column_units(w):
    n = w.shape[1] // P
    return np.ascontiguousarray(w.reshape(KD, P, n, P).transpose(2, 1, 0, 3)).reshape(n, P, UNIT)


def padded(w):
    out = np.zeros((w.shape[0], P), w.dtype)
    out[:, :w.shape[1]] = w
    return out


def columns(v):
    return np.ascontiguousarray(v.reshape(-1, P).T)


def twice(v):
    return np.concatenate([v, v]).reshape(P, 1)


def block_diagonal(w):
    out = np.zeros(w.shape[:-2] + (P, P), w.dtype)
    out[..., :HD, :HD] = w
    out[..., HD:, HD:] = w
    return out


def head_columns(w, heads):
    return np.concatenate([w[:, h * HD:(h + 1) * HD] for h in heads], axis=1)


def head_rows(w, heads):
    return np.concatenate([w[h * HD:(h + 1) * HD] for h in heads], axis=0)


NSA_ORDER = [(2 * half + f) * 4 + j for j in range(4) for half in range(2) for f in range(2)]
SWA_ORDER = [4 * f + j for j in range(4) for f in range(2)]


def weight_stream(a):
    out = []
    w = a["even_w_in"][0]
    cb, cc, ch, q, k, v, f = (column_units(x) if x.shape[1] > 8 else column_units(padded(x))
                              for x in np.split(w, [512, 1024, 1536, 2048, 2560, 3072], axis=1))
    out += [f, np.stack([q, k, v, cc, ch, cb], axis=1).reshape(24, P, UNIT), column_units(a["even_w_out"][0])]

    def experts(l):
        u = a["peer_u"][l].reshape(NE, NE, KD, P).transpose(1, 3, 2, 0).reshape(NE, P, UNIT)
        v = a["peer_v"][l].reshape(NE, NE, D).transpose(1, 0, 2)
        return [column_units(a["peer_w_q"][l]), u, v]

    out += experts(0)
    q, kc, vc, ks, vs, kw, vw, gl = np.split(a["odd_w_in"][0], [1024 + 256 * i for i in range(7)], axis=1)
    w1 = block_diagonal(a["odd_cmp_w1"][0].reshape(2, CMP_LEN, HD, HD))
    w1 = w1.reshape(2, 4, 8, P, P).transpose(0, 1, 3, 2, 4).reshape(8, P, UNIT)
    out += [column_units(x) for x in (kc, vc, ks, kw, vs, vw)]
    out += [w1, column_units(padded(gl)), column_units(head_columns(q, NSA_ORDER)),
            column_units(head_rows(a["odd_w_out"][0], NSA_ORDER))]
    out += experts(1)

    def ffn(l, n):
        g, u = column_units(a["ffn_w_gate_2"][l, n]), column_units(a["ffn_w_up_2"][l, n])
        return [np.stack([g, u], axis=1).reshape(2 * NF, P, UNIT), a["ffn_w_down_2"][l, n].reshape(NF, P, D)]

    for l in range(2):
        out += ffn(l, 0)
        qa, ka, va, qb, kb, vb = np.split(a["mix_w_in_2"][l], [512, 640, 768, 1280, 1792], axis=1)
        qa, qb, kb, vb = (column_units(x) for x in (head_columns(qa, SWA_ORDER), qb, kb, vb))
        out += [column_units(ka), column_units(va), qa[:1]]
        out += [np.concatenate([np.stack([qb[i], kb[i], vb[i]]), qa[i + 1:i + 2]]) for i in range(4)]
        wo = a["mix_w_out_2"][l]
        out += [column_units(np.concatenate([head_rows(wo[:512], SWA_ORDER), wo[512:]], axis=0))]
        out += ffn(l, 1)
    return np.concatenate(out, axis=0)


def buckets(dist):
    n = np.maximum(dist, 0)
    nf = np.maximum(n, 1).astype(np.float32)
    large = 16 + (np.log(nf / np.float32(16)) / np.float32(math.log(128 / 16)) * np.float32(16)).astype(np.int32)
    return np.where(n < 16, n, np.minimum(large, 31))


def bias_constants():
    dist = 255 - np.arange(512)
    hot = ((buckets(dist)[None] == np.arange(32)[:, None]) & (dist >= 0)[None]).astype(np.float32)
    causal = np.where(dist >= 0, 0.0, BIG).astype(np.float32)
    window = np.where((dist >= 0) & (dist < 128), 0.0, BIG).astype(np.float32)
    mask = np.broadcast_to(causal, (16, 512))
    mask2 = np.concatenate([np.broadcast_to(window, (8, 512)), np.broadcast_to(causal, (8, 512))])
    return hot, mask, mask2


def packed_params(a):
    f = np.float32
    t = np.arange(P)
    cmask = np.concatenate([np.where(t[None] > t[:, None], BIG, 0.0),
                            np.where(np.arange(S)[None] > P + t[:, None], BIG, 0.0)], axis=1).astype(f)
    adab = np.concatenate([columns(a["ada_b"].reshape(-1)), columns(a["ada_b_2"].reshape(-1))], axis=1)
    mixb = []
    gain = []
    for l in range(2):
        b = a["mix_b_in_2"][l]
        mixb += [columns(head_rows(b[:512].reshape(-1, 1), SWA_ORDER).reshape(-1)), columns(b[512:640]),
                 columns(b[768:1280]), columns(b[1280:1792])]
        g = a["group_gain_2"][l]
        gain += [columns(head_rows(g[:512].reshape(-1, 1), SWA_ORDER).reshape(-1)), columns(g[512:])]
    sinks = np.concatenate([a["attn_sinks_2"][l][SWA_ORDER] for l in range(2)])
    bf = np.zeros((P, 1), f)
    bf[:8, 0] = a["even_b_f"][0]
    parts = {
        "ident": np.eye(P, dtype=f), "ones": np.ones((P, P), f), "bd": block_diagonal(np.ones((HD, HD), f)),
        "iota": np.broadcast_to(t.astype(f), (P, P)), "cmask": cmask,
        "rowmask": (t >= CMP_LEN - 1).astype(f).reshape(P, 1), "adab": adab,
        "c": np.concatenate([columns(a["c"][0]), columns(a["c_2"][0])], axis=1),
        "norm": columns(a["norm_g"].reshape(-1)), "pre": columns(a["norm_pre_2"].reshape(-1)),
        "post": columns(a["norm_post_2"].reshape(-1)),
        "convw": a["even_conv_w"][0].reshape(3, 4, P).transpose(2, 1, 0).reshape(P, 12), "bf": bf,
        "fqg": twice(a["even_q_g"][0]), "fkg": twice(a["even_k_g"][0]), "nqg": twice(a["odd_q_g"][0]),
        "nkg": np.concatenate([twice(a["odd_k_g"][0, i]) for i in range(3)], axis=1),
        "pos": np.concatenate([np.concatenate([a["odd_cmp_pos"][0, i].T] * 2) for i in range(2)], axis=1),
        "w2": np.concatenate([block_diagonal(a["odd_cmp_w2"][0, i]) for i in range(2)], axis=1),
        "keys": np.concatenate([a["peer_keys"][l].transpose(0, 2, 1).reshape(P, NE) for l in range(2)], axis=1),
        "bgate": np.broadcast_to(a["odd_b_gate"][0], (P, 48)), "mixb": np.concatenate(mixb, axis=1),
        "gain": np.concatenate(gain, axis=1), "sinks": np.broadcast_to(sinks, (P, 16)),
    }
    return np.ascontiguousarray(np.concatenate([parts[n] for n, _ in _COLS], axis=1))


def packed_tables(a):
    hot, mask, mask2 = bias_constants()
    out = np.zeros((32, NTAB), np.float32)
    for name, v in (("rel", a["rel_table"]), ("rel2", a["rel_bias_2"]), ("hot", hot), ("mask", mask), ("mask2", mask2)):
        c, w = TAB[name]
        out[:v.shape[0], c:c + w] = v
    return out


def packed_ada(a):
    def cut(w):
        l, _, n = w.shape
        return w.reshape(l, KD, P, n // UNIT, UNIT).transpose(0, 3, 1, 2, 4).reshape(-1, P, UNIT)
    return np.concatenate([cut(a["ada_w"]), cut(a["ada_w_2"])], axis=0)


def layout(a):
    b = a["mix_b_in_2"]
    vrow = np.stack([np.concatenate([b[l, 640:768], b[l, 1792:2304]]) for l in range(2)]).reshape(1, 2, 5, P)
    return {
        "xT": np.ascontiguousarray(a["x"][0].T.reshape(KD, P, S).transpose(1, 0, 2)),
        "par": packed_params(a), "tab": packed_tables(a), "vrow": np.ascontiguousarray(vrow),
        "ada": packed_ada(a), "stream": weight_stream(a),
    }


def build(nc, arrays, upto=None):
    args = [nc.dram_tensor(n, v.shape, F32, kind="ExternalInput").ap() for n, v in arrays.items()]
    out = nc.dram_tensor("outT", (P, KD, S), F32, kind="ExternalOutput").ap()
    program(nc, *args, out, upto=upto)


def kernel(**inputs):
    import concourse.bacc as bacc
    from concourse.bass_utils import run_bass_kernel_spmd

    arrays = layout({k: np.asarray(v) for k, v in inputs.items()})
    nc = bacc.Bacc("TRN2", target_bir_lowering=False, num_devices=1)
    build(nc, arrays)
    got = run_bass_kernel_spmd(nc, [arrays], core_ids=[0]).results[0]["outT"]
    return np.ascontiguousarray(got.transpose(1, 0, 2).reshape(D, S).T).reshape(1, S, D)
```

```python
import math
from contextlib import ExitStack

import numpy as np

import concourse.bass as bass
from concourse import mybir

F32 = mybir.dt.float32
F32R = mybir.dt.float32r
U32 = mybir.dt.uint32
ALU = mybir.AluOpType
ACT = mybir.ActivationFunctionType
AX = mybir.AxisListType

P = 128
S = 256
TT = S // P
D = 1024
KD = D // P
HD = 64
SCALE = HD ** -0.5
EPS = 1e-6
BIG = 1e30
FMAX = 3.0e38
UNIT = 1024
SLOTS = 4
FF = 2816
NF = FF // P
NE = 128
PH = 8
TOPK = 16
NCMP = 15
CMP_LEN = 32
GB = 4
NPLAIN = 40
EARLY = 6 * KD
NVEC = 30
TW = 384

_COLS = [("ident", P), ("ones", P), ("bd", P), ("iota", P), ("cmask", TW), ("rowmask", 1),
         ("adab", NVEC * KD), ("c", 2 * KD), ("norm", 4 * KD), ("pre", 6 * KD), ("post", 6 * KD),
         ("convw", 12), ("bf", 1), ("fqg", 1), ("fkg", 1), ("nqg", 1), ("nkg", 3),
         ("pos", 2 * CMP_LEN), ("w2", 2 * P), ("keys", 2 * NE), ("bgate", 48),
         ("mixb", 2 * 13), ("gain", 2 * KD), ("sinks", 2 * 8)]
COL = {}
_at = 0
for _n, _w in _COLS:
    COL[_n] = (_at, _w)
    _at += _w
NPAR = _at
TAB = {"rel": (0, 16), "rel2": (16, 16), "hot": (32, 512), "mask": (544, 512), "mask2": (1056, 512)}
NTAB = 1568

MIX0_UNITS = 1 + 24 + 8
MIX1_UNITS = 12 + 8 + 1 + 8 + 8
PEER_UNITS = 8 + 2 * NE
FFN_UNITS = 3 * NF
HYB_UNITS = 2 + 16 + 8
PHASES = ["mix0", "peer0", "mix1", "peer1", "ffn0", "hyb0", "ffn1", "ffn2", "hyb1", "ffn3"]
_SIZE = {"mix0": MIX0_UNITS, "mix1": MIX1_UNITS, "peer": PEER_UNITS, "ffn": FFN_UNITS, "hyb": HYB_UNITS}


def phase_units(name):
    return _SIZE[name] if name in _SIZE else _SIZE[name[:-1]]


def program(nc, xT, par, tab, vrow, ada, stream, outT, upto=None):
    phases = PHASES[:upto]
    start = {}
    units = 0
    for ph in phases:
        start[ph] = units
        units += phase_units(ph)
    att0 = {"mix0": 0, "mix1": 8, "hyb0": 8 + 48, "hyb1": 8 + 48 + 16}
    pair0 = {"mix0": 1, "mix1": 5, "hyb0": 13, "hyb1": 21}
    bias0 = {"mix1": 0, "hyb0": 4, "hyb1": 8}
    hn0 = {"mix0": 0, "mix1": 8}
    split0, nsplit = {}, 0
    for ph in PHASES:
        split0[ph] = nsplit
        nsplit += 2 * NE - NPLAIN if ph.startswith("peer") else 3 * NF if ph.startswith("ffn") else 0
    split_no = {ph: i for i, ph in enumerate(p for p in PHASES if p[:3] in ("pee", "ffn"))}
    norm_no = {"mix0": 0, "peer0": 1, "mix1": 2, "peer1": 3}
    k = 4
    for ph in PHASES[4:]:
        norm_no[ph] = k
        k += 2

    with ExitStack() as ctx:
        place = {}

        def sb(name, shape, dt=F32):
            place[name] = -(-nc.sbuf_base // 32) * 32
            return ctx.enter_context(nc.sbuf_tensor(name, shape, dt))

        def over(name, other, shape, at=0):
            return nc.alloc_sbuf_tensor_at(name, shape, F32R, offset=place[other] + 4 * at)

        def sem(name):
            return ctx.enter_context(nc.semaphore(name))

        bias_rows = nc.dram_tensor("bias_rows", (32, P * 512), F32).ap()

        ps = [ctx.enter_context(nc.psum_tensor(f"ps{i}", [P, 512], F32)) for i in range(8)]
        x = sb("x", [P, KD, S])
        hT = sb("hT", [P, KD, S])
        ring = sb("ring", [P, SLOTS, UNIT])
        mods = sb("mods", [P, NVEC, KD])
        prm = sb("prm", [P, NPAR])
        stat = sb("stat", [P, 2, S])
        acol = sb("acol", [P, KD])
        small = sb("small", [P, 64])
        arena = sb("arena", [P, NE, S])
        score = sb("score", [P, TT, 16, NE])
        eq = sb("eq", [P, NE, TOPK])
        pick = sb("pick", [P, 7, NE])

        flat = arena[:].rearrange("p a b -> p (a b)")
        used = [0]

        def cut(n, shape=None):
            a = used[0]
            used[0] += n
            assert used[0] <= NE * S
            return flat[:, a:a + n]

        def pc(name, i=0, n=None):
            a, w = COL[name]
            return prm[:, a + i:a + i + (w - i if n is None else n)]

        ident, ones, bd, iota = pc("ident"), pc("ones"), pc("bd"), pc("iota")
        eps = small[:, 0:1]

        sq = cut(KD * S).rearrange("p (a b) -> p a b", a=KD)
        vr = cut(1280).rearrange("p (l a b) -> p l a b", l=2, a=5)
        sum_at = used[0]
        oT = cut(KD * S).rearrange("p (a b) -> p a b", a=KD)
        qs = cut(2 * S).rearrange("p (a b) -> p a b", a=2)
        qs_all = cut(8 * S).rearrange("p (a b) -> p a b", a=8)
        ks = cut(6 * S).rearrange("p (a b) -> p a b", b=S)
        v_sb = cut(4 * TT * 2 * P).rearrange("p (a b) -> p a b", b=P)
        neg = cut(2 * TW).rearrange("p (a b) -> p a b", a=2)
        prob = cut(2 * TW).rearrange("p (a b) -> p a b", a=2)
        pt = cut(2 * TW).rearrange("p (a b) -> p a b", a=2)
        nb = cut(4 * TW).rearrange("p (e a b) -> p e a b", e=2, a=2)
        hsq = cut(S)
        hstd = cut(2 * S).rearrange("p (a b) -> p a b", a=2)
        hrec = cut(S)
        ccs = cut(S)
        u_pad = cut(S + 2)
        conv_t = cut(2 * S).rearrange("p (a b) -> p a b", a=2)
        cum = cut(S)
        ftmp = cut(4 * S).rearrange("p (a b) -> p a b", a=4)
        cumrow = cut(8 * S).rearrange("p (a b) -> p a b", a=8)
        gates = cut(TT * 48).rearrange("p (a b) -> p a b", a=TT)
        gsum = cut(TT * 48).rearrange("p (a b) -> p a b", a=TT)
        blk = cut(2 * CMP_LEN * 2 * NCMP).rearrange("p (a l c n) -> p a l c n", a=2, l=CMP_LEN, c=2)
        kcv = cut(4 * S).rearrange("p (a b) -> p a b", a=4)
        chid = cut(2 * 32).rearrange("p (a b) -> p a b", a=2)
        kc_sb = cut(32)
        vc_sb = cut(2 * P).rearrange("p (a b) -> p a b", a=2)
        negm = cut(4).rearrange("p (a b) -> p a b", a=2)
        rows = cut(4).rearrange("p (a b) -> p a b", a=2)
        sink_e = cut(4).rearrange("p (a b) -> p a b", a=2)
        rinv = cut(4).rearrange("p (a b) -> p a b", a=2)
        coef = cut(4).rearrange("p (a b) -> p a b", a=2)
        nsk = cut(2)
        ffn_at = used[0]
        hid = cut(2 * S).rearrange("p (a b) -> p a b", a=2)
        sl = cut(2 * S).rearrange("p (a b) -> p a b", a=2)
        gtmp = cut(KD * S).rearrange("p (a b) -> p a b", a=KD)
        end_at = used[0]
        used[0] = ffn_at
        tabs = cut(NTAB)
        erow = cut(2 * 512).rearrange("p (a n) -> p a n", a=2)
        acc4 = cut(4 * UNIT).rearrange("p (a n) -> p a n", a=4)
        adaw = score[:].rearrange("p a g n -> p (a g n)").rearrange("p (a n) -> p a n", a=SLOTS)
        acc = hT[:].rearrange("p a b -> p (a b)").rearrange("p (a n) -> p a n", a=2)
        assert end_at <= NE * S
        used[0] = sum_at
        hparts = over("hidden_parts", "arena", [P, 2, NF, S], sum_at)
        cut(2 * NF * S)
        assert used[0] <= ffn_at
        cact = small[:, 40:56]
        r_sv = pick[:, 0:2, :].rearrange("p a b -> p (a b)").rearrange("p (g k) -> p g k", g=16)
        r_si = sb("r_si", [P, 16, TOPK], U32)
        r_sif = pick[:, 2:4, :].rearrange("p a b -> p (a b)").rearrange("p (g k) -> p g k", g=16)
        r_cv = pick[:, 4, :].rearrange("p (g k) -> p g k", g=PH)
        r_ci = sb("r_ci", [P, PH, TOPK], U32)
        r_ab = sb("r_ab", [P, 2, NE], U32)
        r_abf = pick[:, 5:7, :]
        r_out = sb("r_out", [P, TT, 3, NE])
        r_outT = sb("r_outT", [P, 3, S])
        r_sum = small[:, 8:16]
        r_rec = small[:, 16:24]
        hot = score[:].rearrange("p a g n -> p (a g n)").rearrange(
            "p (b w t n) -> p b w t n", b=GB, w=2, t=4)
        whi = over("unit_high", "eq", [P, 2, UNIT])
        wlo = over("unit_low", "ring", [P, SLOTS, UNIT])
        xparts = over("norm_parts", "score", [P, 2, KD, S])
        ahi = over("expert_high", "pick", [P, 2, S])
        alo = over("expert_low", "r_out", [P, 2, S])
        ysb = flat[:, NE * S - TT * D:].rearrange("p (t n) -> p t n", t=TT)
        pq = eq[:].rearrange("p a b -> p (a b)")[:, 0:2 * S].rearrange("p (a b) -> p a b", a=2)

        passed = sem("passed")
        params_in = sem("params_in")
        loaded = [sem(f"unit_loaded{s}") for s in range(SLOTS)]
        unit_done = sem("unit_done")
        setup_done = sem("setup_done")
        c_ready = sem("c_ready")
        tab_ready = sem("tab_ready")
        tab_read = sem("tab_read")
        bias_written = sem("bias_written")
        ada_loaded = [sem(f"ada_loaded{s}") for s in range(SLOTS)]
        ada_late = [sem(f"ada_late{s}") for s in range(SLOTS)]
        ada_used = sem("ada_used")
        ada_acc = sem("ada_acc")
        ada_sum = sem("ada_sum")
        ada_read = sem("ada_read")
        x_ready = sem("x_ready")
        sq_ready = sem("sq_ready")
        ss_ready = sem("ss_ready")
        std_ready = sem("std_ready")
        mid_ready = sem("mid_ready")
        h_ready = sem("h_ready")
        y_ready = sem("y_ready")
        silu_ready = sem("silu_ready")
        ffn_h = sem("ffn_h")
        hn_sq = sem("hn_sq")
        hn_ss = sem("hn_ss")
        hn_std = sem("hn_std")
        hn_out = sem("hn_out")
        logf_ready = sem("logf_ready")
        logf_act = sem("logf_act")
        cum_ready = sem("cum_ready")
        cum_row = sem("cum_row")
        conv_c = sem("conv_c")
        conv_u = sem("conv_u")
        conv_out = sem("conv_out")
        v_ready = sem("v_ready")
        q_ready = sem("q_ready")
        s_ready = sem("s_ready")
        neg_ready = sem("neg_ready")
        exp_ready = sem("exp_ready")
        q_staged = sem("q_staged")
        pn_ready = sem("pn_ready")
        t_ready = sem("t_ready")
        pt_ready = sem("pt_ready")
        o_done = sem("o_done")
        o_read = sem("o_read")
        bias_in = [sem(f"bias_in{e}") for e in range(2)]
        kv_out = sem("kv_out")
        kv_raw = sem("kv_raw")
        blk_ready = sem("blk_ready")
        cmp_h = sem("cmp_h")
        cmp_mm = sem("cmp_mm")
        cmp_vc = sem("cmp_vc")
        gate_z = sem("gate_z")
        gate_s = sem("gate_s")
        gate_ready = sem("gate_ready")
        on_ready = sem("on_ready")
        pq_ready = sem("pq_ready")
        ps_ready = sem("ps_ready")
        ps_read = sem("ps_read")
        gelu_ready = sem("gelu_ready")
        rexp_in = sem("rexp_in")
        rexp_out = sem("rexp_out")
        route_ready = sem("route_ready")
        routeT_ready = sem("routeT_ready")
        routeT_read = sem("routeT_read")
        hot_ready = sem("hot_ready")
        hot2_ready = sem("hot2_ready")
        g_ready = sem("g_ready")
        g_read = sem("g_read")
        out_done = sem("out_done")
        xhi_ready = sem("xhi_ready")
        xlo_ready = sem("xlo_ready")
        whi_ready = sem("whi_ready")
        wlo_ready = sem("wlo_ready")
        ahi_ready = sem("ahi_ready")
        alo_ready = sem("alo_ready")
        hhi_ready = sem("hhi_ready")
        hlo_ready = sem("hlo_ready")
        y_act = sem("y_act")
        y_dve = sem("y_dve")
        y_turned = sem("y_turned")

        def slot_of(unit):
            return ring[:, unit % SLOTS, :].rearrange("p (k n) -> p k n", k=KD)

        def wait_unit(pe, unit, it=0, per=0):
            pe.wait_ge(loaded[unit % SLOTS], it * (per // SLOTS * 16) + 16 * (unit // SLOTS + 1))

        def parts_of(unit, n):
            return whi[:, n % 2, :], wlo[:, unit % SLOTS, :]

        def wait_used(eng, unit, it=0, per=0):
            eng.wait_ge(unit_done, it * per + unit + 1)

        def wait_alone(eng, semaphore, value):
            eng.wait_ge(semaphore, value)
            eng.sem_inc(passed, 1)

        block = ctx.enter_context(nc.Block())

        @block.sync
        def _(sp):
            sp.dma_start(prm[:], par).then_inc(params_in, 16)
            sp.dma_start(tabs[0:32, :], tab).then_inc(params_in, 16)
            sp.dma_start(x[:], xT).then_inc(params_in, 16)
            for u in range(SLOTS):
                sp.dma_start(ring[:, u], stream[u]).then_inc(loaded[u], 16)
            rounds = units // SLOTS
            with sp.Fori(1, rounds) as i:
                for s in range(SLOTS):
                    sp.wait_ge(unit_done, i * SLOTS + (s - SLOTS + 1))
                    sp.dma_start(ring[:, s], stream[i * SLOTS + s]).then_inc(loaded[s], 16)
            for u in range(rounds * SLOTS, units):
                sp.wait_ge(unit_done, u - SLOTS + 1)
                sp.dma_start(ring[:, u % SLOTS], stream[u]).then_inc(loaded[u % SLOTS], 16)
            sp.wait_ge(x_ready, KD * len(phases))
            sp.dma_start(outT, x[:]).then_inc(out_done, 16)
            sp.wait_ge(out_done, 16)

        @block.tensor
        def _(pe):
            def products(out, unit, rhs, it=0, per=0, m=P, h_from=None):
                w = slot_of(unit)
                wait_unit(pe, unit, it, per)
                for kt in range(KD):
                    if h_from is not None:
                        pe.wait_ge(h_ready, h_from + kt + 1)
                    mm = pe.matmul(out, w[:, kt, 0:m], rhs(kt), start=(kt == 0), stop=(kt == KD - 1))
                mm.then_inc(unit_done, 1)

            def products_split(out, unit, n, it=0, per=0):
                hi, lo = (w.rearrange("p (k n) -> p k n", k=KD) for w in parts_of(unit, n))
                pe.wait_ge(wlo_ready, it * per + (n + 1))
                for kt in range(KD):
                    pe.matmul(out, hi[:, kt, :], xparts[:, 0, kt, :], start=(kt == 0), stop=False)
                    pe.matmul(out, hi[:, kt, :], xparts[:, 1, kt, :], start=False, stop=False)
                    mm = pe.matmul(out, lo[:, kt, :], xparts[:, 0, kt, :], start=False, stop=(kt == KD - 1))
                mm.then_inc(unit_done, 1)

            def products_t(bank, unit, n=P, it=0, per=0, brow=None):
                w = slot_of(unit)
                wait_unit(pe, unit, it, per)
                for tt in range(TT):
                    out = bank[:, tt * n:(tt + 1) * n]
                    for kt in range(KD):
                        mm = pe.matmul(out, hT[:, kt, tt * P:(tt + 1) * P], w[:, kt, 0:n],
                                       start=(kt == 0), stop=(kt == KD - 1 and brow is None))
                    if brow is not None:
                        mm = pe.matmul(out, ones[0:1, :], brow, start=False, stop=True)
                mm.then_inc(unit_done, 1)

            def sum_squares(no):
                for kt in range(KD):
                    pe.wait_ge(sq_ready, 4 * no + kt // 2 + 1)
                    mm = pe.matmul(ps[0][:, 0:S], ones, sq[:, kt, :], start=(kt == 0), stop=(kt == KD - 1))
                mm.then_inc(ss_ready, 1)

            def head_norm(c, bank=ps[3]):
                pe.wait_ge(hn_sq, c + 1)
                pe.wait_ge(hn_std, c + 1)
                pe.matmul(bank[:, 0:S], bd, hsq, start=True, stop=True).then_inc(hn_ss, 1)

            def scores(g, k, inst):
                pe.wait_ge(neg_ready, g + k + 1)
                h = slice(inst["half"] * HD, inst["half"] * HD + HD)
                bank = ps[4 + k % 2]
                if inst["kind"] == "cmp":
                    for tt in range(TT):
                        mm = pe.matmul(bank[:, tt * NCMP:(tt + 1) * NCMP], inst["q"][h, tt * P:(tt + 1) * P],
                                       inst["k"][h, :], start=True, stop=True)
                else:
                    row = inst.get("row")
                    for tt in range(TT):
                        out = bank[:, 0:P] if tt == 0 else bank[:, P:TW]
                        n = P * (tt + 1)
                        mm = pe.matmul(out, inst["q"][h, tt * P:(tt + 1) * P], inst["k"][h, 0:n],
                                       start=True, stop=row is None)
                        if row is not None:
                            mm = pe.matmul(out, ones[0:1, :], row(n), start=False, stop=True)
                mm.then_inc(s_ready, 1)

            def attend(g, k, inst, ahead=None, before=()):
                bank = ps[6 + k % 2]
                pr, pT = prob[:, k % 2], pt[:, k % 2]
                pe.wait_ge(pn_ready, g + k + 1)
                if inst["kind"] == "cmp":
                    for tt in range(TT):
                        mm = pe.transpose(bank[0:NCMP, tt * P:(tt + 1) * P], pr[:, tt * NCMP:(tt + 1) * NCMP], ident)
                else:
                    for b in range(3):
                        mm = pe.transpose(bank[:, b * P:(b + 1) * P], pr[:, b * P:(b + 1) * P], ident)
                mm.then_inc(t_ready, 1)
                if ahead is not None:
                    scores(g, k + 2, ahead)
                pe.wait_ge(pt_ready, g + k + 1)
                for semaphore, value in before:
                    pe.wait_ge(semaphore, value)
                half = inst["half"]
                out = ps[inst.get("bank", 2) + half][half * HD:half * HD + HD, 0:S]
                begins, ends = inst["begins"], inst["ends"]
                if inst["kind"] == "cmp":
                    mm = pe.matmul(out, inst["v"], pT[0:NCMP, 0:S], start=begins, stop=ends)
                else:
                    pe.matmul(out, inst["v"][0], pT[:, 0:S], start=begins, stop=False)
                    mm = pe.matmul(out[:, P:S], inst["v"][1], pT[:, S:TW], start=False, stop=ends)
                if inst["last"]:
                    mm.then_inc(o_done, 1)

            def output(unit):
                for n in range(KD):
                    products(ps[4 + n // 2][:, (n % 2) * S:(n % 2 + 1) * S], unit + n, lambda kt: oT[:, kt, :])

            def column_sums(bank, sums):
                for n in range(KD):
                    mm = pe.matmul(bank[:, n:n + 1], sums[:, n * P:(n + 1) * P], ones[:, 0:1], start=True, stop=True)
                mm.then_inc(ada_sum, 1)

            def spread(unit, n, it, per, f, first, last):
                hi, lo = (w.rearrange("p (k n) -> p k n", k=KD) for w in parts_of(unit, n))
                pe.wait_ge(wlo_ready, it * per + (n + 1))
                for m in range(KD):
                    out = ps[4 + m // 2][:, (m % 2) * S:(m % 2 + 1) * S]
                    pe.matmul(out, hi[:, m, :], hparts[:, 0, f, :], start=first and m % 2 == 0, stop=False, skip_group_check=True)
                    pe.matmul(out, hi[:, m, :], hparts[:, 1, f, :], start=False, stop=False, skip_group_check=True)
                    mm = pe.matmul(out, lo[:, m, :], hparts[:, 0, f, :], start=False, stop=last, skip_group_check=True)
                mm.then_inc(unit_done, 1)

            def spread_t(unit, n, a, it, per, first, last):
                hi, lo = parts_of(unit, n)
                pe.wait_ge(wlo_ready, it * per + (n + 1))
                pe.wait_ge(alo_ready, it * per + (a + 1))
                for tt in range(TT):
                    toks = slice(tt * P, (tt + 1) * P)
                    for c, (act_part, w) in enumerate(((ahi, hi), (ahi, lo), (alo, hi))):
                        for b in range(2):
                            mm = pe.matmul(ps[4 + 2 * tt + b][:, :], act_part[:, a % 2, toks], w[:, b * 512:(b + 1) * 512],
                                           start=first and c == 0, stop=last and c == 2)
                mm.then_inc(unit_done, 1)

            def mix0(u):
                products(ps[0][0:8, 0:S], u, lambda kt: hT[:, kt, :], m=8, h_from=0)
                u += 1
                pe.wait_ge(logf_ready, 1)
                h = lambda kt: hT[:, kt, :]
                with pe.Fori(0, 2) as i:
                    for e in range(2):
                        v = u + 6 * e
                        r = i * 2 + e
                        pe.wait_ge(conv_c, r + 1)
                        products(ps[0][:, 0:S], v, h, i, 12)
                        pe.wait_ge(conv_u, r + 1)
                        products(ps[1][:, 0:S], v + 1, h, i, 12)
                        pe.wait_ge(o_read, r + pair0["mix0"])
                        head_norm(r * 2)
                        products_t(ps[2], v + 2, P, i, 12)
                        head_norm(r * 2 + 1)
                        pe.wait_ge(hn_out, r * 2 + 2)
                        if e == 0:
                            pe.wait_ge(cum_row, 16)
                        insts = [dict(half=f, kind="full", q=qs[:, 0], k=ks[:, 0], begins=True, ends=True, last=f == 1,
                                      v=[v_sb[:, b, f * HD:f * HD + HD] for b in range(2)],
                                      row=lambda n, hd=r * 2 + f: cumrow[0:1, hd, 0:n]) for f in range(2)]
                        scores(r * 2, 0, insts[0])
                        scores(r * 2, 1, insts[1])
                        products(ps[0][:, 0:S], v + 3, h, i, 12)
                        products(ps[1][:, 0:S], v + 4, h, i, 12)
                        pe.wait_ge(v_ready, r + 1)
                        products(ps[2][:, 0:S], v + 5, h, i, 12)
                        attend(r * 2, 0, insts[0], before=((conv_out, r + 1),))
                        attend(r * 2, 1, insts[1])
                u += 24
                pe.wait_ge(o_read, pair0["mix0"] + 4)
                output(u)
                pe.wait_ge(ada_acc, 6)
                for a in range(4):
                    column_sums(ps[a], acc4[:, a])

            def mix1(u):
                h = lambda kt: hT[:, kt, :]
                hn = hn0["mix1"]
                for n in range(4):
                    if n >= 2:
                        pe.wait_ge(kv_raw, n - 1)
                    products(ps[n % 2][:, 0:S], u + n, h, h_from=KD * norm_no_h["mix1"] if n == 0 else None)
                for n in range(4):
                    if n < 2:
                        pe.wait_ge(kv_raw, 3 + n)
                    else:
                        pe.wait_ge(hn_out, hn + n - 1)
                    products(ps[n % 2][:, 0:S], u + 4 + n, h)
                    if n:
                        head_norm(hn + n - 1)
                for n in range(4):
                    if n == 1:
                        head_norm(hn + 3)
                    if n < 2:
                        pe.wait_ge(hn_out, hn + 3 + n)
                    else:
                        pe.wait_ge(kv_out, n - 1)
                    products_t(ps[n % 2], u + 8 + n)
                pe.wait_ge(kv_out, 4)
                u += 12
                for a in range(2):
                    pe.wait_ge(blk_ready, 2 * (a + 1))
                    for q in range(4):
                        w = slot_of(u + 4 * a + q)
                        wait_unit(pe, u + 4 * a + q)
                        for l in range(8):
                            mm = pe.matmul(ps[a][:, 0:2 * NCMP], w[:, l, :], blk[:, a, q * 8 + l, :, :],
                                           start=(q == 0 and l == 0), stop=(q == 3 and l == 7))
                        mm.then_inc(unit_done, 1)
                u += 8
                products_t(ps[2], u, 48)
                u += 1
                pe.wait_ge(cmp_h, 1)
                pe.matmul(ps[0][:, 0:2 * NCMP], pc("w2", 0, P), chid[:, 0, 0:2 * NCMP],
                          start=True, stop=True).then_inc(cmp_mm, 1)
                pe.wait_ge(cmp_h, 2)
                for c in range(2):
                    mm = pe.matmul(ps[1][0:NCMP, c * P:(c + 1) * P], chid[:, 1, c * NCMP:(c + 1) * NCMP],
                                   pc("w2", P, P), start=True, stop=True)
                mm.then_inc(cmp_mm, 1)
                pe.wait_ge(hn_sq, hn + 5)
                pe.matmul(ps[3][:, 0:2 * NCMP], bd, hsq[:, 0:2 * NCMP], start=True, stop=True).then_inc(hn_ss, 1)
                pe.wait_ge(cmp_vc, 1)
                pe.wait_ge(hn_out, hn + 5)
                with pe.Fori(0, 2) as i:
                    for e in range(4):
                        pe.wait_ge(hn_out, i * 4 + (hn + 4 + e))
                        products(ps[e % 2][:, 0:S], u + e, h, i, 4)
                        if e:
                            head_norm(i * 4 + (hn + 4 + e))
                    head_norm(i * 4 + (hn + 8))
                u += 8
                pe.wait_ge(gate_ready, 1)
                with pe.Fori(0, 4) as i:
                    g, r = i * 12 + att0["mix1"], i * 2 + pair0["mix1"]
                    insts = [
                        dict(half=f, kind="cmp" if kind == 0 else "full", q=qs[:, half], bank=2 - 2 * half, pair=half,
                             k=kc_sb[:, half * NCMP:(half + 1) * NCMP] if kind == 0 else ks[:, 1 + 2 * (kind - 1) + half],
                             v=(vc_sb[0:NCMP, half, f * HD:f * HD + HD] if kind == 0 else
                                [v_sb[:, (4 * (kind - 1)) + 2 * half + b, f * HD:f * HD + HD] for b in range(2)]),
                             begins=kind == 0, ends=kind == 2, last=kind == 2 and f == 1)
                        for half in range(2) for kind in range(3) for f in range(2)]
                    pe.wait_ge(q_staged, i * 2 + 1)
                    scores(g, 0, insts[0])
                    scores(g, 1, insts[1])
                    for k, inst in enumerate(insts):
                        if k == 4:
                            pe.wait_ge(q_staged, i * 2 + 2)
                        attend(g, k, inst, insts[k + 2] if k < 10 else None,
                               before=((o_read, r + (inst["pair"] - 1)),) if inst["begins"] else ())
                pe.wait_ge(o_read, pair0["mix1"] + 8)
                output(u)

            def hyb(ph, l, u):
                h = lambda kt: hT[:, kt, :]
                products(ps[1][:, 0:S], u, h, h_from=KD * norm_no_h[ph])
                pe.wait_ge(cum_row, 32)
                products_t(ps[2], u + 1, brow=vr[0:1, l, 0, :])
                products(ps[0][:, 0:S], u + 2, h)
                u += 3
                pe.wait_ge(v_ready, 4 + 5 * l + 1)

                def pairs(i, more):
                    g, r = i * 4 + att0[ph], i * 2 + pair0[ph]
                    pe.wait_ge(q_ready, i * 3 + (13 * l + 2))
                    window = [dict(half=f, kind="full", q=qs[:, 0], k=ks[:, 1], begins=True, ends=True, last=f == 1,
                                   v=[v_sb[:, 2 + b, f * HD:f * HD + HD] for b in range(2)]) for f in range(2)]
                    scores(g, 0, window[0])
                    scores(g, 1, window[1])
                    products(ps[1][:, 0:S], u, h, i, 4)
                    products(ps[0][:, 0:S], u + 1, h, i, 4)
                    pe.wait_ge(q_ready, i * 3 + (13 * l + 3))
                    products_t(ps[1], u + 2, P, i, 4, brow=vr[0:1, l, i + 1, :])
                    attend(g, 0, window[0], before=((o_read, r),))
                    attend(g, 1, window[1])
                    pe.wait_ge(q_ready, i * 3 + (13 * l + 4))
                    pe.wait_ge(v_ready, i + (4 + 5 * l + 2))
                    g = g + 2
                    causal = [dict(half=f, kind="full", q=qs[:, 1], k=ks[:, 0], begins=True, ends=True, last=f == 1,
                                   v=[v_sb[:, b, f * HD:f * HD + HD] for b in range(2)]) for f in range(2)]
                    scores(g, 0, causal[0])
                    scores(g, 1, causal[1])
                    if more:
                        products(ps[0][:, 0:S], u + 3, h, i, 4)
                    attend(g, 0, causal[0], before=((o_read, r + 1),))
                    attend(g, 1, causal[1])

                with pe.Fori(0, 3) as i:
                    pairs(i, True)
                pairs(3, False)
                u += 15
                pe.wait_ge(o_read, pair0[ph] + 8)
                pe.wait_ge(on_ready, 6 * l + 2)
                for grp in range(2):
                    for kt in range(4):
                        mm = pe.matmul(ps[grp][:, 0:S], ones, sq[:, 4 * grp + kt, :], start=(kt == 0), stop=(kt == 3))
                mm.then_inc(on_ready, 1)
                pe.wait_ge(on_ready, 6 * l + 6)
                output(u)

            def ffn(ph, no, u):
                n = split0[ph]
                pe.wait_ge(xlo_ready, 4 * split_no[ph] + 4)
                with pe.Fori(0, NF // 2) as i:
                    for e in range(2):
                        pe.wait_ge(ffn_h, i * 2 + (NF * no + e + 1))
                        for w in range(2):
                            products_split(ps[2 * e + w][:, 0:S], u + 2 * e + w, n + 2 * e + w, i, 4)
                u, n = u + 2 * NF, n + 2 * NF
                for f in range(2):
                    pe.wait_ge(hlo_ready, NF * no + f + 1)
                    spread(u + f, n + f, 0, 0, f, f == 0, False)
                with pe.Fori(0, 4) as i:
                    for e in range(4):
                        pe.wait_ge(hlo_ready, i * 4 + (NF * no + e + 3))
                        spread(u + 2 + e, n + 2 + e, i, 4, i * 4 + (2 + e), False, False)
                for f in range(18, NF):
                    pe.wait_ge(hlo_ready, NF * no + f + 1)
                    spread(u + f, n + f, 0, 0, f, False, f == NF - 1)

            def peer(ph, l, u):
                h = lambda kt: hT[:, kt, :]
                keys = pc("keys", l * NE, NE)
                for hd in range(PH):
                    if hd >= 2:
                        pe.wait_ge(pq_ready, PH * l + hd - 1)
                    products(ps[hd % 2][:, 0:S], u + hd, h, h_from=KD * norm_no_h[ph] if hd == 0 else None)
                    pe.wait_ge(pq_ready, PH * l + hd + 1)
                    if hd >= 2:
                        pe.wait_ge(ps_read, PH * l + hd - 1)
                    for tt in range(TT):
                        for half in range(2):
                            rows_ = slice(half * HD, half * HD + HD)
                            mm = pe.matmul(ps[2 + 2 * (hd % 2) + half][:, tt * P:(tt + 1) * P],
                                           pq[rows_, hd % 2, tt * P:(tt + 1) * P], keys[rows_, :],
                                           start=True, stop=True)
                    mm.then_inc(ps_ready, 1)
                u += PH
                pe.wait_ge(ps_read, PH * (l + 1))
                with pe.Fori(0, NPLAIN // 4) as i:
                    for e in range(4):
                        pe.wait_ge(gelu_ready, i * 4 + (NE * l + e + 1))
                        products(ps[e % 2][:, 0:S], u + e, h, i, 4)
                n = split0[ph]
                pe.wait_ge(xlo_ready, 4 * split_no[ph] + 4)
                with pe.Fori(0, (NE - NPLAIN) // 4) as i:
                    for e in range(4):
                        pe.wait_ge(gelu_ready, i * 4 + (NE * l + NPLAIN + e + 1))
                        products_split(ps[e % 2][:, 0:S], u + NPLAIN + e, n + e, i, 4)
                u += NE
                n += NE - NPLAIN
                for tt in range(TT):
                    pe.wait_ge(route_ready, TT * l + tt + 1)
                    for w in range(3):
                        mm = pe.transpose(ps[2][:, w * P:(w + 1) * P] if tt == 0 else ps[3][:, w * P:(w + 1) * P],
                                          r_out[:, tt, w, :], ident)
                    mm.then_inc(routeT_ready, 1)
                pe.wait_ge(routeT_read, TT * (l + 1))
                pe.wait_ge(gelu_ready, NE * (l + 1) + 2)
                with pe.Fori(0, S // 4 // GB) as i:
                    for e in range(GB):
                        pe.wait_ge(hot_ready, i * GB + (S // 4 * l + e + 1))
                        pe.wait_ge(hot2_ready, i * GB + (S // 4 * l + e + 1))
                        pe.wait_ge(g_read, i * GB + (S // 4 * l + e + 1))
                        for t in range(4):
                            mm = pe.matmul(ps[e][:, t * NE:(t + 1) * NE], hot[:, e, 0, t, :], hot[:, e, 1, t, :],
                                           start=True, stop=True)
                        mm.then_inc(g_ready, 1)
                pe.wait_ge(g_read, S // 4 * (l + 1) + GB)
                a = NE * l

                def half(h, it=0):
                    for e in range(8):
                        k = 8 * h + e
                        spread_t(u + k, n + k, a + k, it, 16, isinstance(it, int) and k == 0, False)
                    pe.wait_ge(ada_acc, it * 2 + (6 + 12 * l + h + 1))
                    pe.wait_ge(ada_read, it * 2 + (6 + 12 * l + h - 1))
                    column_sums(ps[h % 2], acc[:, h % 2])

                half(0)
                with pe.Fori(0, 5) as i:
                    half(1, i)
                    half(2, i)
                half(11)
                with pe.Fori(0, 7) as i:
                    for e in range(4):
                        spread_t(u + 96 + e, n + 96 + e, a + 96 + e, i, 4, False, False)
                for k in range(NE - 4, NE):
                    spread_t(u + k, n + k, a + k, 0, 0, False, k == NE - 1)
                for b in range(2):
                    pe.wait_ge(y_act, 2 * l + b + 1)
                    pe.wait_ge(y_dve, 2 * l + b + 1)
                    for k in range(4 * b, 4 * b + 4):
                        for tt in range(TT):
                            c0 = (k % 2) * S + tt * P
                            mm = pe.transpose(ps[k // 2][:, c0:c0 + P], ysb[:, tt, k * P:(k + 1) * P], ident)
                        if k % 2:
                            mm.then_inc(y_turned, 1)

            pe.wait_ge(params_in, 48)
            pe.wait_ge(tab_ready, 1)
            for a, name in enumerate(("rel", "rel2")):
                c0, w = TAB[name]
                h0 = TAB["hot"][0]
                mm = pe.matmul(ps[2 + a][0:16, :], tabs[0:32, c0:c0 + w], tabs[0:32, h0:h0 + 512], start=True, stop=True)
            mm.then_inc(tab_read, 1)
            for ph in phases:
                sum_squares(norm_no[ph])
                if ph == "mix0":
                    for v in range(2):
                        pe.wait_ge(ada_acc, v + 1)
                        column_sums(ps[4 + v], acc[:, v])
                u = start[ph]
                if ph == "mix0":
                    mix0(u)
                elif ph == "mix1":
                    mix1(u)
                elif ph.startswith("peer"):
                    peer(ph, int(ph[-1]), u)
                elif ph.startswith("ffn"):
                    ffn(ph, int(ph[-1]), u)
                else:
                    hyb(ph, int(ph[-1]), u)
                if norm_no[ph] >= 4:
                    sum_squares(norm_no[ph] + 1)

        @block.scalar
        def _(act):
            def high(unit, n, it=0, per=0):
                hi, _ = parts_of(unit, n)
                wait_unit(act, unit, it, per)
                nc.scalar.copy(hi, ring[:, unit % SLOTS, :]).then_inc(whi_ready, 1)

            def norm_high(q):
                nc.scalar.copy(xparts[:, 0, 2 * q:2 * q + 2, :], hT[:, 2 * q:2 * q + 2, :]).then_inc(xhi_ready, 1)

            def norm_in(no, ph):
                i = phases.index(ph)
                for q in range(4):
                    if i:
                        act.wait_ge(x_ready, KD * (i - 1) + 2 * q + 2)
                    nc.scalar.activation(sq[:, 2 * q:2 * q + 2, :], x[:, 2 * q:2 * q + 2, :], ACT.Square).then_inc(sq_ready, 1)
                if ph.startswith("ffn"):
                    for k in range(2):
                        high(start[ph] + k, split0[ph] + k)
                act.wait_ge(ss_ready, no + 1)
                nc.scalar.activation(stat[:, 0], ps[0][:, 0:S], ACT.Sqrt, bias=eps, scale=1.0 / D).then_inc(std_ready, 1)

            def shift(ph, vec):
                n = norm_no_h[ph]
                for kt in range(KD):
                    act.wait_ge(mid_ready, KD * n + kt + 1)
                    nc.scalar.activation(hT[:, kt, :], hT[:, kt, :], ACT.Identity,
                                         bias=mods[:, vec, kt:kt + 1]).then_inc(h_ready, 1)
                    if ph.startswith("ffn") and kt % 2:
                        act.drain()
                        norm_high(kt // 2)

            def norm_out(no, unit_last):
                wait_used(act, unit_last)
                for q in range(4):
                    nc.scalar.activation(sq[:, 2 * q:2 * q + 2, :], ps[4 + q][:].rearrange("p (a b) -> p a b", a=2),
                                         ACT.Square).then_inc(sq_ready, 1)
                act.wait_ge(ss_ready, no + 1)
                nc.scalar.activation(stat[:, 0], ps[0][:, 0:S], ACT.Sqrt, bias=eps, scale=1.0 / D).then_inc(std_ready, 1)

            def head_norm(c, bank, n=S, b=0, sums=ps[3]):
                nc.scalar.activation(hsq[:, 0:n], bank[:, 0:n], ACT.Square).then_inc(hn_sq, 1)
                act.wait_ge(hn_ss, c + 1)
                nc.scalar.activation(hstd[:, b, 0:n], sums[:, 0:n], ACT.Sqrt, bias=eps, scale=1.0 / HD).then_inc(hn_std, 1)

            def exps(g, k, inst):
                act.wait_ge(neg_ready, g + k + 3)
                b = k % 2
                n = NCMP if inst["kind"] == "cmp" else None
                for tt in range(TT):
                    cols = slice(tt * NCMP, (tt + 1) * NCMP) if n else (slice(0, P) if tt == 0 else slice(P, TW))
                    a = nc.scalar.activation(prob[:, b, cols], neg[:, b, cols], ACT.Exp, bias=negm[:, b, tt:tt + 1],
                                             scale=-1.0, accum_out=rows[:, b, tt:tt + 1])
                    if inst.get("sink"):
                        a = nc.scalar.activation(sink_e[:, b, tt:tt + 1], nsk[:, inst["half"]:inst["half"] + 1],
                                                 ACT.Exp, bias=negm[:, b, tt:tt + 1], scale=-1.0)
                a.then_inc(exp_ready, 1)

            def turned(g, k, inst):
                act.wait_ge(t_ready, g + k + 1)
                if inst["kind"] == "cmp":
                    c = nc.scalar.copy(pt[0:NCMP, k % 2, 0:S], ps[6 + k % 2][0:NCMP, 0:S])
                else:
                    c = nc.scalar.copy(pt[:, k % 2, :], ps[6 + k % 2][:, 0:TW])
                c.then_inc(pt_ready, 1)

            def attention(g, insts):
                exps(g, 0, insts[0])
                exps(g, 1, insts[1])
                for k, inst in enumerate(insts):
                    turned(g, k, inst)
                    if k + 2 < len(insts):
                        exps(g, k + 2, insts[k + 2])

            def ada_load(n, it=0, per=0, count=4):
                for q in range(n, n + count):
                    if q >= SLOTS or per:
                        act.wait_ge(ada_used, it * per + (q - SLOTS + 1))
                    act.dma_start(adaw[:, q % SLOTS], ada[it * per + q] if per else ada[q]).then_inc(ada_loaded[q % SLOTS], 16)

            full = [dict(half=f, kind="full") for f in range(2)]

            def mix0(u):
                act.wait_ge(logf_ready, 1)
                nc.scalar.activation(ftmp[0:8, 2, :], ftmp[0:8, 1, :], ACT.Exp)
                act.drain()
                nc.scalar.activation(ftmp[0:8, 3, :], ftmp[0:8, 2, :], ACT.Ln, bias=1.0).then_inc(logf_act, 1)
                u += 1

                def pair(r, more):
                    wait_used(act, u, r, 6)
                    head_norm(r * 2, ps[0])
                    wait_used(act, u + 1, r, 6)
                    head_norm(r * 2 + 1, ps[1], b=1)
                    wait_used(act, u + 2, r, 6)
                    nc.scalar.copy(v_sb[:, 0:2, :], ps[2][:, 0:S].rearrange("p (a b) -> p a b", a=2)).then_inc(v_ready, 1)
                    exps(r * 2, 0, full[0])
                    exps(r * 2, 1, full[1])
                    ada_load(20, r, 8)
                    wait_used(act, u + 3, r, 6)
                    nc.scalar.copy(ccs, ps[0][:, 0:S]).then_inc(conv_c, 1)
                    turned(r * 2, 0, full[0])
                    turned(r * 2, 1, full[1])
                    if more:
                        ada_load(24, r, 8)

                with act.Fori(0, 3) as r:
                    pair(r, True)
                pair(3, False)

            def mix1(u):
                hn = hn0["mix1"]
                for n in range(4):
                    wait_used(act, u + n)
                    nc.scalar.copy(kcv[:, n, :], ps[n % 2][:, 0:S]).then_inc(kv_raw, 1)
                for n in range(4):
                    wait_used(act, u + 4 + n)
                    head_norm(hn + n, ps[n % 2], b=n % 2)
                for n in range(4):
                    wait_used(act, u + 8 + n)
                    nc.scalar.copy(v_sb[:, 2 * n:2 * n + 2, :],
                                   ps[n % 2][:, 0:S].rearrange("p (a b) -> p a b", a=2)).then_inc(kv_out, 1)
                u += 12
                for a in range(2):
                    wait_used(act, u + 4 * a + 3)
                    nc.scalar.activation(chid[:, a, 0:2 * NCMP], ps[a][:, 0:2 * NCMP], ACT.Gelu_apprx_tanh).then_inc(cmp_h, 1)
                u += 8
                act.wait_ge(cmp_mm, 1)
                head_norm(hn + 4, ps[0], 2 * NCMP)
                act.wait_ge(cmp_mm, 2)
                nc.scalar.copy(vc_sb[0:NCMP, :, :], ps[1][0:NCMP, 0:2 * P].rearrange("p (a b) -> p a b", a=2)).then_inc(cmp_vc, 1)
                act.wait_ge(gate_z, 1)
                nc.scalar.activation(gates, gsum, ACT.Sigmoid).then_inc(gate_s, 1)
                u += 1
                with act.Fori(0, 2) as i:
                    for e in range(4):
                        wait_used(act, u + e, i, 4)
                        head_norm(i * 4 + (hn + 5 + e), ps[e % 2], b=e % 2)
                insts = [dict(half=f, kind="cmp" if kind == 0 else "full")
                         for half in range(2) for kind in range(3) for f in range(2)]
                with act.Fori(0, 4) as i:
                    attention(i * 12 + att0["mix1"], insts)

            def hyb(ph, l, u):
                wait_used(act, u + 1)
                nc.scalar.copy(v_sb[:, 2:4, :], ps[2][:, 0:S].rearrange("p (a b) -> p a b", a=2)).then_inc(v_ready, 1)
                u += 3
                window = [dict(half=f, kind="full", sink=True) for f in range(2)]

                def pairs(i):
                    g = i * 4 + att0[ph]
                    exps(g, 0, window[0])
                    exps(g, 1, window[1])
                    wait_used(act, u + 2, i, 4)
                    nc.scalar.copy(v_sb[:, 0:2, :], ps[1][:, 0:S].rearrange("p (a b) -> p a b", a=2)).then_inc(v_ready, 1)
                    turned(g, 0, window[0])
                    turned(g, 1, window[1])
                    attention(g + 2, full)

                with act.Fori(0, 3) as i:
                    pairs(i)
                pairs(3)
                act.wait_ge(o_read, pair0[ph] + 8)
                for grp in range(2):
                    nc.scalar.activation(sq[:, 4 * grp:4 * grp + 4, :], oT[:, 4 * grp:4 * grp + 4, :], ACT.Square).then_inc(on_ready, 1)
                act.wait_ge(on_ready, 6 * l + 3)
                for grp in range(2):
                    a = nc.scalar.activation(conv_t[:, grp, :], ps[grp][:, 0:S], ACT.Sqrt, bias=eps, scale=1.0 / 512)
                a.then_inc(on_ready, 1)

            def ffn(ph, no, u):
                n = split0[ph]
                with act.Fori(0, NF // 2) as i:
                    for e in range(2):
                        g, k = u + 2 * e, n + 2 * e
                        wait_used(act, g, i, 4)
                        high(g + 2, k + 2, i, 4)
                        nc.scalar.activation(sl[:, e, :], ps[2 * e][:, 0:S], ACT.Silu).then_inc(silu_ready, 1)
                        wait_used(act, g + 1, i, 4)
                        high(g + 3, k + 3, i, 4)
                        act.wait_ge(ffn_h, i * 2 + (NF * no + e + 3))
                        nc.scalar.copy(hparts[:, 0, i * 2 + e, :], hid[:, e, :]).then_inc(hhi_ready, 1)
                u, n = u + 2 * NF, n + 2 * NF
                with act.Fori(0, 5) as i:
                    for e in range(4):
                        wait_used(act, u + e, i, 4)
                        high(u + e + 2, n + e + 2, i, 4)

            def peer(ph, l, u):
                for hd in range(PH):
                    wait_used(act, u + hd)
                    nc.scalar.copy(pq[:, hd % 2, :], ps[hd % 2][:, 0:S]).then_inc(pq_ready, 1)
                    act.wait_ge(ps_ready, PH * l + hd + 1)
                    for half in range(2):
                        c = nc.scalar.copy(score[:, :, 2 * hd + half, :],
                                           ps[2 + 2 * (hd % 2) + half][:, 0:S].rearrange("p (t n) -> p t n", t=TT))
                    c.then_inc(ps_read, 1)
                u += PH
                def plain(lo, hi):
                    with act.Fori(lo, hi) as i:
                        for e in range(4):
                            gelu(u + e, e, i)

                def gelu(unit, j, it=0):
                    wait_used(act, unit, it, 4)
                    nc.scalar.activation(arena[:, it * 4 + j, :], ps[j % 2][:, 0:S], ACT.Gelu_apprx_tanh).then_inc(gelu_ready, 1)

                for tt, (lo, hi) in enumerate(((0, 4), (4, 8))):
                    plain(lo, hi)
                    act.wait_ge(rexp_in, TT * l + tt + 1)
                    nc.scalar.activation(r_out[:, tt, 2, :], r_cv[:].rearrange("p g k -> p (g k)"), ACT.Exp).then_inc(rexp_out, 1)
                plain(8, NPLAIN // 4 - 1)
                act.wait_ge(route_ready, TT * (l + 1))
                for q in range(4):
                    norm_high(q)
                n = split0[ph]
                for k in range(4):
                    gelu(u + NPLAIN - 4 + k, NPLAIN - 4 + k)
                    if k >= 2:
                        high(u + NPLAIN + k - 2, n + k - 2)
                v = u + NPLAIN
                with act.Fori(0, (NE - NPLAIN) // 4 - 1) as i:
                    for e in range(4):
                        wait_used(act, v + e, i, 4)
                        high(v + e + 2, n + e + 2, i, 4)
                        gelu(v + e, NPLAIN + e, i)
                for k in range(NE - 4, NE):
                    wait_used(act, u + k)
                    high(u + k + 2, n + k - NPLAIN + 2)
                    gelu(u + k, k)
                u += NE
                n += NE - NPLAIN
                act.wait_ge(routeT_read, TT * (l + 1))
                oT4 = r_outT[:].rearrange("p w (c b t) -> p w c b t", b=GB, t=4)
                with act.Fori(0, S // 4 // GB) as i:
                    for c in range(0, GB, 2):
                        for e in range(c, c + 2):
                            act.wait_ge(g_ready, i * GB + (S // 4 * l + e + 1))
                            for t in range(4):
                                nc.scalar.activation(hot[:, e, 1, t, :], iota, ACT.Square, bias=oT4[:, 1, i, e, t:t + 1])
                        act.drain()
                        for e in range(c, c + 2):
                            nc.scalar.activation(hot[:, e, 1, :, :], hot[:, e, 1, :, :], ACT.Relu, bias=1.0,
                                                 scale=-1.0).then_inc(hot2_ready, 1)

                def activations_high(j, slot):
                    nc.scalar.copy(ahi[:, slot, :], arena[:, j, :]).then_inc(ahi_ready, 1)

                act.wait_ge(g_read, S // 4 * (l + 1) + GB)
                for k in range(2):
                    activations_high(k, k)
                with act.Fori(0, NE // 4 - 1) as i:
                    for e in range(4):
                        wait_used(act, u + e, i, 4)
                        high(u + e + 2, n + e + 2, i, 4)
                        activations_high(i * 4 + (e + 2), e % 2)
                for k in range(NE - 4, NE - 2):
                    wait_used(act, u + k)
                    high(u + k + 2, n + k + 2)
                    activations_high(k + 2, k % 2)
                wait_used(act, u + NE - 1)
                for b in range(2):
                    nc.scalar.copy(ysb[:, 0, b * 512:(b + 1) * 512], ps[4 + b][:]).then_inc(y_act, 1)

            act.wait_ge(params_in, 48)
            act.wait_ge(setup_done, 1)
            nc.scalar.activation(cact, pc("c"), ACT.Silu).then_inc(c_ready, 1)
            ada_load(0)
            for ph in phases:
                norm_in(norm_no[ph], ph)
                if ph == "mix0":
                    for n in range(4, 20, 4):
                        ada_load(n)
                    act.wait_ge(ada_read, 2)
                shift(ph, vec_of(ph))
                u = start[ph]
                if ph == "mix0":
                    mix0(u)
                elif ph == "mix1":
                    mix1(u)
                elif ph.startswith("peer"):
                    peer(ph, int(ph[-1]), u)
                elif ph.startswith("ffn"):
                    ffn(ph, int(ph[-1]), u)
                else:
                    hyb(ph, int(ph[-1]), u)
                if norm_no[ph] >= 4:
                    norm_out(norm_no[ph] + 1, u + phase_units(ph) - 1)

        @block.vector
        def _(dve):
            V = nc.vector

            def low(unit, n, it=0, per=0):
                hi, lo = parts_of(unit, n)
                dve.wait_ge(whi_ready, it * per + (n + 1))
                V.tensor_tensor(out=lo, in0=ring[:, unit % SLOTS, :], in1=hi, op=ALU.subtract).then_inc(wlo_ready, 1)

            def norm_low(ph):
                for q in range(4):
                    dve.wait_ge(xhi_ready, 4 * split_no[ph] + q + 1)
                    V.tensor_tensor(out=xparts[:, 1, 2 * q:2 * q + 2, :], in0=hT[:, 2 * q:2 * q + 2, :],
                                    in1=xparts[:, 0, 2 * q:2 * q + 2, :], op=ALU.subtract).then_inc(xlo_ready, 1)

            def norm_in(ph, vec, gain):
                V.scalar_tensor_tensor(out=acol[:], in0=mods[:, vec + 1, :], scalar=1.0, in1=gain, op0=ALU.add, op1=ALU.mult)
                if ph.startswith("ffn"):
                    for k in range(2):
                        low(start[ph] + k, split0[ph] + k)
                dve.wait_ge(std_ready, norm_no[ph] + 1)
                V.reciprocal(stat[:, 1], stat[:, 0])
                dve.drain()
                for kt in range(KD):
                    V.scalar_tensor_tensor(out=hT[:, kt, :], in0=x[:, kt, :], scalar=acol[:, kt:kt + 1], in1=stat[:, 1],
                                           op0=ALU.mult, op1=ALU.mult).then_inc(mid_ready, 1)

            def y_of(n, bank=4):
                return ps[bank + n // 2][:, (n % 2) * S:(n % 2 + 1) * S]

            def add_plain(ph, vec):
                turned = ph.startswith("peer")
                if not turned:
                    wait_used(dve, start[ph] + phase_units(ph) - 1)
                for n in range(KD):
                    if turned:
                        dve.wait_ge(y_turned, 4 * int(ph[-1]) + n // 2 + 1)
                    V.scalar_tensor_tensor(out=x[:, n, :], in0=y_of(n, 0 if turned else 4), scalar=mods[:, vec + 2, n:n + 1], in1=x[:, n, :],
                                           op0=ALU.mult, op1=ALU.add).then_inc(x_ready, 1)
                dve.drain()

            def add_normed(ph, vec, post, factor):
                V.scalar_tensor_tensor(out=acol[:], in0=mods[:, vec + 2, :], scalar=factor, in1=post, op0=ALU.mult, op1=ALU.mult)
                dve.wait_ge(std_ready, norm_no[ph] + 2)
                V.reciprocal(stat[:, 1], stat[:, 0])
                dve.drain()
                for n in range(KD):
                    V.scalar_tensor_tensor(out=gtmp[:, n, :], in0=y_of(n), scalar=acol[:, n:n + 1], in1=stat[:, 1],
                                           op0=ALU.mult, op1=ALU.mult)
                dve.drain()
                for n in range(KD):
                    V.tensor_tensor(out=x[:, n, :], in0=x[:, n, :], in1=gtmp[:, n, :], op=ALU.add).then_inc(x_ready, 1)
                dve.drain()

            def head_norm(c, out, bank, gcol, n=S, b=0):
                dve.drain()
                dve.wait_ge(hn_std, c + 2)
                V.reciprocal(hrec[:, 0:n], hstd[:, b, 0:n])
                dve.drain()
                V.scalar_tensor_tensor(out=out, in0=bank[:, 0:n], scalar=gcol, in1=hrec[:, 0:n],
                                       op0=ALU.mult, op1=ALU.mult).then_inc(hn_out, 1)

            def lowest(g, k, inst):
                wait_alone(dve, s_ready, g + k + 1)
                b = k % 2
                bank = ps[4 + b]
                first = inst.get("sink", FMAX)
                for tt in range(TT):
                    if inst["kind"] == "cmp":
                        cols = slice(tt * NCMP, (tt + 1) * NCMP)
                        o = (1 - tt) * P + CMP_LEN - 1
                        bias = nb[:, inst["nb"], inst["half"], o:o + 16 * (NCMP - 1) + 1:16]
                    else:
                        cols = slice(0, P) if tt == 0 else slice(P, TW)
                        if inst.get("row"):
                            bias = pc("cmask")[:, cols]
                        else:
                            bias = nb[:, inst["nb"], inst["half"], P:2 * P] if tt == 0 else nb[:, inst["nb"], inst["half"], 0:S]
                    m = V.tensor_tensor_reduce(out=neg[:, b, cols], in0=bank[:, cols], in1=bias, scale=1.0, scalar=first,
                                               op0=ALU.add, op1=ALU.min, accum_out=negm[:, b, tt:tt + 1])
                m.then_inc(neg_ready, 1)

            def normalize(g, k, inst):
                b = k % 2
                dve.wait_ge(exp_ready, g + k + 1)
                if "sink" in inst:
                    V.tensor_tensor(out=rows[:, b, :], in0=rows[:, b, :], in1=sink_e[:, b, :], op=ALU.add)
                    dve.drain()
                V.reciprocal(rinv[:, b, :], rows[:, b, :])
                dve.drain()
                for tt in range(TT):
                    if inst["kind"] == "cmp":
                        cols = slice(tt * NCMP, (tt + 1) * NCMP)
                    else:
                        cols = slice(0, P) if tt == 0 else slice(P, TW)
                    gate = inst["gate"][:, tt:tt + 1] if "gate" in inst else None
                    m = V.tensor_scalar(prob[:, b, cols], prob[:, b, cols], rinv[:, b, tt:tt + 1], gate, ALU.mult,
                                        ALU.bypass if gate is None else ALU.mult)
                m.then_inc(pn_ready, 1)

            def take_outputs(pairs, chunk, bank=2):
                dve.wait_ge(o_done, pairs)
                V.tensor_copy(oT[0:HD, chunk, :], ps[bank][0:HD, 0:S])
                V.tensor_copy(oT[HD:P, chunk, :], ps[bank + 1][HD:P, 0:S]).then_inc(o_read, 1)

            def ada_unit(sums, n, cc, k, it=0, per=0):
                dve.drain()
                arrived, before = (ada_loaded, 0) if n < EARLY else (ada_late, EARLY)
                dve.wait_ge(arrived[n % SLOTS], it * (per // SLOTS * 16) + 16 * ((n - before) // SLOTS + 1))
                col = cact[:, cc + k:cc + k + 1]
                w = adaw[:, n % SLOTS]
                if k == 0:
                    m = V.tensor_scalar(sums, w, col, None, ALU.mult)
                else:
                    m = V.scalar_tensor_tensor(out=sums, in0=w, scalar=col, in1=sums, op0=ALU.mult, op1=ALU.add)
                m.then_inc(ada_used, 1)
                if k == KD - 1:
                    dve.drain()
                    V.tensor_copy(small[:, 60:61], sums[:, 0:1]).then_inc(ada_acc, 1)

            def ada_part(sums, n, cc, first, it=0, per=0):
                for q in range(4):
                    ada_unit(sums, n + q, cc, (0 if first else 4) + q, it, per)

            def ada_take(v, bank):
                V.tensor_tensor(out=mods[:, v, :], in0=bank[:, 0:KD],
                                in1=pc("adab").rearrange("p (v k) -> p v k", v=NVEC)[:, v, :], op=ALU.add).then_inc(ada_read, 1)

            def mix0(u):
                V.memset(u_pad[:, 0:2], 0.0)
                wait_used(dve, u)
                V.tensor_scalar(ftmp[0:8, 0, :], ps[0][0:8, 0:S], pc("bf")[0:8, :], None, ALU.add)
                dve.drain()
                V.scalar_tensor_tensor(out=ftmp[0:8, 1, :], in0=ftmp[0:8, 0, :], scalar=-1.0, in1=ftmp[0:8, 0, :],
                                       op0=ALU.mult, op1=ALU.min).then_inc(logf_ready, 1)
                dve.wait_ge(logf_act, 1)
                V.scalar_tensor_tensor(out=ftmp[0:8, 1, :], in0=ftmp[0:8, 0, :], scalar=0.0, in1=ftmp[0:8, 3, :],
                                       op0=ALU.min, op1=ALU.subtract)
                V.memset(ftmp[0:8, 2, :], 1.0)
                dve.drain()
                V.tensor_tensor_scan(cum[0:8, :], ftmp[0:8, 2, :], ftmp[0:8, 1, :], 0.0, ALU.mult, ALU.add).then_inc(cum_ready, 1)
                gq = small[:, 1:2]
                V.tensor_scalar(gq, pc("fqg"), -SCALE, None, ALU.mult)
                dve.drain()
                u += 1
                w0 = COL["convw"][0]
                with dve.Fori(0, 2) as i:
                    for e in range(2):
                        r = i * 2 + e
                        ada_part(acc4[:, r, :], 16 + 8 * e, 0, True, i, 16)
                        head_norm(r * 2, qs[:, 0], ps[0], gq)
                        head_norm(r * 2 + 1, ks[:, 0], ps[1], pc("fkg"), b=1)
                        insts = [dict(half=f, kind="full", row=True) for f in range(2)]
                        for k in range(2):
                            lowest(r * 2, k, insts[k])
                        for k in range(2):
                            normalize(r * 2, k, insts[k])
                        ada_part(acc4[:, r, :], 20 + 8 * e, 0, False, i, 16)
                        dve.wait_ge(conv_c, r + 2)
                        wait_used(dve, u + 6 * e + 4, i, 12)
                        V.tensor_tensor(out=u_pad[:, 2:S + 2], in0=ps[1][:, 0:S], in1=ccs, op=ALU.mult).then_inc(conv_u, 1)
                        dve.drain()
                        wc = [prm[:, w0:w0 + 12].rearrange("p (c k) -> p c k", k=3)[:, r, q:q + 1] for q in range(3)]
                        V.tensor_scalar(conv_t[:, 0, :], u_pad[:, 0:S], wc[0], None, ALU.mult)
                        dve.drain()
                        V.scalar_tensor_tensor(out=conv_t[:, 1, :], in0=u_pad[:, 1:S + 1], scalar=wc[1], in1=conv_t[:, 0, :],
                                               op0=ALU.mult, op1=ALU.add)
                        dve.drain()
                        V.scalar_tensor_tensor(out=conv_t[:, 0, :], in0=u_pad[:, 2:S + 2], scalar=wc[2], in1=conv_t[:, 1, :],
                                               op0=ALU.mult, op1=ALU.add)
                        dve.drain()
                        wait_used(dve, u + 6 * e + 5, i, 12)
                        V.tensor_tensor(out=oT[:, r, :], in0=ps[2][:, 0:S], in1=conv_t[:, 0, :], op=ALU.mult).then_inc(conv_out, 1)
                        take_outputs(r + pair0["mix0"], r + 4)
                for a in range(4):
                    dve.wait_ge(ada_sum, 3 + a)
                    ada_take(2 + a, ps[a])
                dve.drain()

            def mix1(u):
                hn = hn0["mix1"]
                gq = small[:, 2:3]
                V.tensor_scalar(gq, pc("nqg"), -SCALE, None, ALU.mult)
                dve.drain()
                for n in range(4):
                    head_norm(hn + n, ks[:, 1 + n], ps[n % 2], pc("nkg", 1 + n // 2, 1), b=n % 2)
                head_norm(hn + 4, kc_sb[:, 0:2 * NCMP], ps[0], pc("nkg", 0, 1), 2 * NCMP)
                u += 20
                wait_used(dve, u)
                V.tensor_tensor(out=gsum, in0=ps[2][:, 0:TT * 48].rearrange("p (a b) -> p a b", a=TT),
                                in1=pc("bgate").unsqueeze(1).to_broadcast([P, TT, 48]), op=ALU.add).then_inc(gate_z, 1)
                dve.wait_ge(gate_s, 1)
                g3 = gates[:].rearrange("p t (h y) -> p t h y", y=3)
                V.tensor_scalar(g3[:, 0, :, 0], g3[:, 0, :, 0], pc("rowmask"), None, ALU.mult).then_inc(gate_ready, 1)
                dve.drain()
                g6 = gates[:].rearrange("p t (a f j y) -> p t a f j y", a=2, f=2, j=4)
                u += 1
                with dve.Fori(0, 2) as i:
                    for e in range(4):
                        head_norm(i * 4 + (hn + 5 + e), qs_all[:, i * 4 + e, :], ps[e % 2], gq, b=e % 2)
                with dve.Fori(0, 4) as i:
                    g, r = i * 12 + att0["mix1"], i * 2 + pair0["mix1"]
                    insts = [dict(half=f, kind="cmp" if kind == 0 else "full", nb=half, gate=g6[:, :, half, f, i, kind])
                             for half in range(2) for kind in range(3) for f in range(2)]
                    dve.wait_ge(bias_in[0], i * 32 + 32 * (bias0["mix1"] + 1))
                    lowest(g, 0, insts[0])
                    lowest(g, 1, insts[1])
                    for k, inst in enumerate(insts):
                        normalize(g, k, inst)
                        if k == 4:
                            dve.wait_ge(bias_in[1], i * 32 + 32 * (bias0["mix1"] + 1))
                        if k < 10:
                            lowest(g, k + 2, insts[k + 2])
                        if k == 8:
                            take_outputs(r, i * 2)
                    take_outputs(r + 1, i * 2 + 1, 0)
                dve.drain()

            def hyb(ph, l, u):
                bcol = prm[:, COL["mixb"][0] + 13 * l:COL["mixb"][0] + 13 * l + 13]

                def project(out, bank, col, scale):
                    V.tensor_scalar(out, bank[:, 0:S], col, scale, ALU.add, ALU.mult).then_inc(q_ready, 1)

                sk = prm[:, COL["sinks"][0] + 8 * l:COL["sinks"][0] + 8 * l + 8].rearrange("p (j f) -> p j f", f=2)
                b3 = bcol[:, 0:4].rearrange("p (a b) -> p a b", b=1)
                b4 = bcol[:, 5:9].rearrange("p (a b) -> p a b", b=1)
                b5 = bcol[:, 9:13].rearrange("p (a b) -> p a b", b=1)
                wait_used(dve, u)
                project(ks[:, 1], ps[1], bcol[:, 4:5], 1.0)
                wait_used(dve, u + 2)
                project(qs[:, 0], ps[0], bcol[:, 0:1], -SCALE)
                u += 3
                window = [dict(half=f, kind="full", nb=0, sink=nsk[:, f:f + 1]) for f in range(2)]
                causal = [dict(half=f, kind="full", nb=1) for f in range(2)]

                def pairs(i, more):
                    g, r = i * 4 + att0[ph], i * 2 + pair0[ph]
                    V.tensor_scalar(nsk, sk[:, i, :], -1.0, None, ALU.mult)
                    dve.drain()
                    dve.wait_ge(bias_in[0], i * 32 + 32 * (bias0[ph] + 1))
                    for k in range(2):
                        lowest(g, k, window[k])
                    for k in range(2):
                        normalize(g, k, window[k])
                    wait_used(dve, u, i, 4)
                    project(qs[:, 1], ps[1], b4[:, i, :], -SCALE)
                    wait_used(dve, u + 1, i, 4)
                    project(ks[:, 0], ps[0], b5[:, i, :], 1.0)
                    take_outputs(r, i)
                    dve.wait_ge(bias_in[1], i * 32 + 32 * (bias0[ph] + 1))
                    g = g + 2
                    for k in range(2):
                        lowest(g, k, causal[k])
                    for k in range(2):
                        normalize(g, k, causal[k])
                    if more:
                        wait_used(dve, u + 3, i, 4)
                        project(qs[:, 0], ps[0], b3[:, i + 1, :], -SCALE)
                    take_outputs(r + 1, i + 4)

                with dve.Fori(0, 3) as i:
                    pairs(i, True)
                pairs(3, False)
                dve.wait_ge(on_ready, 6 * l + 4)
                g0 = COL["gain"][0] + KD * l
                for grp in range(2):
                    V.reciprocal(sq[:, grp, :], conv_t[:, grp, :])
                    dve.drain()
                    for kt in range(4):
                        n = 4 * grp + kt
                        m = V.scalar_tensor_tensor(out=oT[:, n, :], in0=oT[:, n, :], scalar=prm[:, g0 + n:g0 + n + 1],
                                                   in1=sq[:, grp, :], op0=ALU.mult, op1=ALU.mult)
                    m.then_inc(on_ready, 1)
                dve.drain()

            def ffn(ph, no, u):
                norm_low(ph)
                n = split0[ph]
                with dve.Fori(0, NF // 2) as i:
                    for e in range(2):
                        g, k = u + 2 * e, n + 2 * e
                        low(g + 2, k + 2, i, 4)
                        dve.wait_ge(silu_ready, i * 2 + (NF * no + e + 1))
                        wait_used(dve, g + 1, i, 4)
                        V.tensor_tensor(out=hid[:, e, :], in0=ps[2 * e + 1][:, 0:S], in1=sl[:, e, :],
                                        op=ALU.mult).then_inc(ffn_h, 1)
                        low(g + 3, k + 3, i, 4)
                        dve.wait_ge(hhi_ready, i * 2 + (NF * no + e + 1))
                        f = i * 2 + e
                        V.tensor_tensor(out=hparts[:, 1, f, :], in0=hid[:, e, :], in1=hparts[:, 0, f, :],
                                        op=ALU.subtract).then_inc(hlo_ready, 1)
                u, n = u + 2 * NF, n + 2 * NF
                with dve.Fori(0, 5) as i:
                    for e in range(4):
                        low(u + e + 2, n + e + 2, i, 4)

            def peer(ph, l, u):
                dve.wait_ge(ps_read, PH * (l + 1))
                for tt in range(TT):
                    sc = score[:, tt]
                    for g in range(16):
                        V.max(r_sv[:, g, 0:8], sc[:, g, :])
                    dve.drain()
                    for g in range(16):
                        V.max_index(r_si[:, g, 0:8], r_sv[:, g, 0:8], sc[:, g, :])
                    dve.drain()
                    for g in range(16):
                        V.match_replace(sc[:, g, :], r_sv[:, g, 0:8], sc[:, g, :], -FMAX)
                    dve.drain()
                    for g in range(16):
                        V.max(r_sv[:, g, 8:16], sc[:, g, :])
                    dve.drain()
                    for g in range(16):
                        V.max_index(r_si[:, g, 8:16], r_sv[:, g, 8:16], sc[:, g, :])
                    dve.drain()
                    V.tensor_copy(r_sif, r_si[:])
                    cand = sc.rearrange("p g n -> p (g n)").rearrange("p (h a b) -> p h a b", h=PH, a=TOPK)
                    sv4 = r_sv.rearrange("p (h w) k -> p h w k", w=2)
                    for h in range(PH):
                        V.tensor_tensor(out=cand[:, h], in0=sv4[:, h, 0, :].unsqueeze(2).to_broadcast([P, TOPK, TOPK]),
                                        in1=sv4[:, h, 1, :].unsqueeze(1).to_broadcast([P, TOPK, TOPK]), op=ALU.add)
                    dve.drain()
                    cf = sc.rearrange("p g n -> p (g n)").rearrange("p (h c) -> p h c", h=PH)
                    for h in range(PH):
                        V.max(r_cv[:, h, 0:8], cf[:, h, :])
                    dve.drain()
                    for h in range(PH):
                        V.max_index(r_ci[:, h, 0:8], r_cv[:, h, 0:8], cf[:, h, :])
                    dve.drain()
                    for h in range(PH):
                        V.match_replace(cf[:, h, :], r_cv[:, h, 0:8], cf[:, h, :], -FMAX)
                    dve.drain()
                    for h in range(PH):
                        V.max(r_cv[:, h, 8:16], cf[:, h, :])
                    dve.drain()
                    for h in range(PH):
                        V.max_index(r_ci[:, h, 8:16], r_cv[:, h, 8:16], cf[:, h, :])
                    dve.drain()
                    cif = r_ci[:].rearrange("p h k -> p (h k)")
                    V.tensor_scalar(r_ab[:, 0, :], cif, 4, None, ALU.logical_shift_right)
                    V.tensor_scalar(r_ab[:, 1, :], cif, 15, None, ALU.bitwise_and)
                    V.tensor_copy(r_sum, r_cv[:, :, 0])
                    dve.drain()
                    V.tensor_copy(r_abf, r_ab[:])
                    V.tensor_tensor(out=r_cv, in0=r_cv, in1=r_sum.unsqueeze(2).to_broadcast([P, PH, TOPK]),
                                    op=ALU.subtract).then_inc(rexp_in, 1)
                    dve.drain()
                    si4 = r_sif.rearrange("p (h w) k -> p h w k", w=2)
                    for w in range(2):
                        V.tensor_tensor(out=eq[:], in0=r_abf[:, w, :].unsqueeze(2).to_broadcast([P, NE, TOPK]),
                                        in1=iota[:, 0:TOPK].unsqueeze(1).to_broadcast([P, NE, TOPK]), op=ALU.is_equal)
                        dve.drain()
                        for h in range(PH):
                            V.tensor_tensor(out=eq[:, h * TOPK:(h + 1) * TOPK, :], in0=eq[:, h * TOPK:(h + 1) * TOPK, :],
                                            in1=si4[:, h, w, :].unsqueeze(1).to_broadcast([P, TOPK, TOPK]), op=ALU.mult)
                        dve.drain()
                        V.tensor_reduce(r_out[:, tt, w, :], eq[:], AX.X, ALU.add)
                        dve.drain()
                    dve.wait_ge(rexp_out, TT * l + tt + 1)
                    e3 = r_out[:, tt, 2, :].rearrange("p (h k) -> p h k", h=PH)
                    V.tensor_reduce(r_sum, e3, AX.X, ALU.add)
                    dve.drain()
                    V.reciprocal(r_rec, r_sum)
                    dve.drain()
                    V.tensor_tensor(out=e3, in0=e3, in1=r_rec.unsqueeze(2).to_broadcast([P, PH, TOPK]),
                                    op=ALU.mult).then_inc(route_ready, 1)
                norm_low(ph)
                n = split0[ph]
                u += PH
                with dve.Fori(0, (NE - NPLAIN) // 4) as i:
                    for e in range(4):
                        low(u + NPLAIN + e, n + e, i, 4)
                u += NE
                n += NE - NPLAIN
                for k in range(2):
                    low(u + k, n + k)
                for tt in range(TT):
                    dve.wait_ge(routeT_ready, TT * l + tt + 1)
                    toks = slice(tt * P, (tt + 1) * P)
                    V.tensor_copy(r_outT[:, 0:3:2, toks], ps[2 + tt][:, 0:3 * P].rearrange("p (w t) -> p w t", w=3)[:, 0:3:2, :])
                    V.tensor_scalar(r_outT[:, 1, toks], ps[2 + tt][:, P:2 * P], -1.0, None, ALU.mult)
                    dve.drain()
                    V.tensor_copy(small[:, 61:62], r_outT[:, 1, tt * P:tt * P + 1]).then_inc(routeT_read, 1)
                dve.drain()
                dve.wait_ge(gelu_ready, NE * (l + 1) + 2)

                def weigh(i, e):
                    dve.wait_ge(g_ready, i * GB + (S // 4 * l + e + 1 + GB))
                    a = arena[:].rearrange("p j (c b t) -> p j c b t", b=GB, t=4)[:, :, i, e, :]
                    V.tensor_tensor(out=a, in0=ps[e][:].rearrange("p (t j) -> p j t", t=4), in1=a,
                                    op=ALU.mult).then_inc(g_read, 1)

                oT4 = r_outT[:].rearrange("p w (c b t) -> p w c b t", b=GB, t=4)
                def first_rows(i, e):
                    for t in range(4):
                        m = V.tensor_scalar(hot[:, e, 0, t, :], iota, oT4[:, 0, i, e, t:t + 1], oT4[:, 2, i, e, t:t + 1],
                                            ALU.is_equal, ALU.mult)
                    m.then_inc(hot_ready, 1)

                with dve.Fori(0, S // 4 // GB) as i:
                    for e in range(GB):
                        first_rows(i, e)
                        if e >= GB // 2:
                            weigh(i, e - GB // 2)
                    for e in range(GB // 2, GB):
                        weigh(i, e)
                a = NE * l

                def activations_low(j, k, it=0, per=0):
                    dve.wait_ge(ahi_ready, it * per + (k + 1))
                    V.tensor_tensor(out=alo[:, k % 2, :], in0=arena[:, j, :], in1=ahi[:, k % 2, :],
                                    op=ALU.subtract).then_inc(alo_ready, 1)

                def vector(h, it):
                    if l == 1:
                        return it * 2 + (18 + h), KD
                    return (it + (12 + h // 2), KD) if h % 2 else (it + (6 + h // 2), 0)

                def half(h, it=0):
                    m = EARLY + 96 * l + 8 * h
                    for e in range(8):
                        k = 8 * h + e + 2
                        low(u + k, n + k, it, 16)
                        activations_low(it * 16 + k, a + k, it, 16)
                        ada_unit(acc[:, h % 2], m + e, vector(h, it)[1], e, it, 16)
                    if h:
                        take(h - 1, it)

                def take(h, it=0):
                    dve.wait_ge(ada_sum, it * 2 + (6 + 12 * l + h + 1))
                    ada_take(vector(h, it)[0], ps[h % 2])

                dve.drain()
                for k in range(2):
                    activations_low(k, a + k)
                half(0)
                with dve.Fori(0, 5) as i:
                    half(1, i)
                    half(2, i)
                half(11)
                with dve.Fori(0, 7) as i:
                    for e in range(4):
                        k = 96 + e + 2
                        low(u + k, n + k, i, 4)
                        activations_low(i * 4 + k, a + k, i, 4)
                for k in range(NE - 2, NE):
                    low(u + k, n + k)
                    activations_low(k, a + k)
                take(11)
                wait_used(dve, u + NE - 1)
                for b in range(2):
                    V.tensor_copy(ysb[:, 1, b * 512:(b + 1) * 512], ps[6 + b][:]).then_inc(y_dve, 1)

            V.memset(eps, EPS)
            V.memset(small[:, 4:5], 0.0).then_inc(neg_ready, 2)
            V.memset(small[:, 5:6], 0.0).then_inc(ffn_h, 2)
            V.memset(small[:, 6:7], 0.0).then_inc(gelu_ready, 2)
            V.memset(small[:, 7:8], 0.0).then_inc(g_read, GB)
            for semaphore in (conv_c, conv_u, hn_std, o_read):
                dve.sem_inc(semaphore, 1)
            dve.sem_inc(g_ready, GB)
            V.memset(small[:, 24:25], 0.0).then_inc(setup_done, 1)
            dve.wait_ge(params_in, 48)
            h0 = TAB["hot"][0]
            V.tensor_scalar(tabs[0:32, h0:h0 + 512], tabs[0:32, h0:h0 + 512], -1.0, None, ALU.mult).then_inc(tab_ready, 1)
            dve.wait_ge(tab_read, 1)
            for a, name in enumerate(("mask", "mask2")):
                m0 = TAB[name][0]
                m = V.tensor_tensor(out=erow[0:16, a, :], in0=ps[2 + a][0:16, :], in1=tabs[0:16, m0:m0 + 512], op=ALU.add)
            m.then_inc(tab_ready, 1)
            dve.wait_ge(c_ready, 1)
            for v in range(2):
                ada_part(acc[:, v], 8 * v, 0, True)
                ada_part(acc[:, v], 8 * v + 4, 0, False)
            for v in range(2):
                dve.wait_ge(ada_sum, v + 1)
                ada_take(v, ps[4 + v])
            dve.drain()
            for ph in phases:
                vec = vec_of(ph)
                if norm_no[ph] < 4:
                    gain = pc("norm", KD * norm_no[ph], KD)
                else:
                    gain = pc("pre", KD * ((norm_no[ph] - 4) // 2), KD)
                norm_in(ph, vec, gain)
                u = start[ph]
                if ph == "mix0":
                    mix0(u)
                elif ph == "mix1":
                    mix1(u)
                elif ph.startswith("peer"):
                    peer(ph, int(ph[-1]), u)
                elif ph.startswith("ffn"):
                    ffn(ph, int(ph[-1]), u)
                else:
                    hyb(ph, int(ph[-1]), u)
                if norm_no[ph] < 4:
                    add_plain(ph, vec)
                else:
                    add_normed(ph, vec, pc("post", KD * ((norm_no[ph] - 4) // 2), KD), 1.0 if ph.startswith("hyb") else 0.5)

        @block.gpsimd
        def _(pool):
            G = nc.gpsimd

            def bias(e, f, head):
                src = bias_rows[head, 127:127 + P * 511].rearrange("(p w) -> p w", w=511)[:, 0:TW]
                pool.dma_start(nb[:, e, f, :], src).then_inc(bias_in[e], 16)

            def mix0():
                pool.wait_ge(cum_ready, 1)
                pool.dma_start(cumrow[0:1, :, :], cum[0:8, :]).then_inc(cum_row, 16)

            def mix1():
                for a in range(2):
                    pool.wait_ge(kv_raw, 2 * a + 2)
                    for c in range(2):
                        src = kcv[:, 2 * a + c, :]
                        toks = bass.AP(src.tensor, src.offset, [list(src.ap[0]), [1, CMP_LEN], [16, NCMP]])
                        G.tensor_tensor(out=blk[:, a, :, c, :], in0=toks,
                                        in1=pc("pos", a * CMP_LEN, CMP_LEN).unsqueeze(2).to_broadcast([P, CMP_LEN, NCMP]),
                                        op=ALU.add).then_inc(blk_ready, 1)
                pool.wait_ge(hn_out, hn0["mix1"] + 13)
                with pool.Fori(0, 4) as i:
                    for half in range(2):
                        pool.wait_ge(o_read, i * 2 + (half + pair0["mix1"] - 1))
                        for f in range(2):
                            bias(half, f, i + (8 * half + 4 * f))
                        G.tensor_copy(qs[:, half, :], qs_all[:, i * 2 + half, :]).then_inc(q_staged, 1)

            def hyb(ph, l):
                pool.wait_ge(x_ready, KD * phases.index(ph))
                if l == 0:
                    pool.dma_start(vr[0:1, :, :, :], vrow).then_inc(cum_row, 16)
                with pool.Fori(0, 4) as i:
                    for e in range(2):
                        pool.wait_ge(o_read, i * 2 + (e + pair0[ph] - 1))
                        for f in range(2):
                            bias(e, f, i + (16 + 4 * f) if e == 0 else i * 2 + (24 + f))

            def peer(l):
                pool.wait_ge(g_read, S // 4 * (l + 1) + GB)
                m = EARLY + 96 * l
                for q in range(SLOTS):
                    pool.dma_start(adaw[:, q], ada[m + q]).then_inc(ada_late[q], 16)
                with pool.Fori(0, 96 // SLOTS - 1) as i:
                    for q in range(SLOTS):
                        pool.wait_ge(ada_used, i * SLOTS + (m + q + 1))
                        pool.dma_start(adaw[:, q], ada[i * SLOTS + (m + SLOTS + q)]).then_inc(ada_late[q], 16)

            pool.wait_ge(tab_ready, 2)
            pool.wait_ge(h_ready, 1)
            for a in range(2):
                pool.dma_start(bias_rows[16 * a:16 * a + 16].rearrange("h (p n) -> h p n", p=P),
                               erow[0:16, a, :].unsqueeze(1).to_broadcast([16, P, 512])).then_inc(bias_written, 16)
            pool.wait_ge(bias_written, 32)
            for ph in phases:
                if ph == "mix0":
                    mix0()
                elif ph == "mix1":
                    mix1()
                elif ph.startswith("peer"):
                    peer(int(ph[-1]))
                elif ph.startswith("hyb"):
                    hyb(ph, int(ph[-1]))


def vec_of(ph):
    return 3 * PHASES.index(ph)


norm_no_h = {ph: i for i, ph in enumerate(PHASES)}


def column_units(w):
    n = w.shape[1] // P
    return np.ascontiguousarray(w.reshape(KD, P, n, P).transpose(2, 1, 0, 3)).reshape(n, P, UNIT)


def padded(w):
    out = np.zeros((w.shape[0], P), w.dtype)
    out[:, :w.shape[1]] = w
    return out


def columns(v):
    return np.ascontiguousarray(v.reshape(-1, P).T)


def twice(v):
    return np.concatenate([v, v]).reshape(P, 1)


def block_diagonal(w):
    out = np.zeros(w.shape[:-2] + (P, P), w.dtype)
    out[..., :HD, :HD] = w
    out[..., HD:, HD:] = w
    return out


def head_columns(w, heads):
    return np.concatenate([w[:, h * HD:(h + 1) * HD] for h in heads], axis=1)


def head_rows(w, heads):
    return np.concatenate([w[h * HD:(h + 1) * HD] for h in heads], axis=0)


NSA_ORDER = [(2 * half + f) * 4 + j for j in range(4) for half in range(2) for f in range(2)]
SWA_ORDER = [4 * f + j for j in range(4) for f in range(2)]


def weight_stream(a):
    out = []
    w = a["even_w_in"][0]
    cb, cc, ch, q, k, v, f = (column_units(x) if x.shape[1] > 8 else column_units(padded(x))
                              for x in np.split(w, [512, 1024, 1536, 2048, 2560, 3072], axis=1))
    out += [f, np.stack([q, k, v, cc, ch, cb], axis=1).reshape(24, P, UNIT), column_units(a["even_w_out"][0])]

    def experts(l):
        u = a["peer_u"][l].reshape(NE, NE, KD, P).transpose(1, 3, 2, 0).reshape(NE, P, UNIT)
        v = a["peer_v"][l].reshape(NE, NE, D).transpose(1, 0, 2)
        return [column_units(a["peer_w_q"][l]), u, v]

    out += experts(0)
    q, kc, vc, ks, vs, kw, vw, gl = np.split(a["odd_w_in"][0], [1024 + 256 * i for i in range(7)], axis=1)
    w1 = block_diagonal(a["odd_cmp_w1"][0].reshape(2, CMP_LEN, HD, HD))
    w1 = w1.reshape(2, 4, 8, P, P).transpose(0, 1, 3, 2, 4).reshape(8, P, UNIT)
    out += [column_units(x) for x in (kc, vc, ks, kw, vs, vw)]
    out += [w1, column_units(padded(gl)), column_units(head_columns(q, NSA_ORDER)),
            column_units(head_rows(a["odd_w_out"][0], NSA_ORDER))]
    out += experts(1)

    def ffn(l, n):
        g, u = column_units(a["ffn_w_gate_2"][l, n]), column_units(a["ffn_w_up_2"][l, n])
        return [np.stack([g, u], axis=1).reshape(2 * NF, P, UNIT), a["ffn_w_down_2"][l, n].reshape(NF, P, D)]

    for l in range(2):
        out += ffn(l, 0)
        qa, ka, va, qb, kb, vb = np.split(a["mix_w_in_2"][l], [512, 640, 768, 1280, 1792], axis=1)
        qa, qb, kb, vb = (column_units(x) for x in (head_columns(qa, SWA_ORDER), qb, kb, vb))
        out += [column_units(ka), column_units(va), qa[:1]]
        out += [np.concatenate([np.stack([qb[i], kb[i], vb[i]]), qa[i + 1:i + 2]]) for i in range(4)]
        wo = a["mix_w_out_2"][l]
        out += [column_units(np.concatenate([head_rows(wo[:512], SWA_ORDER), wo[512:]], axis=0))]
        out += ffn(l, 1)
    return np.concatenate(out, axis=0)


def buckets(dist):
    n = np.maximum(dist, 0)
    nf = np.maximum(n, 1).astype(np.float32)
    large = 16 + (np.log(nf / np.float32(16)) / np.float32(math.log(128 / 16)) * np.float32(16)).astype(np.int32)
    return np.where(n < 16, n, np.minimum(large, 31))


def bias_constants():
    dist = 255 - np.arange(512)
    hot = ((buckets(dist)[None] == np.arange(32)[:, None]) & (dist >= 0)[None]).astype(np.float32)
    causal = np.where(dist >= 0, 0.0, BIG).astype(np.float32)
    window = np.where((dist >= 0) & (dist < 128), 0.0, BIG).astype(np.float32)
    mask = np.broadcast_to(causal, (16, 512))
    mask2 = np.concatenate([np.broadcast_to(window, (8, 512)), np.broadcast_to(causal, (8, 512))])
    return hot, mask, mask2


def packed_params(a):
    f = np.float32
    t = np.arange(P)
    cmask = np.concatenate([np.where(t[None] > t[:, None], BIG, 0.0),
                            np.where(np.arange(S)[None] > P + t[:, None], BIG, 0.0)], axis=1).astype(f)
    adab = np.concatenate([columns(a["ada_b"].reshape(-1)), columns(a["ada_b_2"].reshape(-1))], axis=1)
    mixb = []
    gain = []
    for l in range(2):
        b = a["mix_b_in_2"][l]
        mixb += [columns(head_rows(b[:512].reshape(-1, 1), SWA_ORDER).reshape(-1)), columns(b[512:640]),
                 columns(b[768:1280]), columns(b[1280:1792])]
        g = a["group_gain_2"][l]
        gain += [columns(head_rows(g[:512].reshape(-1, 1), SWA_ORDER).reshape(-1)), columns(g[512:])]
    sinks = np.concatenate([a["attn_sinks_2"][l][SWA_ORDER] for l in range(2)])
    bf = np.zeros((P, 1), f)
    bf[:8, 0] = a["even_b_f"][0]
    parts = {
        "ident": np.eye(P, dtype=f), "ones": np.ones((P, P), f), "bd": block_diagonal(np.ones((HD, HD), f)),
        "iota": np.broadcast_to(t.astype(f), (P, P)), "cmask": cmask,
        "rowmask": (t >= CMP_LEN - 1).astype(f).reshape(P, 1), "adab": adab,
        "c": np.concatenate([columns(a["c"][0]), columns(a["c_2"][0])], axis=1),
        "norm": columns(a["norm_g"].reshape(-1)), "pre": columns(a["norm_pre_2"].reshape(-1)),
        "post": columns(a["norm_post_2"].reshape(-1)),
        "convw": a["even_conv_w"][0].reshape(3, 4, P).transpose(2, 1, 0).reshape(P, 12), "bf": bf,
        "fqg": twice(a["even_q_g"][0]), "fkg": twice(a["even_k_g"][0]), "nqg": twice(a["odd_q_g"][0]),
        "nkg": np.concatenate([twice(a["odd_k_g"][0, i]) for i in range(3)], axis=1),
        "pos": np.concatenate([np.concatenate([a["odd_cmp_pos"][0, i].T] * 2) for i in range(2)], axis=1),
        "w2": np.concatenate([block_diagonal(a["odd_cmp_w2"][0, i]) for i in range(2)], axis=1),
        "keys": np.concatenate([a["peer_keys"][l].transpose(0, 2, 1).reshape(P, NE) for l in range(2)], axis=1),
        "bgate": np.broadcast_to(a["odd_b_gate"][0], (P, 48)), "mixb": np.concatenate(mixb, axis=1),
        "gain": np.concatenate(gain, axis=1), "sinks": np.broadcast_to(sinks, (P, 16)),
    }
    return np.ascontiguousarray(np.concatenate([parts[n] for n, _ in _COLS], axis=1))


def packed_tables(a):
    hot, mask, mask2 = bias_constants()
    out = np.zeros((32, NTAB), np.float32)
    for name, v in (("rel", a["rel_table"]), ("rel2", a["rel_bias_2"]), ("hot", hot), ("mask", mask), ("mask2", mask2)):
        c, w = TAB[name]
        out[:v.shape[0], c:c + w] = v
    return out


def packed_ada(a):
    def cut(w):
        l, _, n = w.shape
        return w.reshape(l, KD, P, n // UNIT, UNIT).transpose(0, 3, 1, 2, 4).reshape(-1, P, UNIT)
    w = np.concatenate([cut(a["ada_w"]), cut(a["ada_w_2"])], axis=0).reshape(NVEC, KD, P, UNIT)
    order = list(range(6)) + [6 * b + 6 + k for k in range(6) for b in range(2)] + list(range(18, NVEC))
    return w[order].reshape(-1, P, UNIT)


def layout(a):
    b = a["mix_b_in_2"]
    vrow = np.stack([np.concatenate([b[l, 640:768], b[l, 1792:2304]]) for l in range(2)]).reshape(1, 2, 5, P)
    return {
        "xT": np.ascontiguousarray(a["x"][0].T.reshape(KD, P, S).transpose(1, 0, 2)),
        "par": packed_params(a), "tab": packed_tables(a), "vrow": np.ascontiguousarray(vrow),
        "ada": packed_ada(a), "stream": weight_stream(a),
    }


def build(nc, arrays, upto=None):
    args = [nc.dram_tensor(n, v.shape, F32, kind="ExternalInput").ap() for n, v in arrays.items()]
    out = nc.dram_tensor("outT", (P, KD, S), F32, kind="ExternalOutput").ap()
    program(nc, *args, out, upto=upto)


def kernel(**inputs):
    import concourse.bacc as bacc
    from concourse.bass_utils import run_bass_kernel_spmd

    arrays = layout({k: np.asarray(v) for k, v in inputs.items()})
    nc = bacc.Bacc("TRN2", target_bir_lowering=False, num_devices=1)
    build(nc, arrays)
    got = run_bass_kernel_spmd(nc, [arrays], core_ids=[0]).results[0]["outT"]
    return np.ascontiguousarray(got.transpose(1, 0, 2).reshape(D, S).T).reshape(1, S, D)
```
